# Optimizing a Trainium2 kernel written in Bass

```python
import jax, jax.numpy as jnp
from jax import lax
import numpy as np

D_MODEL = 1024
BATCH = 1
SEQ = 256
DEPTH = 2

CHUNK = 64
EPS = 1e-6
POOL_WINDOWS = (2, 4, 8, 16)
POOL_GROUP = D_MODEL // 4
POOL_WIDTH = 4 * POOL_GROUP
SGU_LEN = 128
SGU_HEAD_DIM = 128
SGU_WIDTH = D_MODEL
SGU_HEADS = SGU_WIDTH // SGU_HEAD_DIM
GLA_HEADS = 4
GLA_KW = D_MODEL // 2
GLA_VW = D_MODEL
GLA_DK = GLA_KW // GLA_HEADS
GLA_DV = GLA_VW // GLA_HEADS
GLA_RANK = 16
GLA_TAU = 16.0
SB_HEAD_DIM = 128
SB_WIDTH = D_MODEL
SB_HEADS = SB_WIDTH // SB_HEAD_DIM
SB_QBLOCK = 128
EVEN_SIZES = (POOL_WIDTH, SGU_WIDTH, SGU_WIDTH, POOL_WIDTH + SGU_WIDTH)
ODD_SIZES = (GLA_KW, GLA_KW, GLA_VW, GLA_RANK, SB_WIDTH, SB_WIDTH, SB_WIDTH, GLA_VW + SB_WIDTH)
EVEN_IN = sum(EVEN_SIZES)
ODD_IN = sum(ODD_SIZES)
EVEN_MIX = POOL_WIDTH + SGU_WIDTH
ODD_MIX = GLA_VW + SB_WIDTH
N_EVEN = (DEPTH + 1) // 2
N_ODD = DEPTH // 2


def _split(t, sizes):
    idx = [int(i) for i in np.cumsum(sizes)[:-1]]
    return jnp.split(t, idx, axis=-1)

def rmsnorm(x, g):
    xf = x.astype(jnp.float32)
    y = xf * lax.rsqrt(jnp.mean(xf * xf, axis=-1, keepdims=True) + EPS)
    return (y * g.astype(jnp.float32)).astype(x.dtype)

def ada_modulate(x, c, norm_g, ada_w, ada_b):
    ada = jax.nn.silu(c) @ ada_w + ada_b
    shift, scale, gate = jnp.split(ada, 3, axis=-1)
    h = rmsnorm(x, norm_g) * (1.0 + scale[:, None, :]) + shift[:, None, :]
    return h, gate[:, None, :]

def pool_mixer(a, pool_w, pool_scale):
    B_, S, _ = a.shape
    af = a.astype(jnp.float32)
    cs = jnp.concatenate([jnp.zeros_like(af[:, :1]), jnp.cumsum(af, axis=1)], axis=1)
    t = np.arange(S)
    outs = []
    for g, w in enumerate(POOL_WINDOWS):
        sl = slice(g * POOL_GROUP, (g + 1) * POOL_GROUP)
        start = np.maximum(t + 1 - w, 0)
        count = jnp.asarray((t + 1 - start).astype(np.float32))
        win_sum = cs[:, 1:, sl] - cs[:, start, sl]
        outs.append(win_sum / count[None, :, None] - af[..., sl])
    p = jnp.stack(outs, axis=2).astype(a.dtype)
    y = jnp.einsum('bsgc,gcd->bsgd', p, pool_w).reshape(B_, S, POOL_WIDTH)
    return y * pool_scale

def spatial_gating(u, v, norm_g, w_s, b_s):
    B_, S, _ = u.shape
    n = S // SGU_LEN
    vh = rmsnorm(v, norm_g).reshape(B_, n, SGU_LEN, SGU_HEADS, SGU_HEAD_DIM)
    mask = jnp.tril(jnp.ones((SGU_LEN, SGU_LEN), dtype=bool))
    w = jnp.where(mask[None], w_s, jnp.zeros_like(w_s))
    z = jnp.einsum('hts,bnshd->bnthd', w, vh) + b_s.T[None, None, :, :, None]
    return u * z.reshape(B_, S, SGU_WIDTH)

def gla(q, k, v, log_a):
    B_, S = q.shape[:2]
    n = S // CHUNK
    r = lambda t: t.astype(jnp.float32).reshape(B_, n, CHUNK, *t.shape[2:])
    qf = r(q) * (GLA_DK ** -0.5)
    kf, vf, la = r(k), r(v), r(log_a)
    bcum = jnp.cumsum(la, axis=2)
    b_last = bcum[:, :, -1]
    q_dec = qf * jnp.exp(bcum)
    k_inv = kf * jnp.exp(-bcum)
    k_end = kf * jnp.exp(b_last[:, :, None] - bcum)
    mask = jnp.tril(jnp.ones((CHUNK, CHUNK), dtype=bool))
    att = jnp.einsum('bnthk,bnshk->bnhts', q_dec, k_inv)
    att = jnp.where(mask, att, 0.0)
    o_intra = jnp.einsum('bnhts,bnshv->bnthv', att, vf)

    def step(state, xs):
        qd, ke, vc, bl = xs
        o = jnp.einsum('bthk,bhkv->bthv', qd, state)
        state = jnp.exp(bl)[..., None] * state + jnp.einsum('bshk,bshv->bhkv', ke, vc)
        return state, o

    s0 = jnp.zeros((B_, GLA_HEADS, GLA_DK, GLA_DV), jnp.float32)
    xs = (jnp.moveaxis(q_dec, 1, 0), jnp.moveaxis(k_end, 1, 0), jnp.moveaxis(vf, 1, 0), jnp.moveaxis(b_last, 1, 0))
    _, o_inter = lax.scan(step, s0, xs)
    o = o_intra + jnp.moveaxis(o_inter, 0, 1)
    return o.reshape(B_, S, GLA_HEADS, GLA_DV).astype(v.dtype)

def stick_breaking(q, k, v):
    B_, S, H, Dh = q.shape
    scale = Dh ** -0.5
    outs = []
    for i in range(S // SB_QBLOCK):
        q0, q1 = i * SB_QBLOCK, (i + 1) * SB_QBLOCK
        z = jnp.einsum('bthd,bshd->bhts', q[:, q0:q1], k[:, :q1]).astype(jnp.float32) * scale
        strict = np.arange(q1)[None, :] < np.arange(q0, q1)[:, None]
        log_beta = jax.nn.log_sigmoid(z)
        log_1m = jnp.where(strict, jax.nn.log_sigmoid(-z), 0.0)
        after = lax.cumsum(log_1m, axis=3, reverse=True) - log_1m
        w = jnp.where(strict, jnp.exp(log_beta + after), 0.0)
        outs.append(jnp.einsum('bhts,bshd->bthd', w.astype(v.dtype), v[:, :q1]))
    return jnp.concatenate(outs, axis=1)

def even_layer(x, c, norm_g, ada_w, ada_b, in_w, pool_w, pool_scale, sgu_norm_g, sgu_w, sgu_b, out_w):
    h, gate_res = ada_modulate(x, c, norm_g, ada_w, ada_b)
    a, u, v, gate = _split(h @ in_w, EVEN_SIZES)
    ya = pool_mixer(a, pool_w, pool_scale)
    yb = spatial_gating(u, v, sgu_norm_g, sgu_w, sgu_b)
    y = jnp.concatenate([ya, yb], axis=-1) * jax.nn.silu(gate)
    return x + gate_res * (y @ out_w)

def odd_layer(x, c, norm_g, ada_w, ada_b, in_w, gate_w, gate_b, gla_norm_g, out_w):
    B_, S, _ = x.shape
    h, gate_res = ada_modulate(x, c, norm_g, ada_w, ada_b)
    gq, gk, gv, glr, sq, sk, sv, gate = _split(h @ in_w, ODD_SIZES)
    log_a = jax.nn.log_sigmoid((glr @ gate_w + gate_b).astype(jnp.float32)) / GLA_TAU
    hd = lambda t, n, d: t.reshape(B_, S, n, d)
    yc = gla(hd(gq, GLA_HEADS, GLA_DK), hd(gk, GLA_HEADS, GLA_DK), hd(gv, GLA_HEADS, GLA_DV),
             hd(log_a, GLA_HEADS, GLA_DK))
    yc = rmsnorm(yc, gla_norm_g).reshape(B_, S, GLA_VW)
    yd = stick_breaking(hd(sq, SB_HEADS, SB_HEAD_DIM), hd(sk, SB_HEADS, SB_HEAD_DIM),
                        hd(sv, SB_HEADS, SB_HEAD_DIM)).reshape(B_, S, SB_WIDTH)
    y = jnp.concatenate([yc, yd], axis=-1) * jax.nn.silu(gate)
    return x + gate_res * (y @ out_w)

def first_inputs(seed: int = 0) -> dict:
    key = jax.random.key(seed)
    ks = jax.random.split(key, 20)
    nrm = lambda k, shape, s: jax.random.normal(k, shape, jnp.float32) * s
    return {
        "x": nrm(ks[0], (BATCH, SEQ, D_MODEL), 1.0),
        "c": nrm(ks[1], (BATCH, D_MODEL), 1.0),
        "ada_w": nrm(ks[2], (DEPTH, D_MODEL, 3 * D_MODEL), 0.5 * D_MODEL ** -0.5),
        "ada_b": nrm(ks[3], (DEPTH, 3 * D_MODEL), 0.02),
        "norm_g": 1.0 + nrm(ks[4], (DEPTH, D_MODEL), 0.05),
        "even_in_w": nrm(ks[5], (N_EVEN, D_MODEL, EVEN_IN), D_MODEL ** -0.5),
        "pool_w": nrm(ks[6], (N_EVEN, 4, POOL_GROUP, POOL_GROUP), POOL_GROUP ** -0.5),
        "pool_scale": 1.0 + nrm(ks[7], (N_EVEN, POOL_WIDTH), 0.1),
        "sgu_norm_g": 1.0 + nrm(ks[8], (N_EVEN, SGU_WIDTH), 0.05),
        "sgu_w": nrm(ks[9], (N_EVEN, SGU_HEADS, SGU_LEN, SGU_LEN), SGU_LEN ** -0.5),
        "sgu_b": 1.0 + nrm(ks[10], (N_EVEN, SGU_HEADS, SGU_LEN), 0.1),
        "even_out_w": nrm(ks[11], (N_EVEN, EVEN_MIX, D_MODEL), EVEN_MIX ** -0.5),
        "odd_in_w": nrm(ks[12], (N_ODD, D_MODEL, ODD_IN), D_MODEL ** -0.5),
        "gla_gate_w": nrm(ks[13], (N_ODD, GLA_RANK, GLA_KW), GLA_RANK ** -0.5),
        "gla_gate_b": nrm(ks[14], (N_ODD, GLA_KW), 0.1),
        "gla_norm_g": 1.0 + nrm(ks[15], (N_ODD, GLA_HEADS, GLA_DV), 0.05),
        "odd_out_w": nrm(ks[16], (N_ODD, ODD_MIX, D_MODEL), ODD_MIX ** -0.5),
        "final_g": 1.0 + nrm(ks[17], (D_MODEL,), 0.05),
    }

def first_block(x, c, ada_w, ada_b, norm_g, even_in_w, pool_w, pool_scale, sgu_norm_g, sgu_w, sgu_b,
              even_out_w, odd_in_w, gla_gate_w, gla_gate_b, gla_norm_g, odd_out_w, final_g):
    for i in range(DEPTH):
        j = i // 2
        if i % 2 == 0:
            x = even_layer(x, c, norm_g[i], ada_w[i], ada_b[i], even_in_w[j], pool_w[j], pool_scale[j],
                           sgu_norm_g[j], sgu_w[j], sgu_b[j], even_out_w[j])
        else:
            x = odd_layer(x, c, norm_g[i], ada_w[i], ada_b[i], odd_in_w[j], gla_gate_w[j], gla_gate_b[j],
                          gla_norm_g[j], odd_out_w[j])
    return rmsnorm(x, final_g)


DEPTH_2 = 1

HEAD_DIM = 64
ATTN_GROUPS = ((128, 1), (512, 4), (2048, 16))
N_GROUPS = len(ATTN_GROUPS)
ATTN_HEADS_PER_GROUP = 4
ATTN_GROUP_WIDTH = ATTN_HEADS_PER_GROUP * HEAD_DIM
Q_BLOCK = 128
ROPE_THETA = 10000.0
RWKV_HEADS = 8
RWKV_WIDTH = RWKV_HEADS * HEAD_DIM
DECAY_LORA = 32
ICLR_LORA = 32
GATE_LORA = 96
RWKV_GN_EPS = 64e-5
D_FF = 4 * D_MODEL
PLE_DIM = 256
NORM_EPS = 1e-6

ATTN_QKV_COLS = 3 * N_GROUPS * ATTN_GROUP_WIDTH
RWKV_SPLITS = (RWKV_WIDTH, 2 * RWKV_WIDTH, 3 * RWKV_WIDTH,
               3 * RWKV_WIDTH + DECAY_LORA, 3 * RWKV_WIDTH + DECAY_LORA + ICLR_LORA)
RWKV_COLS = 3 * RWKV_WIDTH + DECAY_LORA + ICLR_LORA + GATE_LORA
GATE_COLS = 2 * D_MODEL
IN_COLS = ATTN_QKV_COLS + RWKV_COLS + GATE_COLS


def rmsnorm_2(x, g):
    xf = x.astype(jnp.float32)
    y = xf * lax.rsqrt(jnp.mean(xf * xf, axis=-1, keepdims=True) + NORM_EPS)
    return (y * g.astype(jnp.float32)).astype(x.dtype)

def rope(x, pos):
    half = HEAD_DIM // 2
    inv_freq = ROPE_THETA ** (-jnp.arange(0, HEAD_DIM, 2, dtype=jnp.float32) / HEAD_DIM)
    ang = pos[:, None] * inv_freq[None, :]
    ang = ang.reshape((pos.shape[0],) + (1,) * (x.ndim - 3) + (half,))
    c, s = jnp.cos(ang), jnp.sin(ang)
    xf = x.astype(jnp.float32)
    x1, x2 = xf[..., :half], xf[..., half:]
    return jnp.concatenate([x1 * c - x2 * s, x2 * c + x1 * s], axis=-1).astype(x.dtype)

def token_shift(z):
    return jnp.pad(z[:, :-1], ((0, 0), (1, 0), (0, 0)))

def dilated_attention_branch(z_attn):
    B, S, _ = z_attn.shape
    qkv = z_attn.reshape(B, S, 3, N_GROUPS, ATTN_HEADS_PER_GROUP, HEAD_DIM)
    pos = jnp.arange(S, dtype=jnp.float32)
    q = rope(qkv[:, :, 0], pos)
    k = rope(qkv[:, :, 1], pos)
    v = qkv[:, :, 2]
    qs = [q[:, :, g] for g in range(N_GROUPS)]
    ks = [k[:, :, g] for g in range(N_GROUPS)]
    vs = [v[:, :, g] for g in range(N_GROUPS)]
    scale = HEAD_DIM ** -0.5

    def block(bi):
        start = bi * Q_BLOCK
        t = start + jnp.arange(Q_BLOCK)
        outs, lses = [], []
        for g, (window, dil) in enumerate(ATTN_GROUPS):
            j = jnp.arange(window // dil + 1)
            idx = t[:, None] - dil * j[None, :]
            valid = idx >= 0
            idx_c = jnp.maximum(idx, 0)
            qb = lax.dynamic_slice_in_dim(qs[g], start, Q_BLOCK, axis=1)
            kg = jnp.take(ks[g], idx_c, axis=1)
            vg = jnp.take(vs[g], idx_c, axis=1)
            s = jnp.einsum('bqhd,bqjhd->bqhj', qb, kg, preferred_element_type=jnp.float32) * scale
            s = jnp.where(valid[None, :, None, :], s, -jnp.inf)
            m = jnp.max(s, axis=-1, keepdims=True)
            e = jnp.exp(s - m)
            den = jnp.sum(e, axis=-1)
            o = jnp.einsum('bqhj,bqjhd->bqhd', e, vg.astype(jnp.float32)) / den[..., None]
            outs.append(o)
            lses.append(m[..., 0] + jnp.log(den))
        alpha = jax.nn.softmax(jnp.stack(lses, axis=0), axis=0)
        o = alpha[0][..., None] * outs[0]
        for g in range(1, N_GROUPS):
            o = o + alpha[g][..., None] * outs[g]
        return o.astype(z_attn.dtype)

    out = lax.map(block, jnp.arange(S // Q_BLOCK))
    return out.transpose(1, 0, 2, 3, 4).reshape(B, S, ATTN_GROUP_WIDTH)

def rwkv7_time_mix(z, mu, w0, w2, a0, a2, g2, k_k, k_a, r_k, ln_w, ln_b):
    B, S, _ = z.shape
    f32 = jnp.float32
    z = z + (token_shift(z) - z) * mu
    r, k, v, xw, xa, xg = jnp.split(z, RWKV_SPLITS, axis=-1)
    logw = -jax.nn.softplus(-(w0 + jnp.tanh(xw) @ w2)) - 0.5
    decay = jnp.exp(-jnp.exp(logw.astype(f32)))
    a = jax.nn.sigmoid(a0 + xa @ a2)
    g = jax.nn.sigmoid(xg) @ g2
    heads = lambda t: t.reshape(B, S, RWKV_HEADS, HEAD_DIM).astype(f32)
    kk = heads(k * k_k)
    kk = kk / jnp.maximum(jnp.sqrt(jnp.sum(kk * kk, axis=-1, keepdims=True)), 1e-12)
    k = k * (1.0 + (a - 1.0) * k_a)
    r_h, k_h, v_h, a_h, w_h = heads(r), heads(k), heads(v), heads(a), heads(decay)
    seq = tuple(jnp.moveaxis(t, 1, 0) for t in (r_h, w_h, k_h, v_h, -kk, kk * a_h))

    def step(state, inp):
        r_t, w_t, k_t, v_t, a_t, b_t = inp
        sa = jnp.einsum('bhvk,bhk->bhv', state, a_t)
        state = (state * w_t[:, :, None, :] + sa[..., None] * b_t[:, :, None, :]
                 + v_t[..., None] * k_t[:, :, None, :])
        y = jnp.einsum('bhvk,bhk->bhv', state, r_t)
        return state, y

    state0 = jnp.zeros((B, RWKV_HEADS, HEAD_DIM, HEAD_DIM), f32)
    _, y = lax.scan(step, state0, seq)
    y = jnp.moveaxis(y, 0, 1)
    mean = jnp.mean(y, axis=-1, keepdims=True)
    var = jnp.mean(jnp.square(y - mean), axis=-1, keepdims=True)
    y = (y - mean) * lax.rsqrt(var + RWKV_GN_EPS)
    y = y.reshape(B, S, RWKV_WIDTH) * ln_w.astype(f32) + ln_b.astype(f32)
    bonus = jnp.sum(r_h * k_h * r_k.astype(f32), axis=-1, keepdims=True) * v_h
    y = (y + bonus.reshape(B, S, RWKV_WIDTH)) * g.astype(f32)
    return y.astype(z.dtype)

def second_inputs(seed: int = 0) -> dict:
    key = jax.random.key(seed)
    ks = jax.random.split(key, 32)
    f32 = jnp.float32
    nrm = lambda k, shape, scale: jax.random.normal(k, shape, f32) * scale
    gain = lambda k, n: 1.0 + 0.02 * jax.random.normal(k, (DEPTH_2, n), f32)
    L = DEPTH_2
    return {
        'x': jax.random.normal(ks[0], (BATCH, SEQ, D_MODEL), f32),
        'p': jax.random.normal(ks[1], (DEPTH_2, BATCH, SEQ, PLE_DIM), f32),
        'mix_pre_norm': gain(ks[2], D_MODEL),
        'w_in': nrm(ks[3], (L, D_MODEL, IN_COLS), D_MODEL ** -0.5),
        'rwkv_mu': jax.random.uniform(ks[4], (L, RWKV_COLS), f32, 0.2, 0.8),
        'rwkv_w0': jax.random.uniform(ks[5], (L, RWKV_WIDTH), f32, -4.0, 0.0),
        'rwkv_w2': nrm(ks[6], (L, DECAY_LORA, RWKV_WIDTH), 0.5 * DECAY_LORA ** -0.5),
        'rwkv_a0': nrm(ks[7], (L, RWKV_WIDTH), 0.1),
        'rwkv_a2': nrm(ks[8], (L, ICLR_LORA, RWKV_WIDTH), 0.5 * ICLR_LORA ** -0.5),
        'rwkv_g2': nrm(ks[9], (L, GATE_LORA, RWKV_WIDTH), GATE_LORA ** -0.5),
        'rwkv_k_k': 0.85 + 0.02 * jax.random.normal(ks[10], (L, RWKV_WIDTH), f32),
        'rwkv_k_a': 1.0 + 0.02 * jax.random.normal(ks[11], (L, RWKV_WIDTH), f32),
        'rwkv_r_k': nrm(ks[12], (L, RWKV_HEADS, HEAD_DIM), 0.1),
        'rwkv_ln_w': gain(ks[13], RWKV_WIDTH),
        'rwkv_ln_b': nrm(ks[14], (L, RWKV_WIDTH), 0.02),
        'w_attn_up': nrm(ks[15], (L, ATTN_GROUP_WIDTH, D_MODEL), ATTN_GROUP_WIDTH ** -0.5),
        'w_rwkv_up': nrm(ks[16], (L, RWKV_WIDTH, D_MODEL), RWKV_WIDTH ** -0.5),
        'w_out': nrm(ks[17], (L, D_MODEL, D_MODEL), D_MODEL ** -0.5),
        'mix_post_norm': gain(ks[18], D_MODEL),
        'ffn_pre_norm': gain(ks[19], D_MODEL),
        'w_ff_in': nrm(ks[20], (L, D_MODEL, D_FF), D_MODEL ** -0.5),
        'w_ff_out': nrm(ks[21], (L, D_FF, D_MODEL), D_FF ** -0.5),
        'ffn_post_norm': gain(ks[22], D_MODEL),
        'w_ple': nrm(ks[23], (L, PLE_DIM, D_MODEL), PLE_DIM ** -0.5),
        'w_ple_gate': nrm(ks[24], (L, D_MODEL, D_MODEL), D_MODEL ** -0.5),
        'ple_post_norm': gain(ks[25], D_MODEL),
    }

def second_block(x, p, mix_pre_norm, w_in, rwkv_mu, rwkv_w0, rwkv_w2, rwkv_a0, rwkv_a2, rwkv_g2,
              rwkv_k_k, rwkv_k_a, rwkv_r_k, rwkv_ln_w, rwkv_ln_b, w_attn_up, w_rwkv_up, w_out,
              mix_post_norm, ffn_pre_norm, w_ff_in, w_ff_out, ffn_post_norm, w_ple, w_ple_gate,
              ple_post_norm):
    h = x
    for i in range(DEPTH_2):
        u = rmsnorm_2(h, mix_pre_norm[i])
        z = u @ w_in[i]
        z_attn = z[..., :ATTN_QKV_COLS]
        z_rwkv = z[..., ATTN_QKV_COLS:ATTN_QKV_COLS + RWKV_COLS]
        z_gate = z[..., ATTN_QKV_COLS + RWKV_COLS:]
        o_attn = dilated_attention_branch(z_attn)
        o_rwkv = rwkv7_time_mix(z_rwkv, rwkv_mu[i], rwkv_w0[i], rwkv_w2[i], rwkv_a0[i],
                                rwkv_a2[i], rwkv_g2[i], rwkv_k_k[i], rwkv_k_a[i], rwkv_r_k[i],
                                rwkv_ln_w[i], rwkv_ln_b[i])
        gate_attn, gate_rwkv = jnp.split(jax.nn.sigmoid(z_gate), 2, axis=-1)
        merged = gate_attn * (o_attn @ w_attn_up[i]) + gate_rwkv * (o_rwkv @ w_rwkv_up[i])
        h = h + rmsnorm_2(merged @ w_out[i], mix_post_norm[i])
        f = rmsnorm_2(h, ffn_pre_norm[i])
        f = jnp.square(jax.nn.relu(f @ w_ff_in[i])) @ w_ff_out[i]
        h = h + rmsnorm_2(f, ffn_post_norm[i])
        e = (p[i] @ w_ple[i]) * jax.nn.sigmoid(h @ w_ple_gate[i])
        h = h + rmsnorm_2(e, ple_post_norm[i])
    return h


def setup_inputs(seed=0):
    out = dict(first_inputs(seed))
    for name, value in second_inputs(seed + 1).items():
        if name != "x":
            out[name + "_2"] = value
    return out


def reference(
    x, c, ada_w, ada_b, norm_g, even_in_w, pool_w, pool_scale, sgu_norm_g, sgu_w, sgu_b,
    even_out_w, odd_in_w, gla_gate_w, gla_gate_b, gla_norm_g, odd_out_w, final_g, p_2,
    mix_pre_norm_2, w_in_2, rwkv_mu_2, rwkv_w0_2, rwkv_w2_2, rwkv_a0_2, rwkv_a2_2, rwkv_g2_2,
    rwkv_k_k_2, rwkv_k_a_2, rwkv_r_k_2, rwkv_ln_w_2, rwkv_ln_b_2, w_attn_up_2, w_rwkv_up_2,
    w_out_2, mix_post_norm_2, ffn_pre_norm_2, w_ff_in_2, w_ff_out_2, ffn_post_norm_2, w_ple_2,
    w_ple_gate_2, ple_post_norm_2,
):
    x = first_block(
        x, c, ada_w, ada_b, norm_g, even_in_w, pool_w, pool_scale, sgu_norm_g, sgu_w, sgu_b,
        even_out_w, odd_in_w, gla_gate_w, gla_gate_b, gla_norm_g, odd_out_w, final_g,
    )
    return second_block(
        x, p_2, mix_pre_norm_2, w_in_2, rwkv_mu_2, rwkv_w0_2, rwkv_w2_2, rwkv_a0_2, rwkv_a2_2,
        rwkv_g2_2, rwkv_k_k_2, rwkv_k_a_2, rwkv_r_k_2, rwkv_ln_w_2, rwkv_ln_b_2, w_attn_up_2,
        w_rwkv_up_2, w_out_2, mix_post_norm_2, ffn_pre_norm_2, w_ff_in_2, w_ff_out_2,
        ffn_post_norm_2, w_ple_2, w_ple_gate_2, ple_post_norm_2,
    )


_drawn_inputs = setup_inputs


def setup_inputs(seed=0):
    import zlib

    import numpy as np

    out = dict(_drawn_inputs(seed))
    spreads = {}
    factors = {'pool_scale': 3.112,
     'sgu_norm_g': 7.547,
     'gla_gate_b': 7.145,
     'gla_norm_g': 6.054,
     'rwkv_k_k_2': 40.212,
     'rwkv_k_a_2': 3.747,
     'rwkv_ln_w_2': 4.226,
     'rwkv_ln_b_2': 4.034,
     'mix_post_norm_2': 4.131,
     'ffn_pre_norm_2': 12.21,
     'ffn_post_norm_2': 20.811,
     'ple_post_norm_2': 25.306}
    for name, (base, spread) in spreads.items():
        noise = np.random.default_rng([zlib.crc32(name.encode()), seed]).standard_normal(out[name].shape)
        drawn = base * np.exp(spread * noise) if base else spread * noise
        out[name] = __import__('jax').numpy.asarray(drawn.astype(out[name].dtype))
    for name, factor in factors.items():
        out[name] = (out[name] * factor).astype(out[name].dtype)
    return out
```

```python
from contextlib import ExitStack

import numpy as np

import concourse.bass as bass
from concourse import mybir
from concourse.alu_op_type import AluOpType as ALU

ACT = mybir.ActivationFunctionType
AX = mybir.AxisListType
F32 = mybir.dt.float32
F32R = mybir.dt.float32r
U32 = mybir.dt.uint32

P = 128
T = 256
D = 1024
KD = D // P
UNIT = 2048
CB = 256
RAW = 3
SPL = 3
NBANK = 4
EPS = 1e-6
WINDOWS = (2, 4, 8, 16)
PAD = max(WINDOWS)
GLA_H, GLA_C, GLA_TAU = 4, 64, 16.0
SB_H = 8
AT_G, AT_H, HD = 3, 4, 64
AT_W = AT_H * HD
AT_SPANS = ((128, 1), (512, 4), (2048, 16))
RW_H, RW_C = 8, 128
GN_EPS = 64e-5
KAPPA = float(np.exp(-0.5))
MASKED = -1e30



def constants():
    p = np.arange(P)
    row, col = p[:, None], p[None, :]
    t = np.arange(T)
    f = lambda a: np.ascontiguousarray(a, np.float32)
    out = {
        "ident": f(row == col),
        "ones": f(np.ones((P, P))),
        "ones_head": f(row // HD == col // HD),
        "upto": f(row <= col),
        "before": f(row < col),
        "from_here": f(row >= col),
        "gla_mask": f(np.tile((row <= col) & (row // GLA_C == col // GLA_C), (1, 2))),
        "gla_run": f(np.tile(t % GLA_C != 0, (P, 1))),
        "rw_run": f(np.tile(t % RW_C != 0, (P, 1))),
        "sb_mask": f(np.concatenate([row < col, np.ones((P, P)), row < col], 1)),
    }
    out["sb_neg"] = f(np.where(out["sb_mask"] > 0, 0.0, MASKED))
    out["inv_count"] = f(np.tile(np.concatenate([1.0 / np.minimum(t + 1, w) for w in WINDOWS])[None], (P, 1)))
    inv_freq = 10000.0 ** (-np.arange(0, HD, 2) / HD)
    ang = (t[:, None].astype(np.float32) * inv_freq[None].astype(np.float32)).astype(np.float32)
    cos, sin = np.cos(ang).T, np.sin(ang).T
    out["cos"] = f(np.tile(cos, (4, 1)))
    out["sin"] = f(np.concatenate([-sin, sin, -sin, sin], 0))
    for i in range(2):
        tt = i * P + p[:, None]
        s = np.arange((i + 1) * P)[None]
        out[f"at_neg{i}"] = f(np.concatenate(
            [np.where((tt >= s) & ((tt - s) % dil == 0) & (tt - s <= win), 0.0, MASKED) for win, dil in AT_SPANS], 1))
    b = 1
    while b < RW_C:
        m = (row // (2 * b) == col // (2 * b)) & ((row // b) % 2 == 1) & ((col // b) % 2 == 0)
        out[f"pair{b}"] = f(m)
        b *= 2
    out["pair1_t"] = f(out["pair1"].T)
    return out


def layout(sizes):
    at, places = 0, {}
    for name, n in sizes:
        places[name] = (at, n)
        at += n
    return places, at


BASE = ("ident", "ones", "ones_head", "before", "upto", "from_here")
ODD_ONLY = ("gla_mask", "gla_run", "sb_mask", "sb_neg")
PHASES = (BASE, ("inv_count",), ODD_ONLY,
          tuple(k for k in constants() if k not in BASE + ODD_ONLY + ("inv_count",)))
CONST_PLACES = [layout([(k, constants()[k].shape[1]) for k in ph]) for ph in PHASES]
CONST_AT = [sum(c[1] for c in CONST_PLACES[:i]) for i in range(5)]

ROWS_A, NROWS_A = layout([("ada_b", 48), ("norm_g", 16), ("pool_scale", 8), ("sgu_norm_g", 8), ("gla_gate_b", 4),
                          ("gla_norm_g", 8), ("final_g", 8)])
ROWS_B, NROWS_B = layout([("mix_pre_norm_2", 8), ("rwkv_mu_2", 14), ("rwkv_w0_2", 4), ("rwkv_a0_2", 4),
                          ("rwkv_k_k_2", 4), ("rwkv_k_a_2", 4), ("rwkv_r_k_2", 4), ("rwkv_ln_w_2", 4),
                          ("rwkv_ln_b_2", 4), ("mix_post_norm_2", 8), ("ffn_pre_norm_2", 8),
                          ("ffn_post_norm_2", 8), ("ple_post_norm_2", 8)])

WORK, SPARE = 58, 100
S_ = dict(sq=0, h=8, r=34, k=38, v=42, xx=56, zr=16, zk=21, zv=26, zx=31, lora=52,
          sw=21, a=16, cs=25, cc=29, er=SPARE, kk=SPARE + 4, rn=SPARE + 8, kt=SPARE + 12, rk=SPARE + 16,
          ar=0, b=8, kb=12, bonus=SPARE + 20, vt=SPARE + 24, bt=SPARE + 28, kbt=SPARE + 30, sets=16, y=48,
          gsum=0, grs2=8, q=SPARE, ak=SPARE + 6, av=SPARE + 12, swap=50,
          gate=16, sc=32, pt=38, oa=44, m=0, prod=32, o=32, osq=40, sg=16, yt=20, f=24, p_in=40, p=42, e=44)
N_ROW_LOADS = 22
E_ = dict(v=0, a=8, lev1=17, lev2=26, u=35, wraw=43, wt=47, bb=51, sq=0, h=35, vsq=35, sg=26, yt=30, z=34, inv=SPARE + 8)
O_ = dict(q=0, ki=4, sqq=8, skk=16, svv=24, sb=32, sg=40, yt=44, sq=8, h=16,
          k=SPARE, v=SPARE + 4, kt=SPARE + 12, t1=SPARE + 16, la=SPARE + 20, e=SPARE + 24, sqt=SPARE + 28,
          rs=SPARE + 30, glr=SPARE + 31, st=SPARE + 16, att=SPARE + 22)


STOP = None


def program(nc, ins, consts, out, stop=None):
    x_in = ins["x"].rearrange("a (n p) d -> p (a n) d", p=P)
    out_t = out.rearrange("a (n p) d -> p (a n) d", p=P)

    units, jobs, schedule, ada_units = [], {}, [], []

    def unit(w, k0, nk, c0, nc_, ada=None):
        units.append(dict(src=w[k0 * P:(k0 + nk) * P, c0:c0 + nc_].rearrange("(k p) n -> p k n", p=P),
                          nk=nk, n=nc_, ada=ada, order=len(units), index=sum(u["ada"] is None for u in units)))
        return len(units) - 1

    def job(name, kind, i, layout_, unit_list, nk, x0, ready, col=0, k0=0, blocks=(P, P)):
        steps = [(u, k0 + k, x0 + n * nk + k) for n, u in enumerate(unit_list) for k in range(nk)]
        jobs[name, i] = dict(order=len(jobs), kind=kind, i=i, layout=layout_, steps=steps, ready=ready, col=col,
                             blocks=blocks, name=name)
        schedule.append(("job", (name, i)))

    def proj(name, kind, w, c0, n, x0, ready, layout_="F", kparts=1, krow=0, kmap=None):
        for i in range(n):
            us = [unit(w, krow + KD * kp, KD, c0 + i * CB, CB) for kp in range(kparts)]
            job(name, kind, i, layout_, us, KD, x0, ready)

    def step(name, i=None):
        schedule.append(("step", (name, i)))

    def ada(layer, part, i):
        c0 = part * D + i * CB
        ada_units.append(unit(ins["ada_w"][layer], 0, KD, c0, CB, ada=(layer, c0 // P, len(ada_units))))
        schedule.append(("ada", ada_units[-1]))

    even_w, odd_w, w2nd = ins["even_in_w"][0], ins["odd_in_w"][0], ins["w_in_2"][0]
    HR = lambda n: (lambda xc: ("operand_ready", 8 * n + xc + 1))
    later_ada = [(0, 2, i) for i in range(4)] + [(1, part, i) for part in range(3) for i in range(4)]

    def even(name, kind, w, c0, layout_="F"):
        for i in range(4):
            job(name, kind, i, layout_, [unit(w, 0, KD, c0 + i * CB, CB)], KD, 0, HR(0))
            if i < 3 and len(later_ada) > 4:
                ada(*later_ada.pop(0))

    step("load_x")
    for part in range(2):
        for i in range(4):
            ada(0, part, i)
    step("params")
    step("ada_first")
    step("norm", 0)
    even("ev", "copy_t", even_w, 2048, "T")
    step("sgu_w")
    even("ea", "copy", even_w, 0)
    step("sgu_v")
    step("windows", 0)
    for i in range(4):
        job("eu", "copy", i, "F", [unit(even_w, 0, KD, 1024 + i * CB, CB)], KD, 0, HR(0))
        if i < 3:
            ada(*later_ada.pop(0))
            step("windows", i + 1)
    for i in range(4):
        step("sgu_z", i)
    even("egb", "gate", even_w, 4096)
    step("ada_rest")
    pool_u = unit(ins["pool_w"][0].rearrange("g c d -> (g c) d"), 0, 8, 0, CB)
    for g in range(4):
        job("pool", "pool", g, "F", [pool_u], 2, 8 + 2 * g, lambda xc: ("p_lo", 1), k0=2 * g)
    even("ega", "gate", even_w, 3072)
    proj("eo", "residual", ins["even_out_w"][0], 0, 4, 8, lambda xc: ("y_lo", 8), kparts=2)
    if stop != "even":
        def odd(name, kind, c0, i, layout_="F", n=CB, blocks=(P, P)):
            job(name, kind, i, layout_, [unit(odd_w, 0, KD, c0 + i * CB, n)], KD, 0, HR(1), blocks=blocks)

        stages = []

        def pipeline(names, n):
            for slot in range(n + len(names) - 1):
                yield [(names[k], slot - k) for k in reversed(range(len(names))) if 0 <= slot - k < n]

        step("norm", 1)
        for i in range(2):
            odd("gk", "copy", 512, i)
            ada(*later_ada.pop(0))
        odd("glr", "copy16", 2048, 0, n=16, blocks=(16,))
        odd("gq", "copy", 0, 0)
        ada(*later_ada.pop(0))
        step("gla_z")
        odd("gq", "copy", 0, 1)
        for i in range(4):
            odd("gv", "copy_t", 1024, i, "T")
            if i == 0:
                ada(*later_ada.pop(0))
            if i == 1:
                step("ada_last")
                step("gla_decay")
        odd("sq", "copy", 2064, 0)
        step("gla_kt")
        gla = pipeline(("gla_att", "gla_o", "gla_n"), GLA_H)
        sbs = pipeline(("sb_z", "sb_c", "sb_o"), SB_H)
        order = [("sk", "copy", 3088, 0), ("sv", "copy_t", 4112, 0)]
        for i in range(1, 4):
            order += [("sq", "copy", 2064, i), ("sk", "copy", 3088, i), ("sv", "copy_t", 4112, i)]
        for n, (name, kind, c0, i) in enumerate(order):
            odd(name, kind, c0, i, "T" if kind == "copy_t" else "F")
            for st in next(gla, None) or next(sbs, []):
                step(*st)
        left = list(sbs)
        for i in range(4):
            odd("gga", "gate", 5136, i)
            for sts in left[:1]:
                for st in sts:
                    step(*st)
            left = left[1:]
        for sts in left:
            for st in sts:
                step(*st)
        for i in range(4):
            odd("ggb", "gate", 6160, i)
        proj("oo", "residual", ins["odd_out_w"][0], 0, 4, 8, lambda xc: ("y_lo", 16), kparts=2)
        step("final_norm")
    if stop is None:
        def second(name, kind, c0, i, layout_="F", n=CB, blocks=(P, P)):
            job(name, kind, i, layout_, [unit(w2nd, 0, KD, c0 + i * CB, n)], KD, 0, HR(2), blocks=blocks)

        step("mix_pre")
        second("wx", "wx", 3840, 0, n=160, blocks=(64, 96))
        for name, c0 in (("wk", 2816), ("wv", 3328), ("wr", 2304)):
            for i in range(2):
                second(name, "shifted", c0, i)
            step({"wk": "shift_k", "wr": "shift_r", "wv": "shift_v"}[name])
            if name == "wk":
                step("lora_w")
            if name == "wr":
                step("lora_a")
        attn = [("aq", "rope", 0, i, "F") for i in range(3)] + [("ak", "rope", 768, i, "F") for i in range(3)]
        attn += [("av", "copy_t", 1536, i, "T") for i in range(3)]

        def more():
            if attn:
                second(*attn.pop(0))

        step("head_norms")
        more()
        step("turn_v")
        step("bonus")
        more()
        step("turn_bk")
        more()
        for c in range(2):
            step("rw_pairs", c)
            more()
            for n in range(6):
                step("rw_u", 6 * c + n)
                step("rw_t", 6 * c + n)
                if n % 3 == 2:
                    more()
            step("rw_solve", c)
        while attn:
            more()
        at = pipeline(("at_s", "at_t", "at_o"), 2 * AT_H)
        step("gn_mean")
        for i in range(4):
            second("wga", "sigmoid", 4000, i)
            if i == 1:
                step("rw_gate")
            for st in next(at, []):
                step(*st)
            if i == 0:
                step("gn_var")
        for i in range(4):
            second("wgb", "sigmoid", 5024, i)
            for st in next(at, []):
                step(*st)
        for sts in at:
            for st in sts:
                step(*st)
        step("mixed")
        for i in range(0, 4, 2):
            us = unit(ins["w_rwkv_up_2"][0], 0, 4, i * CB, 2 * CB)
            for k in range(2):
                job("ru", "up", i + k, "F", [us], 4, 8, lambda xc: ("mixed_lo", 1), col=k * CB)
        us = unit(ins["w_attn_up_2"][0], 0, 2, 0, 4 * CB)
        for i in range(4):
            job("au", "up", i, "F", [us], 2, 12, lambda xc: ("mixed_lo", 2), col=i * CB)
        proj("wo", "out", ins["w_out_2"][0], 0, 4, 16, lambda xc: ("merged_lo", (xc - 16) // 2 + 1))
        step("mix_post")
        step("ffn_pre")
        for half in range(2):
            for i in range(8):
                job("fi", "relu2", 8 * half + i, "F", [unit(ins["w_ff_in_2"][0], 0, KD, (8 * half + i) * CB, CB)], KD, 0, HR(3))
            for i in range(4):
                us = [unit(ins["w_ff_out_2"][0], 16 * half + 8 * kp, KD, i * CB, CB) for kp in range(2)]
                job(f"fo{half}", f"ffn{half}", i, "F", us, KD, 8, lambda xc, half=half: ("y_lo", 16 + 8 * (half + 1)))
        step("turn_p")
        us = unit(ins["w_ple_2"][0], 0, 2, 0, 4 * CB)
        for i in range(4):
            job("pe", "ple", i, "F", [us], 2, 8, lambda xc: ("p_lo", 2), col=i * CB)
        step("ffn_post")
        step("ple_x")
        for i in range(4):
            job("pg", "ple_gate", i, "F", [unit(ins["w_ple_gate_2"][0], 0, KD, i * CB, CB)], KD, 0, HR(4))
        step("ple_post")
    step("store")

    visits = 0
    for j in jobs.values():
        for u in sorted({u for u, _, _ in j["steps"]}):
            visits += 1
            units[u]["visited"] = visits
        j["projected"] = visits

    ctx = ExitStack()
    with ctx:
        def sb(name, shape, dt=F32):
            return ctx.enter_context(nc.sbuf_tensor(name, shape, dt))

        sems = {}

        def S(name):
            if name not in sems:
                sems[name] = ctx.enter_context(nc.semaphore(name))
            return sems[name]

        raw = sb("raw", [P, RAW, UNIT])
        w_hi = sb("w_hi", [P, SPL, UNIT], F32R)
        w_lo = sb("w_lo", [P, SPL, UNIT], F32R)
        h_hi = sb("h_hi", [P, KD, T], F32R)
        h_lo = sb("h_lo", [P, KD, T], F32R)
        x = sb("x", [P, KD, T])
        cst = sb("cst", [P, CONST_PLACES[0][1]])
        cst_phase = sb("cst_phase", [P, max(CONST_PLACES[2][1], CONST_PLACES[3][1])])
        rows = sb("rows", [P, 2, P])
        cols = sb("cols", [P, 2, P])
        ada_c = sb("ada_c", [P, 2, 24])
        mod = sb("mod", [P, 2, KD])
        silu_c = sb("silu_c", [P, KD])
        small = sb("small", [P, 64])
        rstd = sb("rstd", [P, T])
        s0 = sb("s0", [P, 4, HD])
        work = sb("work", [P, WORK, T])
        with nc.sbuf_tensor("spare", [P, 32, T], F32) as spare:
            pass
        y_hi = sb("y_hi", [P, 16, T], F32R)
        y_lo = sb("y_lo", [P, 16, T], F32R)
        PJ = [ctx.enter_context(nc.psum_tensor(f"pj{i}", [P, 512], F32)) for i in range(NBANK)]
        M = [ctx.enter_context(nc.psum_tensor(f"m{i}", [P, 512], F32)) for i in range(4)]

        def ar(c, n=1):
            return work[:, c:c + n, :] if c < SPARE else spare[:, c - SPARE:c - SPARE + n, :]

        def flat(c, n):
            return ar(c, n).rearrange("p c t -> p (c t)")

        def K(name):
            for ph, (places, _) in enumerate(CONST_PLACES):
                if name in places:
                    a, n = places[name]
                    return (cst, flat(E_["inv"], 4), cst_phase, cst_phase)[ph][:, a:a + n]
            raise KeyError(name)

        def vec(name, i=0, n=1):
            places, half = (ROWS_A, 0) if name in ROWS_A else (ROWS_B, 1)
            return cols[:, half, places[name][0] + i:places[name][0] + i + n]

        def bc(ap, n, at=1):
            shape = list(ap.shape)
            return ap.unsqueeze(at).broadcast_to(shape[:at] + [n] + shape[at:])

        def operand(part, xc):
            h, y = ((h_hi, y_hi), (h_lo, y_lo))[part]
            return h[:, xc, :] if xc < KD else y[:, xc - KD, :]

        last_raw = {}

        def evacuated(eng, key):
            n = jobs[key]["order"]
            eng.wait_ge(S(f"evacuated{n % NBANK}"), n // NBANK + 1)

        def projected(eng, key):
            eng.wait_ge(S("projected"), jobs[key]["projected"])

        def bank_of(key):
            return PJ[jobs[key]["order"] % NBANK]

        def done_reading(ins_, key):
            ins_.then_inc(S(f"evacuated{jobs[key]['order'] % NBANK}"), 1)

        for k in range(4):
            S(f"evacuated{k}")
        for k in range(RAW):
            S(f"unit_loaded{k}")

        dest = {"ev": E_["v"], "ea": None, "eu": E_["u"], "gq": O_["q"], "gk": O_["k"], "gv": O_["v"],
                "sq": O_["sqq"], "sk": O_["skk"], "sv": O_["svv"], "av": S_["av"]}
        shifted = {"wr": (S_["zr"], S_["r"], 4, 0), "wk": (S_["zk"], S_["k"], 4, 4), "wv": (S_["zv"], S_["v"], 4, 8),
                   "wx": (S_["zx"], S_["xx"], 2, 12)}
        a_pad = work[:, E_["a"]:E_["a"] + 9, :].rearrange("p c t -> p (c t)")[:, 0:8 * (T + PAD)].rearrange(
            "p (c t) -> p c t", c=8)
        lev = [work[:, c:c + 9, :].rearrange("p c t -> p (c t)")[:, 0:8 * (T + PAD)].rearrange(
            "p (c t) -> p c t", c=8) for c in (E_["lev1"], E_["lev2"])]
        gates = [k for kind, k in schedule if kind == "job" and jobs[k]["kind"] in ("gate", "relu2")]
        ropes = [k for kind, k in schedule if kind == "job" and jobs[k]["kind"] == "rope"]
        gate_mix = {"egb": lambda i: (ar(E_["u"] + 2 * i, 2), 8 + 2 * i),
                    "ega": lambda i: (a_pad[:, 2 * i:2 * i + 2, PAD:], 2 * i),
                    "gga": lambda i: (GO(i), 2 * i),
                    "ggb": lambda i: (ar(O_["sqq"] + 2 * i, 2), 8 + 2 * i)}

        def GO(h):
            return work[:, O_["q"]:O_["q"] + 8, :].rearrange("p (b c) t -> p b c t", c=4)[:, :, h, :]

        s0_flat = s0[:, :, :].rearrange("p b d -> p (b d)")
        ada_acc = (flat(55, 1), s0_flat)
        c_rows = s0_flat[0:KD, 0:P]
        v_tok = flat(E_["v"], 8).rearrange("p (n d) -> p n d", n=2)
        w_raw = flat(E_["wraw"], 4).rearrange("p (h s) -> p h s", h=8)
        w_t = flat(E_["wt"], 4).rearrange("p (h s) -> p h s", h=8)
        b_all = flat(E_["bb"], 4).rearrange("p (h s) -> p h s", h=8)
        gv_tok = flat(O_["v"], 8).rearrange("p (n d) -> p n d", n=2)
        kt = flat(O_["kt"], 4).rearrange("p (h n k) -> p h n k", h=GLA_H, n=2)
        sv_tok = flat(O_["svv"], 8).rearrange("p (n d) -> p n d", n=2)

        small_zero = small[:, 40:41]
        eps_col = small[:, 41:42]
        gn_eps_col = small[:, 42:43]
        gate_w = work[0:16, 56:58, :].rearrange("p c t -> p (c t)")
        ar_ = flat(S_["ar"], 8).rearrange("p (b c k t) -> p b c k t", b=4, c=2, k=2)
        b_f = flat(S_["b"], 4).rearrange("p (b t) -> p b t", b=4)
        kb_f = flat(S_["kb"], 4).rearrange("p (b t) -> p b t", b=4)
        r_f, k_f, v_f = (flat(S_[n], 4).rearrange("p (b t) -> p b t", b=4) for n in "rkv")
        xx = flat(S_["xx"], 2).rearrange("p (b t) -> p b t", b=2)
        lora = flat(S_["lora"], 4).rearrange("p (w n) -> p w n", w=2)
        vt = flat(S_["vt"], 4).rearrange("p (c n) -> p c n", c=2)
        bt, kbt = flat(S_["bt"], 2), flat(S_["kbt"], 2)
        y_f = flat(S_["y"], 4).rearrange("p (b t) -> p b t", b=4)
        av_tok = flat(S_["av"], 6).rearrange("p (n d) -> p n d", n=2)
        oa = ar(S_["oa"], 2)
        log_decay = -KAPPA

        def zpad(name):
            at, _, n, _ = shifted[name]
            return flat(at, 5 if n == 4 else 3)[:, 0:n * (T + 1)].rearrange("p (b t) -> p b t", b=n)

        def rset(s):
            c = S_["sets"] + 16 * s
            nm_b = flat(c, 4).rearrange("p (q w) -> p q w", q=4)
            nm_k = flat(c + 4, 4).rearrange("p (q w) -> p q w", q=4)
            t_, tt_, um = (flat(c + 8 + 2 * i, 2).rearrange("p (q w) -> p q w", q=4) for i in range(3))
            return nm_b, nm_k, t_, tt_, um

        w0_all, u_all = flat(S_["sets"] + 14, 2), flat(S_["sets"] + 30, 2)

        def head_of(s, q):
            return 2 * s + q % 2, q // 2

        def wcol(s, q):
            c = (q // 2) * 256 + s * 128 + (q % 2) * HD
            return slice(c, c + HD)

        def sc(n):
            return flat(S_["sc"] + 3 * (n % 2), 3)[:, 0:(n % 2 + 1) * 384]

        def pt(n):
            return flat(S_["pt"] + 3 * (n % 2), 3)

        split_units = [u for u in units if u["ada"] is None]
        last_unit = {key: units[j["steps"][-1][0]]["index"] for key, j in jobs.items()}

        def normed_at(n):
            return ar((E_["h"], O_["h"], S_["h"], S_["h"], S_["h"])[n], 8)

        def gate_tmp(which, g):
            places = E_ if g < 8 else O_ if g < 16 else S_
            return ar(places[which] + 2 * (g % 2), 2)

        def gst(h, c):
            return flat(O_["st"] + 3 * (h % 2) + c, 1)

        def gatt(h):
            return flat(O_["att"] + h % 2, 1)

        def sbw(k):
            return flat(O_["sb"], 8)[:, 384 * k:384 * (k + 1)]

        def run(steps, job_part, split_to, ada_part=None):
            for kind, what in schedule:
                if kind == "job":
                    if split_to is not None:
                        split_to(last_unit[what] + SPL)
                    job_part(what)
                elif kind == "ada" and ada_part:
                    ada_part(what)
                elif kind == "step" and what[0] in steps:
                    if what[1] is None:
                        steps[what[0]]()
                    else:
                        steps[what[0]](what[1])

        block = ctx.enter_context(nc.Block())

        @block.sync
        def _(sp):
            sp.dma_start(c_rows, ins["c"].rearrange("a (n p) -> (a n) p", p=P)).then_inc(S("c_in"), 16)
            for u, un in enumerate(units):
                if u >= RAW:
                    old = units[u - RAW]
                    if old["ada"] is None:
                        sp.wait_ge(S("split"), old["index"] + 1)
                    else:
                        sp.wait_ge(S("ada_acc"), old["ada"][2] + 1)
                sp.dma_start(raw[:, u % RAW, 0:un["nk"] * un["n"]].rearrange("p (k n) -> p k n", k=un["nk"]),
                             un["src"]).then_inc(S(f"unit_loaded{u % RAW}"), 16)

        def unit_loaded(eng, u):
            eng.wait_ge(S(f"unit_loaded{u % RAW}"), 16 * (u // RAW + 1))

        def chainer(eng, name):
            count = [0]

            def link(ins_):
                count[0] += 1
                ins_.then_inc(S(name), 1)
                eng.wait_ge(S(name), count[0])
            return link

        @block.gpsimd
        def _(pool):
            pool.memset(small_zero, 0.0).then_inc(S("scalars_set"), 1)
            pool.memset(gn_eps_col, GN_EPS).then_inc(S("scalars_set"), 1)
            pool.memset(eps_col, EPS).then_inc(S("scalars_set"), 1)
            pool.memset(rows[:, :, :], 0.0).then_inc(S("rows_zero"), 1)
            pool.memset(a_pad[:, :, 0:PAD], 0.0).then_inc(S("pad_zero"), 1)
            pool.memset(lev[0][:, :, 0:PAD], 0.0).then_inc(S("pad_zero"), 1)
            pool.memset(lev[1][:, :, 0:PAD], 0.0).then_inc(S("pad_zero"), 1)
            pool.wait_ge(S("rows_zero"), 1)
            n = 0

            def load_rows(half, r, src):
                pool.dma_start(rows[r:r + src.shape[0], half, 0:src.shape[1]], src).then_inc(S("rows_loaded"), 16)

            for half, places in ((0, ROWS_A), (1, ROWS_B)):
                for name, (r, nr) in places.items():
                    a = ins[name]
                    if name == "rwkv_mu_2":
                        load_rows(half, r, a[0:1, 0:1536].rearrange("a (n p) -> (a n) p", p=P))
                        load_rows(half, r + 12, a[0:1, 1536:1600])
                        load_rows(half, r + 13, a[0:1, 1600:1696])
                        n += 3
                        continue
                    if name == "gla_norm_g":
                        a = a.rearrange("a h (n p) -> (a h n) p", p=P)
                    elif name == "rwkv_r_k_2":
                        a = a.rearrange("a (b h) d -> (a b) (h d)", h=2)
                    elif len(a.shape) == 1:
                        a = a.rearrange("(n p) -> n p", p=P)
                    else:
                        a = a.rearrange("a (n p) -> (a n) p", p=P)
                    load_rows(half, r, a)
                    n += 1
            assert n == N_ROW_LOADS, n
            if stop is None:
                pool.wait_ge(S("sb_arg"), SB_H)
                pool.wait_ge(S("sb_y"), SB_H)
                pool.wait_ge(S("gla_states"), GLA_H)
                pool.dma_start(cst_phase[:, 0:CONST_PLACES[3][1]], consts[:, CONST_AT[3]:CONST_AT[4]]).then_inc(S("late_in"), 16)
                pool.dma_start(lora[0:32, 0, :], ins["rwkv_w2_2"][0]).then_inc(S("late_in"), 16)
                pool.dma_start(lora[32:64, 0, :], ins["rwkv_a2_2"][0]).then_inc(S("late_in"), 16)
                pool.dma_start(lora[0:96, 1, :], ins["rwkv_g2_2"][0]).then_inc(S("late_in"), 16)
                pool.wait_ge(S("operand_ready"), 24)
                for name in ("wr", "wk", "wv", "wx"):
                    pool.memset(zpad(name)[:, :, 0:1], 0.0).then_inc(S("zpad"), 1)
                pool.wait_ge(S("operand_ready"), 32)
                pool.dma_start(ar(S_["p_in"], 2), ins["p_2"][0, 0].rearrange("(n p) d -> p n d", p=P)).then_inc(S("p_in"), 16)

        @block.scalar
        def _(act):
            link = chainer(act, "act_chain")
            act.dma_start(cst[:, :], consts[:, CONST_AT[0]:CONST_AT[1]]).then_inc(S("const_in"), 16)
            act.dma_start(ar(0, 8).rearrange("p (n c) t -> p n (c t)", n=2), x_in).then_inc(S("x_in"), 16)
            act.dma_start(flat(E_["inv"], 4), consts[:, CONST_AT[1]:CONST_AT[2]]).then_inc(S("inv_in"), 16)
            act.dma_start(cst_phase[:, 0:CONST_PLACES[2][1]], consts[:, CONST_AT[2]:CONST_AT[3]]).then_inc(S("odd_const_in"), 16)
            act.dma_start(gate_w, ins["gla_gate_w"][0]).then_inc(S("gate_w_in"), 16)
            act.dma_start(w_raw, ins["sgu_w"][0].rearrange("h t s -> t h s")).then_inc(S("sgu_in"), 16)
            act.dma_start(b_all, ins["sgu_b"][0].rearrange("h t -> (h t)").partition_broadcast(P).rearrange("p (h t) -> p h t", h=8)).then_inc(S("sgu_in"), 16)
            next_split = [0]

            def split_to(end):
                while next_split[0] < min(end, len(split_units)):
                    i = next_split[0]
                    next_split[0] += 1
                    u, n = split_units[i]["order"], split_units[i]["nk"] * split_units[i]["n"]
                    unit_loaded(act, u)
                    if i >= SPL:
                        act.wait_ge(S("projected"), split_units[i - SPL]["visited"])
                    nc.scalar.activation(w_hi[:, i % SPL, 0:n], raw[:, u % RAW, 0:n], ACT.Copy).then_inc(S("split_hi"), 1)

            def squares(n, src, sq, wait):
                for q in range(4):
                    wait(act, q)
                    nc.scalar.activation(ar(sq + 2 * q, 2), src[:, 2 * q:2 * q + 2, :], ACT.Square).then_inc(S("squares"), 1)
                link(nc.scalar.activation(small[:, 44:45], eps_col, ACT.Sqrt))
                act.wait_ge(S("sum_sq"), n + 1)
                nc.scalar.activation(rstd[:, :], M[0][:, 0:T], ACT.Sqrt, bias=eps_col, scale=1.0 / D).then_inc(S("rstd"), 1)

            def upper(n):
                for k in range(KD):
                    act.wait_ge(S("normed"), 8 * n + k + 1)
                    nc.scalar.activation(h_hi[:, k, :], normed_at(n)[:, k, :], ACT.Copy).then_inc(S("operand_hi"), 1)

            def load_x():
                act.wait_ge(S("c_turned"), 1)
                nc.scalar.activation(silu_c[:, :], PJ[0][:, 0:KD], ACT.Silu).then_inc(S("silu_c"), 1)
                for q in range(4):
                    act.wait_ge(S("x_turned"), q + 1)
                    nc.scalar.activation(x[:, 2 * q:2 * q + 2, :], M[q][:, :].rearrange("p (c t) -> p c t", c=2), ACT.Copy).then_inc(S("x_ready"), 1)

            def params():
                act.wait_ge(S("params_turned"), 1)
                nc.scalar.activation(cols[:, :, :], PJ[1][:, 0:2 * P].rearrange("p (c t) -> p c t", c=2), ACT.Copy).then_inc(S("params"), 1)

            def norm(n):
                if n == 0:
                    squares(0, x, E_["sq"], lambda e, q: e.wait_ge(S("x_ready"), q + 1))
                    split_to(1)
                else:
                    squares(1, x, O_["sq"], lambda e, q: evacuated(e, ("eo", q)))
                upper(n)

            def final_norm():
                squares(2, x, O_["sq"], lambda e, q: evacuated(e, ("oo", q)))

            def sgu_v():
                for tt in range(2):
                    for i in range(4):
                        evacuated(act, ("ev", i))
                    if tt == 1:
                        act.wait_ge(S("v_sq"), 1)
                    nc.scalar.activation(flat(E_["vsq"], 4), v_tok[:, tt, :], ACT.Square, accum_out=small[:, tt:tt + 1]).then_inc(S("v_sq"), 1)
                act.wait_ge(S("v_sq"), 2)
                link(nc.scalar.activation(small[:, 2:4], small[:, 0:2], ACT.Ln, bias=eps_col, scale=1.0 / D))
                nc.scalar.activation(small[:, 4:6], small[:, 2:4], ACT.Exp, scale=-0.5).then_inc(S("v_rstd"), 1)

            def windows(part):
                if part < 3:
                    return
                act.wait_ge(S("p"), 1)
                nc.scalar.activation(y_hi[:, 0:8, :], lev[0][:, :, PAD:], ACT.Copy).then_inc(S("p_hi"), 1)

            def gla_z():
                for h in range(GLA_H):
                    act.wait_ge(S("gla_z"), h // 2 + 1)
                    nc.scalar.activation(ar(O_["la"] + h), M[h // 2][:, (h % 2) * T:(h % 2 + 1) * T].unsqueeze(1), ACT.Identity,
                                         bias=vec("gla_gate_b", h)).then_inc(S("gla_la"), 1)
                act.wait_ge(S("gla_la"), 4)
                link(nc.scalar.activation(flat(O_["t1"], 4), flat(O_["la"], 4), ACT.Abs))
                link(nc.scalar.activation(flat(O_["t1"], 4), flat(O_["t1"], 4), ACT.Exp, scale=-1.0))
                nc.scalar.activation(flat(O_["t1"], 4), flat(O_["t1"], 4), ACT.Ln, bias=1.0).then_inc(S("gla_l1p"), 1)

            def gla_decay():
                act.wait_ge(S("gla_cum"), 1)
                nc.scalar.activation(flat(O_["e"], 4), flat(O_["la"], 4), ACT.Exp, scale=1 / GLA_TAU).then_inc(S("gla_exp"), 1)
                act.wait_ge(S("gla_t1_free"), 1)
                nc.scalar.activation(flat(O_["t1"], 4), flat(O_["la"], 4), ACT.Exp, scale=-1 / GLA_TAU).then_inc(S("gla_exp"), 1)
                act.wait_ge(S("gla_rest"), 1)
                nc.scalar.activation(flat(O_["t1"], 4), flat(O_["t1"], 4), ACT.Exp, scale=1 / GLA_TAU).then_inc(S("gla_exp"), 1)

            def gla_kt():
                for b in range(2):
                    act.wait_ge(S("gla_kt_turned"), b + 1)
                    nc.scalar.activation(flat(O_["kt"] + 2 * b, 2), M[b][:, :], ACT.Copy).then_inc(S("gla_kt"), 1)

            def gla_o(h):
                act.wait_ge(S("gla_o_done"), h + 1)
                nc.scalar.activation(GO(h), M[2][:, :].rearrange("p (c t) -> p c t", c=2), ACT.Copy).then_inc(S("gla_o"), 1)
                if h >= 1:
                    act.wait_ge(S("gla_ss"), h)
                nc.scalar.activation(flat(O_["sqt"], 2), M[2][:, :], ACT.Square).then_inc(S("gla_sq"), 1)

            def gla_n(h):
                act.wait_ge(S("gla_ss"), h + 1)
                if h >= 1:
                    act.wait_ge(S("gla_yc"), h)
                link(nc.scalar.activation(flat(O_["rs"], 1), M[3][:, 0:T], ACT.Ln, bias=eps_col, scale=1.0 / 256))
                nc.scalar.activation(flat(O_["rs"], 1), flat(O_["rs"], 1), ACT.Exp, scale=-0.5).then_inc(S("gla_rs"), 1)

            def sb_z(h):
                act.wait_ge(S("sb_z_done"), h + 1)
                if h >= 1:
                    act.wait_ge(S("sb_arg"), h)
                z = sbw(0)
                scale = float(P) ** -0.5
                nc.scalar.activation(z, M[0][:, 0:384], ACT.Copy, scale=scale).then_inc(S("sb_zs"), 1)
                if h >= 1:
                    act.wait_ge(S("sb_l"), h)
                link(nc.scalar.activation(sbw(1), M[0][:, 0:384], ACT.Abs, scale=scale))
                link(nc.scalar.activation(sbw(1), sbw(1), ACT.Exp, scale=-1.0))
                nc.scalar.activation(sbw(1), sbw(1), ACT.Ln, bias=1.0).then_inc(S("sb_l1p"), 1)

            def sb_c(h):
                act.wait_ge(S("sb_arg"), h + 1)
                if h >= 1:
                    act.wait_ge(S("sb_o_done"), h)
                nc.scalar.activation(sbw(4), sbw(3), ACT.Exp).then_inc(S("sb_w"), 1)

            def sb_o(h):
                act.wait_ge(S("sb_o_done"), h + 1)
                nc.scalar.activation(ar(O_["sqq"] + h), M[2][:, 0:T].unsqueeze(1), ACT.Copy).then_inc(S("sb_y"), 1)

            def mix_pre():
                squares(3, x, S_["sq"], lambda e, q: e.wait_ge(S("x_update"), 2 * q + 2))
                upper(2)

            def lora_w():
                act.wait_ge(S("shift"), 1)
                nc.scalar.activation(xx[0:32, 0, :], xx[0:32, 0, :], ACT.Tanh).then_inc(S("lora_x"), 1)
                act.wait_ge(S("lora_w"), 1)
                for b in range(4):
                    nc.scalar.activation(flat(S_["sw"] + b, 1), M[2 + b // 2][:, (b % 2) * T:(b % 2 + 1) * T], ACT.Sigmoid, bias=vec("rwkv_w0_2", b)).then_inc(S("sw"), 1)

            def lora_a():
                act.wait_ge(S("lora_a"), 1)
                act.wait_ge(S("shift"), 3)
                for b in range(4):
                    nc.scalar.activation(flat(S_["a"] + b, 1), M[b // 2][:, (b % 2) * T:(b % 2 + 1) * T], ACT.Sigmoid, bias=vec("rwkv_a0_2", b)).then_inc(S("iclr"), 1)
                act.wait_ge(S("cc"), 1)
                nc.scalar.activation(flat(S_["er"], 4), flat(S_["cc"], 4), ACT.Exp, scale=log_decay).then_inc(S("decays"), 1)
                nc.scalar.activation(flat(S_["sw"], 4), flat(S_["cc"], 4), ACT.Exp, scale=-log_decay).then_inc(S("decays"), 1)
                nc.scalar.activation(flat(S_["cs"], 4), flat(S_["cs"], 4), ACT.Exp, scale=log_decay).then_inc(S("decays"), 1)
                nc.scalar.activation(small[:, 16:20], small[:, 16:20], ACT.Exp, scale=log_decay).then_inc(S("decays"), 1)

            def head_norms():
                act.wait_ge(S("kk"), 1)
                nc.scalar.activation(flat(S_["rn"], 4), flat(S_["kk"], 4), ACT.Square).then_inc(S("kk_sq"), 1)
                act.wait_ge(S("kk"), 2)
                nc.scalar.activation(flat(S_["rn"], 4), flat(S_["rn"], 4), ACT.Sqrt).then_inc(S("kk_root"), 1)

            def turn_v():
                for c in range(2):
                    act.wait_ge(S("v_turned"), c + 1)
                    nc.scalar.activation(vt[:, c, :], M[c][:, :], ACT.Copy).then_inc(S("vt"), 1)

            def turn_bk():
                for c in range(2):
                    act.wait_ge(S("bk_turned"), c + 1)
                    nc.scalar.activation((bt, kbt)[c], M[2 + c][:, :], ACT.Copy).then_inc(S("bkt"), 1)

            def rw_solve(c):
                act.wait_ge(S("rw_w0"), c + 1)
                link(nc.scalar.activation(w0_all[:, 0:T], M[0][:, 0:T], ACT.Copy))
                nc.scalar.activation(w0_all[:, T:2 * T], M[1][:, 0:T], ACT.Copy).then_inc(S("w0"), 1)
                act.wait_ge(S("rw_u0"), c + 1)
                nc.scalar.activation(u_all, M[2][:, :], ACT.Copy).then_inc(S("u0"), 1)
                act.wait_ge(S("rw_y"), c + 1)
                act.wait_ge(S("roped"), 6)
                nc.scalar.activation(y_f[:, :, c * P:(c + 1) * P], M[3][:, :].rearrange("p (b t) -> p b t", b=4), ACT.Copy).then_inc(S("yr"), 1)

            def gn_var():
                act.wait_ge(S("gn_c"), 1)
                nc.scalar.activation(flat(S_["gsum"], 4), flat(S_["y"], 4), ACT.Square).then_inc(S("gn_sq"), 1)
                act.wait_ge(S("gn_ss"), 1)
                for q in range(2):
                    nc.scalar.activation(flat(S_["grs2"] + 2 * q, 2), M[q + 2][:, :], ACT.Ln, bias=gn_eps_col, scale=1.0 / HD).then_inc(S("gn_ln"), 1)
                act.wait_ge(S("gn_ln"), 2)
                nc.scalar.activation(flat(S_["grs2"], 4), flat(S_["grs2"], 4), ACT.Exp, scale=-0.5).then_inc(S("gn_rs"), 1)

            def gn_mean():
                nc.scalar.activation(xx[0:96, 1, :], xx[0:96, 1, :], ACT.Sigmoid).then_inc(S("gate_x"), 1)

            def at_s(n):
                act.wait_ge(S("at_max"), n + 1)
                nc.scalar.activation(sc(n), sc(n), ACT.Exp, bias=small[:, 20 + n:21 + n], accum_out=small[:, 28 + n:29 + n]).then_inc(S("at_exp"), 1)

            def at_t(n):
                act.wait_ge(S("at_turned"), n + 1)
                if n % 2 == 0:
                    nc.scalar.activation(pt(n)[:, 0:384], M[2][:, 0:384], ACT.Copy).then_inc(S("at_pt"), 2)
                else:
                    nc.scalar.activation(pt(n)[:, 0:512], M[2][:, :], ACT.Copy).then_inc(S("at_pt"), 1)
                    nc.scalar.activation(pt(n)[:, 512:768], M[3][:, 0:T], ACT.Copy).then_inc(S("at_pt"), 1)

            def at_o(n):
                h, i = n // 2, n % 2
                half = slice(HD * (h % 2), HD * (h % 2 + 1))
                act.wait_ge(S("at_o"), n + 1)
                nc.scalar.activation(oa[half, h // 2, i * P:(i + 1) * P], M[1][half, T:T + P], ACT.Copy).then_inc(S("at_oa"), 1)

            def mixed():
                act.wait_ge(S("rw_out"), 1)
                nc.scalar.activation(y_hi[:, 0:4, :], ar(S_["y"], 4), ACT.Copy).then_inc(S("mixed_hi"), 1)
                act.wait_ge(S("at_oa"), 2 * AT_H)
                nc.scalar.activation(y_hi[:, 4:6, :], oa, ACT.Copy).then_inc(S("mixed_hi"), 1)

            def mix_post():
                squares(4, ar(S_["o"], 8), S_["osq"], lambda e, q: evacuated(e, ("wo", q)))

            def ffn_pre():
                squares(5, x, S_["sq"], lambda e, q: e.wait_ge(S("x_update"), 8 + 2 * q + 2))
                upper(3)

            def ffn_post():
                squares(6, ar(S_["f"], 8), S_["sq"], lambda e, q: evacuated(e, ("fo1", q)))

            def turn_p():
                act.wait_ge(S("p_turned"), 1)
                nc.scalar.activation(flat(S_["p"], 2), M[1][:, :], ACT.Copy).then_inc(S("p_t"), 1)
                act.wait_ge(S("p_t"), 1)
                projected(act, ("fo1", 3))
                nc.scalar.activation(y_hi[:, 0:2, :], ar(S_["p"], 2), ACT.Copy).then_inc(S("p_hi"), 1)

            def ple_x():
                for k in range(KD):
                    act.wait_ge(S("x_update"), 16 + k + 1)
                    nc.scalar.activation(h_hi[:, k, :], x[:, k, :], ACT.Copy).then_inc(S("operand_hi"), 1)

            def ple_post():
                squares(7, ar(S_["e"], 8), S_["sq"], lambda e, q: e.wait_ge(S("ple"), q + 1))

            steps = dict(mix_pre=mix_pre, lora_w=lora_w, lora_a=lora_a, head_norms=head_norms, turn_v=turn_v, turn_bk=turn_bk, rw_solve=rw_solve,
                         gn_mean=gn_mean, gn_var=gn_var, at_s=at_s, at_t=at_t, at_o=at_o, mixed=mixed, mix_post=mix_post, ffn_pre=ffn_pre, ffn_post=ffn_post,
                         turn_p=turn_p, ple_x=ple_x, ple_post=ple_post, load_x=load_x, params=params, norm=norm, final_norm=final_norm, sgu_v=sgu_v, windows=windows, gla_z=gla_z, gla_decay=gla_decay, gla_kt=gla_kt, gla_o=gla_o, gla_n=gla_n, sb_z=sb_z, sb_c=sb_c, sb_o=sb_o)

            def evac(key):
                j = jobs[key]
                i, b = j["i"], bank_of(key)
                kind = j["kind"]
                if kind in ("copy", "copy_t", "copy16"):
                    projected(act, key)
                    if kind == "copy":
                        if key[0] == "ea":
                            act.wait_ge(S("pad_zero"), 3)
                            to = a_pad[:, 2 * i:2 * i + 2, PAD:]
                        else:
                            to = ar(dest[key[0]] + 2 * i, 2)
                        fr = b[:, :].rearrange("p (c t) -> p c t", c=2)
                    elif kind == "copy_t":
                        to = flat(dest[key[0]], 6 if key[0] == "av" else 8).rearrange("p (n d) -> p n d", n=2)[:, :, i * CB:(i + 1) * CB]
                        fr = b[:, :].rearrange("p (c t) -> p c t", c=2)
                    else:
                        to, fr = flat(O_["glr"], 1)[0:16, :], b[0:16, 0:T]
                    done_reading(nc.scalar.activation(to, fr, ACT.Copy), key)
                two = b[:, :].rearrange("p (c t) -> p c t", c=2)
                if kind in ("shifted", "wx"):
                    projected(act, key)
                    act.wait_ge(S("zpad"), 4)
                    z = zpad(key[0])
                    if kind == "wx":
                        link(nc.scalar.activation(z[0:64, 0, 1:], b[0:64, 0:T], ACT.Copy))
                        done_reading(nc.scalar.activation(z[0:96, 1, 1:], b[0:96, T:2 * T], ACT.Copy), key)
                    else:
                        done_reading(nc.scalar.activation(z[:, 2 * i:2 * i + 2, 1:], two, ACT.Copy), key)
                if kind == "rope":
                    projected(act, key)
                    n = ropes.index(key)
                    if n >= 1:
                        act.wait_ge(S("roped"), n)
                    sw_ = flat(S_["swap"], 2)
                    for g in range(4):
                        to_ = slice(32 * g, 32 * g + 32)
                        fr_ = slice(32 * (g ^ 1), 32 * (g ^ 1) + 32)
                        nc.scalar.activation(sw_[to_, :], b[fr_, :], ACT.Copy).then_inc(S("swapped"), 1)
                if kind == "sigmoid":
                    projected(act, key)
                    if key == ("wga", 0):
                        act.wait_ge(S("yr"), 2)
                    c = S_["gate"] + (0 if key[0] == "wga" else 8) + 2 * i
                    done_reading(nc.scalar.activation(ar(c, 2), two, ACT.Sigmoid), key)
                if kind == "up" and key[0] == "au":
                    act.wait_ge(S("merged"), i + 1)
                    nc.scalar.activation(y_hi[:, 8 + 2 * i:10 + 2 * i, :], ar(S_["m"] + 2 * i, 2), ACT.Copy).then_inc(S("merged_hi"), 1)
                if kind in ("out", "ffn0", "ple"):
                    projected(act, key)
                    done_reading(nc.scalar.activation(ar(S_[{"out": "o", "ffn0": "f", "ple": "e"}[kind]] + 2 * i, 2), two, ACT.Copy), key)
                if kind == "ple_gate":
                    projected(act, key)
                    if i >= 2:
                        act.wait_ge(S("ple"), i - 1)
                    done_reading(nc.scalar.activation(ar(S_["sg"] + 2 * (i % 2), 2), two, ACT.Sigmoid), key)
                if kind in ("gate", "relu2"):
                    g = gates.index(key)
                    projected(act, key)
                    if g >= 2:
                        act.wait_ge(S("y_f"), g - 1)
                    done_reading(nc.scalar.activation(gate_tmp("sg", g), two, ACT.Silu if kind == "gate" else ACT.Relu), key)
                    act.wait_ge(S("y_f"), g + 1)
                    c = gate_mix[key[0]](i)[1] if kind == "gate" else 2 * (i % 8)
                    if key == ("fi", 8):
                        projected(act, ("fo0", 3))
                    nc.scalar.activation(y_hi[:, c:c + 2, :], gate_tmp("yt", g), ACT.Copy).then_inc(S("y_hi"), 1)

            act.wait_ge(S("scalars_set"), 3)
            run(steps, evac, split_to)
            act.wait_ge(S("out_ready"), 4)
            act.dma_start(out_t, ar(0, 8).rearrange("p (n c) t -> p n (c t)", n=2)).then_inc(S("stored"), 16)
            act.wait_ge(S("stored"), 16)

        @block.vector
        def _(dve):
            V = nc.vector
            link = chainer(dve, "dve_chain")
            next_split = [0]

            def modulation_part(u):
                n = units[u]["ada"][2]
                unit_loaded(dve, u)
                if n == 0:
                    dve.wait_ge(S("silu_c"), 1)
                    dve.wait_ge(S("gate_w_in"), 16)
                if n >= 2:
                    dve.wait_ge(S("ada_used"), n - 1)
                w, acc = raw[:, u % RAW, :].rearrange("p (k n) -> p k n", k=KD), ada_acc[n % 2]
                link(V.tensor_scalar(acc, w[:, 0, :], silu_c[:, 0:1], None, ALU.mult))
                for k in range(1, KD):
                    i_ = V.scalar_tensor_tensor(out=acc, in0=w[:, k, :], scalar=silu_c[:, k:k + 1], in1=acc, op0=ALU.mult, op1=ALU.add)
                    if k < KD - 1:
                        link(i_)
                i_.then_inc(S("ada_acc"), 1)

            def ada_to(u_end):
                while next_split[0] < u_end:
                    split_next()

            def split_to(end):
                u_end = split_units[min(end, len(split_units)) - 1]["order"] + 1
                while next_split[0] < u_end:
                    split_next()

            def split_next():
                    u = next_split[0]
                    next_split[0] += 1
                    if units[u]["ada"] is not None:
                        modulation_part(u)
                        return
                    i, n = units[u]["index"], units[u]["nk"] * units[u]["n"]
                    dve.wait_ge(S("split_hi"), i + 1)
                    V.tensor_tensor(w_lo[:, i % SPL, 0:n], raw[:, u % RAW, 0:n], w_hi[:, i % SPL, 0:n].bitcast(F32), ALU.subtract).then_inc(S("split"), 1)

            def lower(n, k):
                dve.wait_ge(S("operand_hi"), 8 * n + k + 1)
                V.tensor_tensor(h_lo[:, k, :], normed_at(n)[:, k, :], h_hi[:, k, :].bitcast(F32), ALU.subtract).then_inc(S("operand_ready"), 1)

            def inverse_root(stat):
                dve.wait_ge(S("rstd"), stat + 1)
                link(V.reciprocal(rstd[:, :], rstd[:, :]))

            scaled = [0]

            def apply_norm(stat, n, src, dst, gain, shift=None):
                inverse_root(stat)
                for k in range(KD + 3):
                    if k < KD:
                        V.scalar_tensor_tensor(out=dst[:, k, :], in0=src[:, k, :], scalar=gain(k), in1=rstd[:, :], op0=ALU.mult,
                                               op1=ALU.mult).then_inc(S("normed" if shift is None else "scaled"), 1)
                        scaled[0] += shift is not None
                    if shift is not None and 1 <= k <= KD:
                        dve.wait_ge(S("scaled"), scaled[0] - (k < KD))
                        V.tensor_scalar(dst[:, k - 1, :], dst[:, k - 1, :], shift(k - 1), None, ALU.add).then_inc(S("normed"), 1)
                    if k >= 3:
                        lower(n, k - 3)

            def modulation(layer):
                return V.scalar_tensor_tensor(out=mod[:, layer, :], in0=ada_c[:, layer, 8:16], scalar=1.0,
                                              in1=vec("norm_g", 8 * layer, 8), op0=ALU.add, op1=ALU.mult)

            def ada_first():
                dve.wait_ge(S("params"), 1)
                dve.wait_ge(S("ada_used"), 8)
                V.tensor_tensor(ada_c[:, 0, 0:16], M[3][:, 0:16], vec("ada_b", 0, 16), ALU.add).then_inc(S("ada_read"), 1)
                dve.wait_ge(S("ada_read"), 1)
                link(modulation(0))

            def ada_rest():
                dve.wait_ge(S("ada_used"), 20)
                V.tensor_tensor(ada_c[:, :, :].rearrange("p l c -> p (l c)")[:, 16:40], M[3][:, 16:40], vec("ada_b", 16, 24), ALU.add).then_inc(S("ada_read"), 1)
                dve.wait_ge(S("ada_read"), 2)
                link(modulation(1))

            def ada_last():
                dve.wait_ge(S("ada_used"), 24)
                V.tensor_tensor(ada_c[:, 1, 16:24], M[3][:, 40:48], vec("ada_b", 40, 8), ALU.add).then_inc(S("ada_read"), 1)
                dve.wait_ge(S("ada_read"), 3)

            def norm(n):
                apply_norm(n, n, x[:, :, :], normed_at(n), lambda k: mod[:, n, k:k + 1], lambda k: ada_c[:, n, k:k + 1])

            def final_norm():
                inverse_root(2)
                for k in range(KD):
                    V.scalar_tensor_tensor(out=x[:, k, :], in0=x[:, k, :], scalar=vec("final_g", k), in1=rstd[:, :], op0=ALU.mult, op1=ALU.mult).then_inc(S("x_update"), 1)
                dve.wait_ge(S("x_update"), 8)

            def sgu_w():
                dve.wait_ge(S("const_in"), 16)
                for b in range(2):
                    dve.wait_ge(S("sgu_w_turned"), b + 1)
                    V.tensor_tensor(w_t[:, 4 * b:4 * b + 4, :], M[1 + b][:, :].rearrange("p (h t) -> p h t", h=4), bc(K("upto"), 4), ALU.mult).then_inc(S("sgu_w"), 1)

            def sgu_v():
                dve.wait_ge(S("v_rstd"), 1)
                for tt in range(2):
                    V.tensor_scalar(v_tok[:, tt, :], v_tok[:, tt, :], small[:, 4 + tt:5 + tt], None, ALU.mult).then_inc(S("v_normed"), 1)

            def windows(part):
                if part == 0:
                    dve.wait_ge(S("pad_zero"), 3)
                    for i in range(4):
                        evacuated(dve, ("ea", i))
                for g, wd in ((0, 2),) if part == 0 else tuple(enumerate(WINDOWS))[1:] if part == 1 else ():
                    src, to = (lev[1 - g % 2] if g else a_pad), lev[g % 2]
                    sh = wd // 2
                    if g == 0:
                        link(V.tensor_tensor(to[:, 0:8, sh:], src[:, 0:8, sh:], src[:, 0:8, 0:-sh], ALU.add))
                    else:
                        link(V.tensor_tensor(to[:, 2 * g:8, PAD:], src[:, 2 * g:8, PAD:], src[:, 2 * g:8, PAD - sh:-sh], ALU.add))
                if part == 2:
                    dve.wait_ge(S("inv_in"), 16)
                inv = K("inv_count").rearrange("p (g t) -> p g t", g=4)
                for g in range(4 if part == 2 else 0):
                    link(V.tensor_tensor(lev[0][:, 2 * g:2 * g + 2, PAD:], lev[g % 2][:, 2 * g:2 * g + 2, PAD:], bc(inv[:, g, :], 2), ALU.mult))
                if part < 3:
                    return
                V.tensor_tensor(lev[0][:, :, PAD:], lev[0][:, :, PAD:], a_pad[:, :, PAD:], ALU.subtract).then_inc(S("p"), 1)
                dve.wait_ge(S("p_hi"), 1)
                V.tensor_tensor(y_lo[:, 0:8, :], lev[0][:, :, PAD:], y_hi[:, 0:8, :].bitcast(F32), ALU.subtract).then_inc(S("p_lo"), 1)

            def sgu_z(i):
                evacuated(dve, ("eu", i))
                dve.wait_ge(S("sgu_in"), 32)
                dve.wait_ge(S("sgu_z"), i + 1)
                for h in (2 * i, 2 * i + 1):
                    z = M[i % 3][:, (h % 2) * T:(h % 2 + 1) * T].rearrange("p (n t) -> p n t", n=2)
                    t = flat(E_["z"], 1)
                    link(V.scalar_tensor_tensor(out=t.rearrange("p (n t) -> p n t", n=2), in0=z, scalar=vec("sgu_norm_g", h),
                                                in1=bc(b_all[:, h, :], 2), op0=ALU.mult, op1=ALU.add))
                    u = flat(E_["u"] + h, 1)
                    V.tensor_tensor(u, u, t, ALU.mult).then_inc(S("sgu_y"), 1)
                    dve.wait_ge(S("sgu_y"), h + 1)

            def gla_z():
                dve.wait_ge(S("gla_l1p"), 1)
                dve.wait_ge(S("odd_const_in"), 16)
                link(V.scalar_tensor_tensor(out=flat(O_["t1"], 4), in0=flat(O_["la"], 4), scalar=0.0, in1=flat(O_["t1"], 4), op0=ALU.min, op1=ALU.subtract))
                for h in range(GLA_H):
                    V.tensor_tensor_scan(flat(O_["la"] + h, 1), K("gla_run"), flat(O_["t1"] + h, 1), 0.0, ALU.mult, ALU.add).then_inc(S("gla_cum_h"), 1)
                dve.wait_ge(S("gla_cum_h"), 4)
                V.tensor_copy(small[:, 10:11], small_zero).then_inc(S("gla_cum"), 1)
                V.tensor_copy(small[:, 11:12], small_zero).then_inc(S("gla_t1_free"), 1)

            def gla_decay():
                for i in range(2):
                    evacuated(dve, ("gq", i))
                    evacuated(dve, ("gk", i))
                dve.wait_ge(S("gla_exp"), 1)
                link(V.scalar_tensor_tensor(out=flat(O_["q"], 4), in0=flat(O_["q"], 4), scalar=float(P) ** -0.5, in1=flat(O_["e"], 4), op0=ALU.mult, op1=ALU.mult))
                dve.wait_ge(S("gla_exp"), 2)
                link(V.tensor_tensor(flat(O_["ki"], 4), flat(O_["k"], 4), flat(O_["t1"], 4), ALU.mult))
                la = flat(O_["la"], 4).rearrange("p (c t) -> p c t", t=GLA_C)
                V.tensor_tensor(flat(O_["t1"], 4).rearrange("p (c t) -> p c t", t=GLA_C), la[:, :, GLA_C - 1:GLA_C].broadcast_to([P, 16, GLA_C]), la, ALU.subtract).then_inc(S("gla_rest"), 1)
                dve.wait_ge(S("gla_exp"), 3)
                V.tensor_tensor(flat(O_["k"], 4), flat(O_["k"], 4), flat(O_["t1"], 4), ALU.mult).then_inc(S("gla_kend"), 1)
                dve.wait_ge(S("gla_kend"), 1)
                link(V.memset(flat(O_["att"], 2), 0.0))

            def gla_att(h):
                dve.wait_ge(S("gla_att"), h + 1)
                if h >= 2:
                    dve.wait_ge(S("gla_o_done"), h - 1)
                link(V.copy_predicated(gatt(h), K("gla_mask").bitcast(U32), M[0][:, 0:T]))
                e = flat(O_["e"], 4).rearrange("p (h t) -> p h t", h=GLA_H)
                us = [M[1][:, 0:T], M[0][:, T:2 * T], M[1][:, T:2 * T]]
                link(V.tensor_copy(gst(h, 0), us[0]))
                for c in (1, 2):
                    ins_ = V.scalar_tensor_tensor(out=gst(h, c), in0=gst(h, c - 1), scalar=e[:, h, GLA_C * (c + 1) - 1:GLA_C * (c + 1)], in1=us[c], op0=ALU.mult, op1=ALU.add)
                    if c == 1:
                        link(ins_)
                ins_.then_inc(S("gla_states"), 1)

            def gla_n(h):
                dve.wait_ge(S("gla_rs"), h + 1)
                dve.wait_ge(S("gla_o"), h + 1)
                for vh in range(2):
                    o = GO(h)[:, vh, :]
                    ins_ = V.scalar_tensor_tensor(out=o, in0=o, scalar=vec("gla_norm_g", 2 * h + vh), in1=flat(O_["rs"], 1), op0=ALU.mult, op1=ALU.mult)
                    if vh == 0:
                        link(ins_)
                ins_.then_inc(S("gla_yc"), 1)

            def sb_z(h):
                dve.wait_ge(S("sb_l1p"), h + 1)
                dve.wait_ge(S("sb_zs"), h + 1)
                if h >= 1:
                    dve.wait_ge(S("sb_c_done"), h)
                link(V.scalar_tensor_tensor(out=sbw(2), in0=sbw(0), scalar=0.0, in1=sbw(1), op0=ALU.max, op1=ALU.add))
                V.tensor_tensor(sbw(2), sbw(2), K("sb_mask"), ALU.mult).then_inc(S("sb_l"), 1)
                if h >= 1:
                    dve.wait_ge(S("sb_w"), h)
                link(V.tensor_tensor(sbw(3), sbw(0), K("sb_neg"), ALU.add))

            def add_normed(stat, src, gain):
                inverse_root(stat)
                for k in range(KD + 1):
                    if k < KD:
                        V.scalar_tensor_tensor(out=src[:, k, :], in0=src[:, k, :], scalar=vec(gain, k), in1=rstd[:, :], op0=ALU.mult, op1=ALU.mult).then_inc(S("scaled"), 1)
                        scaled[0] += 1
                    if k >= 1:
                        dve.wait_ge(S("scaled"), scaled[0] - (k < KD))
                        V.tensor_tensor(x[:, k - 1, :], x[:, k - 1, :], src[:, k - 1, :], ALU.add).then_inc(S("x_update"), 1)

            def mix_pre():
                apply_norm(3, 2, x[:, :, :], normed_at(2), lambda k: vec("mix_pre_norm_2", k))

            def token_shift(names):
                for name in names:
                    _, to, n, mu = shifted[name]
                    for i in range(2 if n == 4 else 1):
                        evacuated(dve, (name, i))
                    z = zpad(name)
                    to = flat(to, n).rearrange("p (b t) -> p b t", b=n)
                    if name == "wx":
                        for b, rows_ in ((0, 64), (1, 96)):
                            link(V.tensor_tensor(to[0:rows_, b, :], z[0:rows_, b, 0:T], z[0:rows_, b, 1:], ALU.subtract))
                            link(V.scalar_tensor_tensor(out=to[0:rows_, b, :], in0=to[0:rows_, b, :], scalar=vec("rwkv_mu_2", mu + b)[0:rows_], in1=z[0:rows_, b, 1:], op0=ALU.mult, op1=ALU.add))
                        continue
                    link(V.tensor_tensor(to, z[:, :, 0:T], z[:, :, 1:], ALU.subtract))
                    for b in range(4):
                        link(V.scalar_tensor_tensor(out=to[:, b, :], in0=to[:, b, :], scalar=vec("rwkv_mu_2", mu + b), in1=z[:, b, 1:], op0=ALU.mult, op1=ALU.add))
                V.tensor_copy(small[:, 9:10], small_zero).then_inc(S("shift"), 1)
                dve.wait_ge(S("shift"), {"wx": 1, "wv": 2, "wr": 3}[names[0]])

            def shift_k():
                token_shift(("wx", "wk"))

            def shift_r():
                token_shift(("wr",))

            def shift_v():
                token_shift(("wv",))

            def lora_a():
                dve.wait_ge(S("late_in"), 64)
                dve.wait_ge(S("sw"), 4)
                for b in range(4):
                    link(V.tensor_tensor_scan(flat(S_["cs"] + b, 1), K("rw_run"), flat(S_["sw"] + b, 1), 0.0, ALU.mult, ALU.add))
                cs = flat(S_["cs"], 4).rearrange("p (b t) -> p b t", t=RW_C)
                mid = cs[:, :, RW_C // 2 - 1:RW_C // 2]
                link(V.tensor_copy(small[:, 16:20].unsqueeze(2), mid[:, 1:8:2, :]))
                link(V.tensor_tensor(flat(S_["cc"], 4).rearrange("p (b t) -> p b t", t=RW_C), cs, mid.broadcast_to([P, 8, RW_C]), ALU.subtract))
                V.tensor_tensor(flat(S_["cs"], 4), flat(S_["cc"], 4), flat(S_["sw"], 4), ALU.subtract).then_inc(S("cc"), 1)

            def head_norms():
                k4, kk4, rn4 = flat(S_["k"], 4), flat(S_["kk"], 4), flat(S_["rn"], 4)
                for b in range(4):
                    i_ = V.tensor_scalar(kk4[:, b * T:(b + 1) * T], k4[:, b * T:(b + 1) * T], vec("rwkv_k_k_2", b), None, ALU.mult)
                    if b < 3:
                        link(i_)
                i_.then_inc(S("kk"), 1)
                dve.wait_ge(S("kk"), 1)
                dve.wait_ge(S("kk_ss"), 1)
                for q in range(2):
                    i_ = V.tensor_scalar(rn4[:, 512 * q:512 * (q + 1)], M[2 + q][:, :], 1e-24, None, ALU.max)
                    if q == 0:
                        link(i_)
                i_.then_inc(S("kk"), 1)
                dve.wait_ge(S("kk_root"), 1)
                link(V.reciprocal(rn4, rn4))
                link(V.tensor_tensor(kk4, kk4, rn4, ALU.mult))
                dve.wait_ge(S("iclr"), 4)
                kt4, a4 = flat(S_["kt"], 4), flat(S_["a"], 4)
                for b in range(4):
                    link(V.tensor_scalar(kt4[:, b * T:(b + 1) * T], a4[:, b * T:(b + 1) * T], -1.0, vec("rwkv_k_a_2", b), ALU.add, ALU.mult))
                link(V.scalar_tensor_tensor(out=k4, in0=kt4, scalar=1.0, in1=k4, op0=ALU.add, op1=ALU.mult))
                for b in range(4):
                    i_ = V.scalar_tensor_tensor(out=flat(S_["rk"] + b, 1), in0=r_f[:, b, :], scalar=vec("rwkv_r_k_2", b), in1=k_f[:, b, :], op0=ALU.mult, op1=ALU.mult)
                    if b < 3:
                        link(i_)
                i_.then_inc(S("rk"), 1)
                dve.wait_ge(S("decays"), 4)
                ea = flat(S_["cs"], 4).rearrange("p (b c t) -> p b c t", b=4, c=2)
                er = flat(S_["er"], 4).rearrange("p (b c t) -> p b c t", b=4, c=2)
                ei = flat(S_["sw"], 4)
                for c in range(2):
                    link(V.scalar_tensor_tensor(out=ar_[:, :, c, 0, :], in0=kk4.rearrange("p (b c t) -> p b c t", b=4, c=2)[:, :, c, :], scalar=-1.0,
                                                in1=ea[:, :, c, :], op0=ALU.mult, op1=ALU.mult))
                    link(V.tensor_tensor(ar_[:, :, c, 1, :], r_f[:, :, c * P:(c + 1) * P], er[:, :, c, :], ALU.mult))
                link(V.tensor_tensor(flat(S_["b"], 4), kk4, a4, ALU.mult))
                link(V.tensor_tensor(flat(S_["b"], 4), flat(S_["b"], 4), ei, ALU.mult))
                link(V.tensor_tensor(flat(S_["kb"], 4), k4, ei, ALU.mult))
                V.tensor_copy(small[:, 12:16].unsqueeze(2), er[:, :, 0, P - 1:P]).then_inc(S("rw_operands"), 1)
                dve.wait_ge(S("rw_operands"), 1)

            def bonus():
                for q in range(2):
                    dve.wait_ge(S("bonus_sum"), q + 1)
                    i_ = V.tensor_tensor(flat(S_["bonus"] + 2 * q, 2), M[q][:, :], flat(S_["v"] + 2 * q, 2), ALU.mult)
                    if q == 0:
                        link(i_)
                i_.then_inc(S("bonus"), 1)
                dve.wait_ge(S("bonus"), 1)

            def rw_pairs(c):
                mask = cst[:, CONST_PLACES[0][0]["before"][0]:CONST_PLACES[0][0]["before"][0] + 2 * P]
                if c == 0:
                    dve.wait_ge(S("vt"), 2)
                for s_ in range(2):
                    n = 2 * c + s_
                    nm_b, nm_k, t_, tt_, _ = rset(s_)
                    dve.wait_ge(S("rw_pairs"), 2 * n + 1)
                    for k in range(4):
                        i_ = V.tensor_tensor((nm_b, nm_k)[k // 2][:, 2 * (k % 2):2 * (k % 2) + 2, :], M[k][:, :].rearrange("p (j w) -> p j w", j=2), bc(mask, 2), ALU.mult)
                        i_.then_inc(S("rw_masked"), 1)
                    dve.wait_ge(S("rw_pairs"), 2 * n + 2)
                    for k in range(2):
                        link(V.tensor_tensor(t_[:, 2 * k:2 * k + 2, :], M[k][:, 0:T].rearrange("p (j w) -> p j w", j=2), bc(K("pair1"), 2), ALU.mult))
                    dve.wait_ge(S("rw_masked"), 4 * n + 4)
                    link(V.tensor_tensor(tt_, nm_b[:, :, 0:P], bc(K("pair1_t"), 4), ALU.mult))
                    link(V.tensor_tensor(t_, t_, bc(K("ident"), 4), ALU.add))
                    V.tensor_tensor(tt_, tt_, bc(K("ident"), 4), ALU.add).then_inc(S("rw_t0"), 1)
                    dve.wait_ge(S("rw_t0"), n + 1)

            def rw_u(m):
                for s_ in range(2):
                    dve.wait_ge(S("rw_u"), 2 * m + s_ + 1)
                    um = rset(s_)[4]
                    V.tensor_tensor(um, M[s_][:, :].rearrange("p (q w) -> p q w", q=4), bc(K(f"pair{2 ** (m % 6 + 1)}"), 4), ALU.mult).then_inc(S("rw_um"), 1)

            def rw_t(m):
                for s_ in range(2):
                    dve.wait_ge(S("rw_t"), 2 * m + s_ + 1)
                    _, _, t_, tt_, _ = rset(s_)
                    if m % 6 < 5:
                        link(V.tensor_tensor(t_, t_, M[s_][:, :].rearrange("p (q w) -> p q w", q=4), ALU.add))
                    V.tensor_tensor(tt_, tt_, M[2 + s_][:, :].rearrange("p (q w) -> p q w", q=4), ALU.add).then_inc(S("rw_new"), 1)
                    dve.wait_ge(S("rw_new"), 2 * m + s_ + 1)

            def rw_solve(c):
                if c == 0:
                    dve.wait_ge(S("rw_s"), 1)
                    for b in range(4):
                        i_ = V.tensor_scalar(s0[:, b, :], M[0][:, b * HD:(b + 1) * HD], small[:, 12 + b:13 + b], small[:, 16 + b:17 + b], ALU.mult, ALU.mult)
                        i_.then_inc(S("s0"), 1)

            def gn_mean():
                for q in range(2):
                    dve.wait_ge(S("gn_sum"), q + 1)
                    y2 = flat(S_["y"] + 2 * q, 2)
                    i_ = V.scalar_tensor_tensor(out=y2, in0=M[q][:, :], scalar=-1.0 / HD, in1=y2, op0=ALU.mult, op1=ALU.add)
                    if q == 0:
                        link(i_)
                i_.then_inc(S("gn_c"), 1)
                dve.wait_ge(S("gn_c"), 1)

            def gn_var():
                dve.wait_ge(S("gn_rs"), 1)
                link(V.tensor_tensor(flat(S_["y"], 4), flat(S_["y"], 4), flat(S_["grs2"], 4), ALU.mult))
                for b in range(4):
                    link(V.tensor_scalar(y_f[:, b, :], y_f[:, b, :], vec("rwkv_ln_w_2", b), vec("rwkv_ln_b_2", b), ALU.mult, ALU.add))
                link(V.tensor_tensor(flat(S_["y"], 4), flat(S_["y"], 4), flat(S_["bonus"], 4), ALU.add))

            def rw_gate():
                for q in range(2):
                    dve.wait_ge(S("rw_g"), q + 1)
                    y2 = flat(S_["y"] + 2 * q, 2)
                    i_ = V.tensor_tensor(y2, y2, M[2 + q][:, :], ALU.mult)
                    if q == 0:
                        link(i_)
                i_.then_inc(S("rw_out"), 1)
                dve.wait_ge(S("rw_out"), 1)

            def at_s(n):
                i = n % 2
                if n >= 2:
                    dve.wait_ge(S("at_turned"), n - 1)
                dve.wait_ge(S("at_s"), n + 1)
                neg = K(f"at_neg{i}")
                parts = ((0, 384, 0),) if i == 0 else ((0, 512, 0), (512, 768, 1))
                for a_, b_, bank in parts:
                    link(V.scalar_tensor_tensor(out=sc(n)[:, a_:b_], in0=M[bank][:, 0:b_ - a_], scalar=float(HD) ** -0.5, in1=neg[:, a_:b_], op0=ALU.mult, op1=ALU.add))
                V.tensor_reduce(small[:, 20 + n:21 + n], sc(n), AX.X, ALU.max, negate=True).then_inc(S("at_max"), 1)
                dve.wait_ge(S("at_exp"), n + 1)
                link(V.reciprocal(small[:, 28 + n:29 + n], small[:, 28 + n:29 + n]))
                V.tensor_scalar(sc(n), sc(n), small[:, 28 + n:29 + n], None, ALU.mult).then_inc(S("at_p"), 1)

            def mixed():
                dve.wait_ge(S("mixed_hi"), 1)
                V.tensor_tensor(y_lo[:, 0:4, :], ar(S_["y"], 4), y_hi[:, 0:4, :].bitcast(F32), ALU.subtract).then_inc(S("mixed_lo"), 1)
                dve.wait_ge(S("mixed_hi"), 2)
                V.tensor_tensor(y_lo[:, 4:6, :], oa, y_hi[:, 4:6, :].bitcast(F32), ALU.subtract).then_inc(S("mixed_lo"), 1)

            def mix_post():
                add_normed(4, ar(S_["o"], 8), "mix_post_norm_2")

            def ffn_pre():
                for k in range(KD):
                    dve.wait_ge(S("x_update"), 8 + k + 1)
                apply_norm(5, 3, x[:, :, :], normed_at(3), lambda k: vec("ffn_pre_norm_2", k))

            def ffn_post():
                add_normed(6, ar(S_["f"], 8), "ffn_post_norm_2")

            def turn_p():
                dve.wait_ge(S("p_hi"), 2)
                V.tensor_tensor(y_lo[:, 0:2, :], ar(S_["p"], 2), y_hi[:, 0:2, :].bitcast(F32), ALU.subtract).then_inc(S("p_lo"), 1)

            def ple_x():
                for k in range(KD):
                    dve.wait_ge(S("operand_hi"), 32 + k + 1)
                    V.tensor_tensor(h_lo[:, k, :], x[:, k, :], h_hi[:, k, :].bitcast(F32), ALU.subtract).then_inc(S("operand_ready"), 1)

            def ple_post():
                add_normed(7, ar(S_["e"], 8), "ple_post_norm_2")

            def sb_c(h):
                dve.wait_ge(S("sb_c_done"), h + 1)
                V.scalar_tensor_tensor(out=sbw(3), in0=M[1][:, 0:384], scalar=-1.0, in1=sbw(3), op0=ALU.mult, op1=ALU.add).then_inc(S("sb_arg"), 1)

            steps = dict(mix_pre=mix_pre, shift_k=shift_k, shift_r=shift_r, shift_v=shift_v, lora_a=lora_a, head_norms=head_norms, bonus=bonus,
                         rw_pairs=rw_pairs, rw_u=rw_u, rw_t=rw_t, rw_solve=rw_solve, gn_mean=gn_mean, gn_var=gn_var, rw_gate=rw_gate,
                         at_s=at_s, mixed=mixed, mix_post=mix_post, ffn_pre=ffn_pre, ffn_post=ffn_post, turn_p=turn_p, ple_x=ple_x,
                         ple_post=ple_post, ada_first=ada_first, ada_rest=ada_rest, ada_last=ada_last, norm=norm, final_norm=final_norm, sgu_w=sgu_w, sgu_v=sgu_v, windows=windows, sgu_z=sgu_z, gla_z=gla_z, gla_decay=gla_decay, gla_att=gla_att, gla_n=gla_n, sb_z=sb_z, sb_c=sb_c)

            def evac(key):
                j = jobs[key]
                i, b = j["i"], bank_of(key)
                kind = j["kind"]
                if kind == "rope":
                    n = ropes.index(key)
                    dve.wait_ge(S("swapped"), 4 * n + 4)
                    to = ar(S_["q" if key[0] == "aq" else "ak"] + 2 * i, 2)
                    sw_ = ar(S_["swap"], 2)
                    done_reading(V.tensor_tensor(to, b[:, :].rearrange("p (c t) -> p c t", c=2), bc(K("cos"), 2), ALU.mult), key)
                    link(V.tensor_tensor(sw_, sw_, bc(K("sin"), 2), ALU.mult))
                    evacuated(dve, key)
                    V.tensor_tensor(to, to, sw_, ALU.add).then_inc(S("roped"), 1)
                if kind == "up":
                    projected(dve, key)
                    two = b[:, :].rearrange("p (c t) -> p c t", c=2)
                    ga, gr = ar(S_["gate"] + 2 * i, 2), ar(S_["gate"] + 8 + 2 * i, 2)
                    mm = ar(S_["m"] + 2 * i, 2)
                    if key[0] == "ru":
                        evacuated(dve, ("wgb", i))
                        done_reading(V.tensor_tensor(mm, two, gr, ALU.mult), key)
                    else:
                        done_reading(V.tensor_tensor(ga, two, ga, ALU.mult), key)
                        evacuated(dve, key)
                        evacuated(dve, ("ru", i))
                        V.tensor_tensor(mm, mm, ga, ALU.add).then_inc(S("merged"), 1)
                        dve.wait_ge(S("merged_hi"), i + 1)
                        V.tensor_tensor(y_lo[:, 8 + 2 * i:10 + 2 * i, :], mm, y_hi[:, 8 + 2 * i:10 + 2 * i, :].bitcast(F32), ALU.subtract).then_inc(S("merged_lo"), 1)
                if kind == "ffn1":
                    projected(dve, key)
                    f_ = ar(S_["f"] + 2 * i, 2)
                    evacuated(dve, ("fo0", i))
                    done_reading(V.tensor_tensor(f_, b[:, :].rearrange("p (c t) -> p c t", c=2), f_, ALU.add), key)
                if kind == "ple_gate":
                    evacuated(dve, key)
                    e_ = ar(S_["e"] + 2 * i, 2)
                    V.tensor_tensor(e_, e_, ar(S_["sg"] + 2 * (i % 2), 2), ALU.mult).then_inc(S("ple"), 1)
                if kind == "relu2":
                    g = gates.index(key)
                    evacuated(dve, key)
                    c = 2 * (i % 8)
                    if g >= 2:
                        dve.wait_ge(S("y_lo"), g - 1)
                    V.tensor_tensor(gate_tmp("yt", g), gate_tmp("sg", g), gate_tmp("sg", g), ALU.mult).then_inc(S("y_f"), 1)
                    dve.wait_ge(S("y_hi"), g + 1)
                    V.tensor_tensor(y_lo[:, c:c + 2, :], gate_tmp("yt", g), y_hi[:, c:c + 2, :].bitcast(F32), ALU.subtract).then_inc(S("y_lo"), 1)
                if kind == "gate":
                    g = gates.index(key)
                    evacuated(dve, key)
                    mix, c = gate_mix[key[0]](i)
                    if key[0] == "ega":
                        evacuated(dve, ("pool", i))
                    if key[0] == "gga":
                        dve.wait_ge(S("gla_yc"), i + 1)
                    if key[0] == "ggb":
                        dve.wait_ge(S("sb_y"), 2 * i + 2)
                    if g >= 2:
                        dve.wait_ge(S("y_lo"), g - 1)
                    V.tensor_tensor(gate_tmp("yt", g), gate_tmp("sg", g), mix, ALU.mult).then_inc(S("y_f"), 1)
                    dve.wait_ge(S("y_hi"), g + 1)
                    V.tensor_tensor(y_lo[:, c:c + 2, :], gate_tmp("yt", g), y_hi[:, c:c + 2, :].bitcast(F32), ALU.subtract).then_inc(S("y_lo"), 1)
                if kind == "pool":
                    projected(dve, key)
                    for fb in range(2):
                        ins_ = V.tensor_scalar(a_pad[:, 2 * i + fb, PAD:], b[:, fb * T:(fb + 1) * T], vec("pool_scale", 2 * i + fb), None, ALU.mult)
                        if fb == 0:
                            link(ins_)
                    done_reading(ins_, key)
                if kind == "residual":
                    projected(dve, key)
                    layer = 0 if key[0] == "eo" else 1
                    for fb in range(2):
                        xc = x[:, 2 * i + fb, :]
                        ins_ = V.scalar_tensor_tensor(out=xc, in0=b[:, fb * T:(fb + 1) * T], scalar=ada_c[:, layer, 16 + 2 * i + fb:17 + 2 * i + fb],
                                                      in1=xc, op0=ALU.mult, op1=ALU.add)
                        if fb == 0:
                            link(ins_)
                    done_reading(ins_, key)

            dve.wait_ge(S("scalars_set"), 3)
            run(steps, evac, split_to, lambda u: ada_to(u + 1))
            for q in range(4):
                dve.wait_ge(S("out_turned"), q + 1)
                V.tensor_copy(ar(2 * q, 2), M[q][:, :].rearrange("p (c t) -> p c t", c=2)).then_inc(S("out_ready"), 1)

        @block.tensor
        def _(pe):
            def turn(to, src):
                n = src.shape[0]
                return nc.tensor.transpose(to, src, K("ident")[0:n, 0:n])

            def sum_squares(n, sq):
                for k in range(KD):
                    if k % 2 == 0:
                        pe.wait_ge(S("squares"), 4 * n + k // 2 + 1)
                    m = nc.tensor.matmul(M[0][:, 0:T], K("ones"), ar(sq + k)[:, 0, :], start=(k == 0), stop=(k == KD - 1))
                m.then_inc(S("sum_sq"), 1)

            def load_x():
                pe.wait_ge(S("const_in"), 16)
                pe.wait_ge(S("c_in"), 16)
                turn(PJ[0][:, 0:KD], c_rows).then_inc(S("c_turned"), 1)
                pe.wait_ge(S("x_in"), 16)
                xt = ar(0, 8).rearrange("p (n c) t -> p n (c t)", n=2)
                for q in range(4):
                    for c in range(2):
                        for tt in range(2):
                            m = turn(M[q][:, c * T + tt * P:c * T + (tt + 1) * P], xt[:, tt, (2 * q + c) * P:(2 * q + c + 1) * P])
                    m.then_inc(S("x_turned"), 1)

            def params():
                pe.wait_ge(S("rows_loaded"), 16 * N_ROW_LOADS)
                turn(PJ[1][:, 0:P], rows[:, 0, :])
                turn(PJ[1][:, P:2 * P], rows[:, 1, :]).then_inc(S("params_turned"), 1)

            def norm(n):
                sum_squares(n, (E_["sq"], O_["sq"])[n])

            def final_norm():
                sum_squares(2, O_["sq"])

            def sgu_w():
                pe.wait_ge(S("sgu_in"), 32)
                for b in range(2):
                    for h in range(4):
                        m = turn(M[1 + b][:, h * P:(h + 1) * P], w_raw[:, 4 * b + h, :])
                    m.then_inc(S("sgu_w_turned"), 1)

            def sgu_z(i):
                pe.wait_ge(S("v_normed"), 2)
                pe.wait_ge(S("sgu_w"), 2)
                if i == 3:
                    pe.wait_ge(S("sgu_y"), 2)
                for h in (2 * i, 2 * i + 1):
                    for n in range(2):
                        m = nc.tensor.matmul(M[i % 3][:, (h % 2) * T + n * P:(h % 2) * T + (n + 1) * P], v_tok[:, n, h * P:(h + 1) * P], w_t[:, h, :], start=True, stop=True)
                m.then_inc(S("sgu_z"), 1)

            def gla_z():
                pe.wait_ge(S("gate_w_in"), 16)
                evacuated(pe, ("glr", 0))
                for h in range(GLA_H):
                    m = nc.tensor.matmul(M[h // 2][:, (h % 2) * T:(h % 2 + 1) * T], gate_w[:, h * P:(h + 1) * P], flat(O_["glr"], 1)[0:16, :], start=True, stop=True)
                    if h % 2:
                        m.then_inc(S("gla_z"), 1)

            def gla_kt():
                pe.wait_ge(S("gla_kend"), 1)
                for b in range(2):
                    for i in range(4):
                        h, n = 2 * b + i // 2, i % 2
                        m = turn(M[b][:, i * P:(i + 1) * P], flat(O_["k"] + h, 1)[:, n * P:(n + 1) * P])
                    m.then_inc(S("gla_kt_turned"), 1)

            def gla_att(h):
                if h == 0:
                    pe.wait_ge(S("gla_kt"), 2)
                evacuated(pe, ("gv", h))
                if h >= 1:
                    pe.wait_ge(S("gla_states"), h)
                q, ki = flat(O_["q"] + h, 1), flat(O_["ki"] + h, 1)
                for n in range(2):
                    nc.tensor.matmul(M[0][:, n * P:(n + 1) * P], ki[:, n * P:(n + 1) * P], q[:, n * P:(n + 1) * P], start=True, stop=True)
                us = [M[1][:, 0:T], M[0][:, T:2 * T], M[1][:, T:2 * T]]
                for c in range(3):
                    half = slice(GLA_C * (c % 2), GLA_C * (c % 2 + 1))
                    m = nc.tensor.matmul(us[c], kt[half, h, c // 2, :], gv_tok[half, c // 2, h * T:(h + 1) * T], start=True, stop=True)
                m.then_inc(S("gla_att"), 1)

            def gla_o(h):
                pe.wait_ge(S("gla_states"), h + 1)
                if h >= 1:
                    pe.wait_ge(S("gla_sq"), h)
                q = flat(O_["q"] + h, 1)
                for vh in range(2):
                    for n in range(2):
                        at = vh * T + n * P
                        nc.tensor.matmul(M[2][:, at:at + P], gv_tok[:, n, h * T + vh * P:h * T + (vh + 1) * P], gatt(h)[:, n * P:(n + 1) * P], start=True, stop=False, skip_group_check=True)
                        for c in range(max(1, 2 * n), 2 * n + 2):
                            m = nc.tensor.matmul(M[2][:, vh * T + c * GLA_C:vh * T + (c + 1) * GLA_C], gst(h, c - 1)[:, vh * P:(vh + 1) * P],
                                                 q[:, c * GLA_C:(c + 1) * GLA_C], start=False, stop=(c == 2 * n + 1), skip_group_check=True)
                m.then_inc(S("gla_o_done"), 1)

            def gla_n(h):
                pe.wait_ge(S("gla_sq"), h + 1)
                if h == 0:
                    pe.wait_ge(S("ada_read"), 3)
                if h >= 1:
                    pe.wait_ge(S("gla_rs"), h)
                for vh in range(2):
                    m = nc.tensor.matmul(M[3][:, 0:T], K("ones"), flat(O_["sqt"] + vh, 1), start=(vh == 0), stop=(vh == 1))
                m.then_inc(S("gla_ss"), 1)

            def sb_z(h):
                if h == 0:
                    pe.wait_ge(S("gla_states"), GLA_H)
                evacuated(pe, ("sq", h // 2))
                evacuated(pe, ("sk", h // 2))
                if h >= 1:
                    pe.wait_ge(S("sb_l1p"), h)
                q, k = flat(O_["sqq"] + h, 1), flat(O_["skk"] + h, 1)
                nc.tensor.matmul(M[0][:, 0:T], k[:, 0:P], q, start=True, stop=True)
                nc.tensor.matmul(M[0][:, T:T + P], k[:, P:T], q[:, P:T], start=True, stop=True).then_inc(S("sb_z_done"), 1)

            def mix_pre():
                sum_squares(3, S_["sq"])

            def mix_post():
                sum_squares(4, S_["osq"])

            def ffn_pre():
                sum_squares(5, S_["sq"])

            def ffn_post():
                sum_squares(6, S_["sq"])

            def ple_post():
                sum_squares(7, S_["sq"])

            def lora_w():
                pe.wait_ge(S("late_in"), 64)
                pe.wait_ge(S("lora_x"), 1)
                for b in range(4):
                    m = nc.tensor.matmul(M[2 + b // 2][:, (b % 2) * T:(b % 2 + 1) * T], lora[0:32, 0, b * P:(b + 1) * P], xx[0:32, 0, :], start=True, stop=True)
                m.then_inc(S("lora_w"), 1)

            def lora_a():
                for b in range(4):
                    m = nc.tensor.matmul(M[b // 2][:, (b % 2) * T:(b % 2 + 1) * T], lora[32:64, 0, b * P:(b + 1) * P], xx[32:64, 0, :], start=True, stop=True)
                m.then_inc(S("lora_a"), 1)

            def head_sums(banks, src, sem_name, each=False):
                for b in range(4):
                    m = nc.tensor.matmul(M[banks + b // 2][:, (b % 2) * T:(b % 2 + 1) * T], K("ones_head"), flat(src + b, 1), start=True, stop=True)
                    if each and b % 2:
                        m.then_inc(S(sem_name), 1)
                if not each:
                    m.then_inc(S(sem_name), 1)

            def head_norms():
                pe.wait_ge(S("kk_sq"), 1)
                pe.wait_ge(S("sw"), 4)
                head_sums(2, S_["rn"], "kk_ss")

            def turn_v():
                pe.wait_ge(S("shift"), 3)
                pe.wait_ge(S("iclr"), 4)
                for c in range(2):
                    for b in range(4):
                        m = turn(M[c][:, b * P:(b + 1) * P], v_f[:, b, c * P:(c + 1) * P])
                    m.then_inc(S("v_turned"), 1)

            def bonus():
                pe.wait_ge(S("rk"), 1)
                pe.wait_ge(S("vt"), 2)
                head_sums(0, S_["rk"], "bonus_sum", each=True)

            def turn_bk():
                pe.wait_ge(S("rw_operands"), 1)
                for c in range(2):
                    for b in range(4):
                        m = turn(M[2 + c][:, b * P:(b + 1) * P], (b_f, kb_f)[c][:, b, 0:P])
                    m.then_inc(S("bk_turned"), 1)

            def rw_pairs(c):
                if c == 0:
                    pe.wait_ge(S("bonus"), 1)
                    pe.wait_ge(S("bkt"), 2)
                else:
                    pe.wait_ge(S("yr"), 1)
                    pe.wait_ge(S("s0"), 4)
                for s_ in range(2):
                    n = 2 * c + s_
                    if s_ == 1:
                        pe.wait_ge(S("rw_t0"), n)
                    for q in range(4):
                        b, half = head_of(s_, q)
                        hs = slice(HD * half, HD * (half + 1))
                        for k, src in enumerate((b_f, kb_f)):
                            m = nc.tensor.matmul(M[2 * k + half][:, (q % 2) * T:(q % 2 + 1) * T], src[hs, b, c * P:(c + 1) * P],
                                                 ar_[hs, b, c, :, :].rearrange("p k t -> p (k t)"), start=True, stop=True)
                    m.then_inc(S("rw_pairs"), 1)
                    pe.wait_ge(S("rw_masked"), 4 * n + 2)
                    for q in range(4):
                        b, half = head_of(s_, q)
                        hs = slice(HD * half, HD * (half + 1))
                        m = nc.tensor.matmul(M[half][:, (q % 2) * P:(q % 2 + 1) * P], ar_[hs, b, c, 0, :], b_f[hs, b, c * P:(c + 1) * P], start=True, stop=True)
                    m.then_inc(S("rw_pairs"), 1)

            def rw_u(m_):
                for s_ in range(2):
                    if m_ % 6 == 0:
                        pe.wait_ge(S("rw_t0"), 2 * (m_ // 6) + 2)
                    else:
                        pe.wait_ge(S("rw_new"), 2 * (m_ - 1) + s_ + 1)
                    nm_b, _, t_, _, _ = rset(s_)
                    for q in range(4):
                        m = nc.tensor.matmul(M[s_][:, q * P:(q + 1) * P], nm_b[:, q, 0:P], t_[:, q, :], start=True, stop=True)
                    m.then_inc(S("rw_u"), 1)

            def rw_t(m_):
                for s_ in range(2):
                    pe.wait_ge(S("rw_um"), 2 * m_ + s_ + 1)
                    _, _, t_, tt_, um = rset(s_)
                    for q in range(4):
                        m = nc.tensor.matmul(M[2 + s_][:, q * P:(q + 1) * P], um[:, q, :], tt_[:, q, :], start=True, stop=True)
                        if m_ % 6 < 5:
                            m = nc.tensor.matmul(M[s_][:, q * P:(q + 1) * P], tt_[:, q, :], um[:, q, :], start=True, stop=True)
                    m.then_inc(S("rw_t"), 1)

            def rw_solve(c):
                pe.wait_ge(S("rw_new"), 12 * c + 12)
                for s_ in range(2):
                    nm_k = rset(s_)[1]
                    for q in range(4):
                        b, half = head_of(s_, q)
                        hs = slice(HD * half, HD * (half + 1))
                        to = M[half][:, s_ * P + (q % 2) * HD:s_ * P + (q % 2 + 1) * HD]
                        m = nc.tensor.matmul(to, nm_k[:, q, 0:P], vt[:, c, (2 * b + half) * HD:(2 * b + half + 1) * HD], start=True, stop=(c == 0), skip_group_check=True)
                        if c == 1:
                            m = nc.tensor.matmul(to, ar_[hs, b, c, 0, :], s0[hs, b, :], start=False, stop=True, skip_group_check=True)
                m.then_inc(S("rw_w0"), 1)
                pe.wait_ge(S("w0"), c + 1)
                for s_ in range(2):
                    tt_ = rset(s_)[3]
                    for q in range(4):
                        m = nc.tensor.matmul(M[2][:, wcol(s_, q)], tt_[:, q, :], w0_all[:, wcol(s_, q)], start=True, stop=True)
                m.then_inc(S("rw_u0"), 1)
                pe.wait_ge(S("u0"), c + 1)
                for s_ in range(2):
                    nm_b, nm_k = rset(s_)[0:2]
                    for q in range(4):
                        b, half = head_of(s_, q)
                        hs = slice(HD * half, HD * (half + 1))
                        to = M[3][hs, b * P:(b + 1) * P]
                        nc.tensor.matmul(to, u_all[:, wcol(s_, q)], nm_b[:, q, P:2 * P], start=True, stop=False, skip_group_check=True)
                        m = nc.tensor.matmul(to, vt[:, c, (2 * b + half) * HD:(2 * b + half + 1) * HD], nm_k[:, q, P:2 * P], start=False, stop=(c == 0), skip_group_check=True)
                        if c == 1:
                            m = nc.tensor.matmul(to, s0[hs, b, :], ar_[hs, b, c, 1, :], start=False, stop=True, skip_group_check=True)
                m.then_inc(S("rw_y"), 1)
                if c == 0:
                    for s_ in range(2):
                        for q in range(4):
                            b, half = head_of(s_, q)
                            hd = slice((2 * b + half) * HD, (2 * b + half + 1) * HD)
                            to = M[0][HD * half:HD * (half + 1), b * HD:(b + 1) * HD]
                            nc.tensor.matmul(to, bt[:, hd], u_all[:, wcol(s_, q)], start=True, stop=False, skip_group_check=True)
                            m = nc.tensor.matmul(to, kbt[:, hd], vt[:, 0, hd], start=False, stop=True, skip_group_check=True)
                    m.then_inc(S("rw_s"), 1)

            def gn_mean():
                pe.wait_ge(S("yr"), 2)
                head_sums(0, S_["y"], "gn_sum", each=True)

            def gn_var():
                pe.wait_ge(S("gn_sq"), 1)
                head_sums(2, S_["gsum"], "gn_ss")

            def rw_gate():
                pe.wait_ge(S("gate_x"), 1)
                pe.wait_ge(S("gn_ln"), 2)
                for b in range(4):
                    m = nc.tensor.matmul(M[2 + b // 2][:, (b % 2) * T:(b % 2 + 1) * T], lora[0:96, 1, b * P:(b + 1) * P], xx[0:96, 1, :], start=True, stop=True)
                    if b % 2:
                        m.then_inc(S("rw_g"), 1)

            def at_s(n):
                h, i = n // 2, n % 2
                hs = slice(HD * (h % 2), HD * (h % 2 + 1))
                if n == 0:
                    pe.wait_ge(S("roped"), 6)
                    pe.wait_ge(S("gn_c"), 1)
                else:
                    pe.wait_ge(S("at_max"), n)
                if i == 1 and n >= 3:
                    pe.wait_ge(S("at_oa"), n - 1)
                q_, k_ = flat(S_["q"], 6).rearrange("p (c t) -> p c t", t=T), flat(S_["ak"], 6).rearrange("p (c t) -> p c t", t=T)
                for g in range(AT_G):
                    at = g * (i + 1) * P
                    m = nc.tensor.matmul(M[at // 512][:, at % 512:at % 512 + (i + 1) * P], q_[hs, 2 * g + h // 2, i * P:(i + 1) * P], k_[hs, 2 * g + h // 2, 0:(i + 1) * P], start=True, stop=True)
                m.then_inc(S("at_s"), 1)

            def at_t(n):
                i = n % 2
                pe.wait_ge(S("at_p"), n + 1)
                if n == 0:
                    pe.wait_ge(S("rw_out"), 1)
                else:
                    pe.wait_ge(S("at_pt"), 2 * n)
                for k in range(AT_G * (i + 1)):
                    m = turn(M[2 + k // 4][:, (k % 4) * P:(k % 4 + 1) * P], sc(n)[:, k * P:(k + 1) * P])
                m.then_inc(S("at_turned"), 1)

            def at_o(n):
                h, i = n // 2, n % 2
                hs = slice(HD * (h % 2), HD * (h % 2 + 1))
                pe.wait_ge(S("at_pt"), 2 * n + 2)
                for k in range(3):
                    evacuated(pe, ("av", k))
                pe.wait_ge(S("at_max"), min(n + 2, 2 * AT_H))
                if n >= 1:
                    pe.wait_ge(S("at_oa"), n)
                total = AT_G * (i + 1)
                for k in range(total):
                    g, st = k // (i + 1), k % (i + 1)
                    m = nc.tensor.matmul(M[1][hs, T:T + P], av_tok[:, st, g * AT_W + h * HD:g * AT_W + (h + 1) * HD], pt(n)[:, k * P:(k + 1) * P],
                                         start=(k == 0), stop=(k == total - 1), skip_group_check=True)
                m.then_inc(S("at_o"), 1)

            def turn_p():
                pe.wait_ge(S("p_in"), 16)
                for c in range(2):
                    for n in range(2):
                        m = turn(M[1][:, c * T + n * P:c * T + (n + 1) * P], ar(S_["p_in"], 2)[:, n, c * P:(c + 1) * P])
                m.then_inc(S("p_turned"), 1)

            def sb_c(h):
                pe.wait_ge(S("sb_l"), h + 1)
                if h >= 1:
                    pe.wait_ge(S("sb_arg"), h)
                nc.tensor.matmul(M[1][:, 0:384], K("from_here"), sbw(2), start=True, stop=False, skip_group_check=True)
                nc.tensor.matmul(M[1][:, P:2 * P], K("ones"), sbw(2)[:, 2 * P:3 * P], start=False, stop=True, skip_group_check=True).then_inc(S("sb_c_done"), 1)

            def sb_o(h):
                pe.wait_ge(S("sb_w"), h + 1)
                evacuated(pe, ("sv", h // 2))
                if h == 0:
                    pe.wait_ge(S("gla_sq"), GLA_H)
                    pe.wait_ge(S("gla_o"), GLA_H)
                if h >= 1:
                    pe.wait_ge(S("sb_y"), h)
                nc.tensor.matmul(M[2][:, 0:T], sv_tok[:, 0, h * P:(h + 1) * P], sbw(4)[:, 0:T], start=True, stop=False, skip_group_check=True)
                nc.tensor.matmul(M[2][:, P:T], sv_tok[:, 1, h * P:(h + 1) * P], sbw(4)[:, T:T + P], start=False, stop=True, skip_group_check=True).then_inc(S("sb_o_done"), 1)

            steps = dict(mix_pre=mix_pre, mix_post=mix_post, ffn_pre=ffn_pre, ffn_post=ffn_post, ple_post=ple_post, lora_w=lora_w, lora_a=lora_a,
                         head_norms=head_norms, turn_v=turn_v, bonus=bonus, turn_bk=turn_bk, rw_pairs=rw_pairs, rw_u=rw_u, rw_t=rw_t,
                         rw_solve=rw_solve, gn_mean=gn_mean, gn_var=gn_var, rw_gate=rw_gate, at_s=at_s, at_t=at_t, at_o=at_o, turn_p=turn_p,
                         load_x=load_x, params=params, norm=norm, final_norm=final_norm, sgu_w=sgu_w, sgu_z=sgu_z, gla_z=gla_z, gla_kt=gla_kt, gla_att=gla_att, gla_o=gla_o, gla_n=gla_n, sb_z=sb_z, sb_c=sb_c, sb_o=sb_o)

            def ada_unit(u):
                layer, blk, n = units[u]["ada"]
                if n == 0:
                    pe.wait_ge(S("x_ready"), 4)
                if n in (8, 20):
                    pe.wait_ge(S("ada_read"), 1 + n // 20)
                pe.wait_ge(S("ada_acc"), n + 1)
                for fb in range(2):
                    m = nc.tensor.matmul(M[3][:, 24 * layer + blk + fb:24 * layer + blk + fb + 1], ada_acc[n % 2][:, fb * P:(fb + 1) * P], K("ones")[:, 0:1], start=True, stop=True)
                m.then_inc(S("ada_used"), 1)

            def run_job(key):
                j = jobs[key]
                n = j["order"]
                if n >= NBANK:
                    pe.wait_ge(S(f"evacuated{n % NBANK}"), n // NBANK)
                b = bank_of(key)
                blocks, steps_ = j["blocks"], j["steps"]
                together = len(set(blocks)) == 1
                order_ = [(s, fb) for s in range(len(steps_)) for fb in range(len(blocks))]
                if not together:
                    order_.sort(key=lambda sf: (sf[1], sf[0]))
                for at, (s, fb) in enumerate(order_):
                    (u, k, xc), un, width = steps_[s], units[steps_[s][0]], blocks[fb]
                    if fb == 0 and (s == 0 or steps_[s - 1][0] != u):
                        pe.wait_ge(S("split"), un["index"] + 1)
                    if fb == 0:
                        pe.wait_ge(S(j["ready"](xc)[0]), j["ready"](xc)[1])
                    wh, wl = (w[:, un["index"] % SPL, k * un["n"]:(k + 1) * un["n"]] for w in (w_hi, w_lo))
                    xh, xl = operand(0, xc), operand(1, xc)
                    if j["layout"] == "F":
                        c = j["col"] + sum(blocks[:fb])
                        to, cs = b[0:width, fb * T:(fb + 1) * T], slice(c, c + width)
                        pairs = ((wh[:, cs], xh), (wh[:, cs], xl), (wl[:, cs], xh))
                    else:
                        ts = slice(fb * P, (fb + 1) * P)
                        cs = slice(j["col"], j["col"] + CB)
                        to = b[:, fb * CB:(fb + 1) * CB]
                        pairs = ((xh[:, ts], wh[:, cs]), (xh[:, ts], wl[:, cs]), (xl[:, ts], wh[:, cs]))
                    for q, (a_, b_) in enumerate(pairs):
                        m = nc.tensor.matmul(to, a_, b_, start=(s == 0 and q == 0 and (fb == 0 or not together)),
                                             stop=(s == len(steps_) - 1 and q == 2), skip_group_check=True)
                    if at + 1 == len(order_) or (together and steps_[order_[at + 1][0]][0] != u):
                        m.then_inc(S("projected"), 1)

            run(steps, run_job, None, ada_unit)
            if stop == "even":
                for i in range(4):
                    evacuated(pe, ("eo", i))
            elif stop == "odd":
                pe.wait_ge(S("x_update"), 8)
            else:
                pe.wait_ge(S("x_update"), 32)
            for q in range(4):
                for c in range(2):
                    for tt in range(2):
                        at = (c * 2 + tt) * P
                        m = turn(M[q][:, at:at + P], x[:, 4 * (q % 2) + 2 * c + tt, (q // 2) * P:(q // 2 + 1) * P])
                m.then_inc(S("out_turned"), 1)


def kernel(**inputs):
    import numpy as _np
    import concourse.bacc as _bacc
    from concourse import mybir as _mybir
    from concourse.bass_utils import run_bass_kernel_spmd as _run

    nc = _bacc.Bacc("TRN2", target_bir_lowering=False, num_devices=1)
    arrays, ins = {}, {}
    for name, a in inputs.items():
        a = _np.ascontiguousarray(a)
        arrays[f"in_{name}_dram"] = a
        ins[name] = nc.dram_tensor(f"in_{name}_dram", a.shape, _mybir.dt.from_np(a.dtype), kind="ExternalInput").ap()
    table = constants()
    a = _np.ascontiguousarray(_np.concatenate([table[name] for names in PHASES for name in names], 1))
    arrays["in_constants_dram"] = a
    consts = nc.dram_tensor("in_constants_dram", a.shape, _mybir.dt.from_np(a.dtype), kind="ExternalInput").ap()
    out = nc.dram_tensor("out_0_dram", (1, T, D), F32, kind="ExternalOutput").ap()
    program(nc, ins, consts, out, STOP)
    r = _run(nc, [arrays], core_ids=[0])
    return r.results[0]["out_0_dram"]
```

```python
from contextlib import ExitStack

import numpy as np

import concourse.bass as bass
from concourse import mybir
from concourse.alu_op_type import AluOpType as ALU

ACT = mybir.ActivationFunctionType
AX = mybir.AxisListType
F32 = mybir.dt.float32
F32R = mybir.dt.float32r
U32 = mybir.dt.uint32

P = 128
T = 256
D = 1024
KD = D // P
UNIT = 2048
CB = 256
RAW = 3
SPL = 3
NBANK = 4
EPS = 1e-6
WINDOWS = (2, 4, 8, 16)
PAD = max(WINDOWS)
ADA_PE = (1, 3, 5)
ADA_DVE = [n for n in range(24) if n not in ADA_PE]
GLA_H, GLA_C, GLA_TAU = 4, 64, 16.0
SB_H = 8
AT_G, AT_H, HD = 3, 4, 64
AT_W = AT_H * HD
AT_SPANS = ((128, 1), (512, 4), (2048, 16))
RW_H, RW_C = 8, 128
GN_EPS = 64e-5
KAPPA = float(np.exp(-0.5))
MASKED = -1e30



def constants():
    p = np.arange(P)
    row, col = p[:, None], p[None, :]
    t = np.arange(T)
    f = lambda a: np.ascontiguousarray(a, np.float32)
    out = {
        "ident": f(row == col),
        "ones": f(np.ones((P, P))),
        "ones_head": f(row // HD == col // HD),
        "upto": f(row <= col),
        "before": f(row < col),
        "from_here": f(row >= col),
        "gla_mask": f(np.tile((row <= col) & (row // GLA_C == col // GLA_C), (1, 2))),
        "gla_run": f(np.tile(t % GLA_C != 0, (P, 1))),
        "rw_run": f(np.tile(t % RW_C != 0, (P, 1))),
        "sb_mask": f(np.concatenate([row < col, np.ones((P, P)), row < col], 1)),
    }
    out["sb_neg"] = f(np.where(out["sb_mask"] > 0, 0.0, MASKED))
    out["inv_count"] = f(np.tile(np.concatenate([1.0 / np.minimum(t + 1, w) for w in WINDOWS])[None], (P, 1)))
    inv_freq = 10000.0 ** (-np.arange(0, HD, 2) / HD)
    ang = (t[:, None].astype(np.float32) * inv_freq[None].astype(np.float32)).astype(np.float32)
    cos, sin = np.cos(ang).T, np.sin(ang).T
    out["cos"] = f(np.tile(cos, (4, 1)))
    out["sin"] = f(np.concatenate([-sin, sin, -sin, sin], 0))
    for i in range(2):
        tt = i * P + p[:, None]
        s = np.arange((i + 1) * P)[None]
        out[f"at_neg{i}"] = f(np.concatenate(
            [np.where((tt >= s) & ((tt - s) % dil == 0) & (tt - s <= win), 0.0, MASKED) for win, dil in AT_SPANS], 1))
    b = 1
    while b < RW_C:
        m = (row // (2 * b) == col // (2 * b)) & ((row // b) % 2 == 1) & ((col // b) % 2 == 0)
        out[f"pair{b}"] = f(m)
        b *= 2
    out["pair1_t"] = f(out["pair1"].T)
    return out


def layout(sizes):
    at, places = 0, {}
    for name, n in sizes:
        places[name] = (at, n)
        at += n
    return places, at


BASE = ("ident", "ones", "ones_head", "before", "upto", "from_here")
ODD_ONLY = ("gla_mask", "gla_run", "sb_mask", "sb_neg")
PHASES = (BASE, ("inv_count",), ODD_ONLY,
          tuple(k for k in constants() if k not in BASE + ODD_ONLY + ("inv_count",)))
CONST_PLACES = [layout([(k, constants()[k].shape[1]) for k in ph]) for ph in PHASES]
CONST_AT = [sum(c[1] for c in CONST_PLACES[:i]) for i in range(5)]

ROWS_A, NROWS_A = layout([("ada_b", 48), ("norm_g", 16), ("pool_scale", 8), ("sgu_norm_g", 8), ("gla_gate_b", 4),
                          ("gla_norm_g", 8), ("final_g", 8)])
ROWS_B, NROWS_B = layout([("mix_pre_norm_2", 8), ("rwkv_mu_2", 14), ("rwkv_w0_2", 4), ("rwkv_a0_2", 4),
                          ("rwkv_k_k_2", 4), ("rwkv_k_a_2", 4), ("rwkv_r_k_2", 4), ("rwkv_ln_w_2", 4),
                          ("rwkv_ln_b_2", 4), ("mix_post_norm_2", 8), ("ffn_pre_norm_2", 8),
                          ("ffn_post_norm_2", 8), ("ple_post_norm_2", 8)])

WORK, SPARE = 58, 100
S_ = dict(sq=0, h=8, r=34, k=38, v=42, xx=56, zr=16, zk=21, zv=26, zx=31, lora=52,
          sw=12, a=8, cs=25, cc=29, er=SPARE, kk=SPARE + 4, rn=SPARE + 8, kt=SPARE + 12, rk=SPARE + 16,
          ar=0, b=8, kb=12, bonus=SPARE + 20, vt=SPARE + 24, bt=SPARE + 28, kbt=SPARE + 30, sets=16, y=48,
          gsum=0, grs2=8, q=SPARE, ak=SPARE + 6, av=SPARE + 12, swap=50,
          gate=16, sc=32, pt=38, oa=44, m=0, o=32, osq=40, sg=16, yt=20, f=24, p_in=40, p=42, e=44)
N_ROW_LOADS = 22
E_ = dict(v=0, a=8, lev1=17, lev2=26, u=35, wraw=43, wt=47, bb=51, sq=0, h=35, vsq=35, sg=26, yt=30, z=34, inv=SPARE + 8)
O_ = dict(q=0, ki=4, sqq=8, skk=16, svv=24, sb=32, sg=40, yt=44, sq=8, h=16,
          k=SPARE, v=SPARE + 4, kt=SPARE + 12, t1=SPARE + 16, la=SPARE + 20, e=SPARE + 24, sqt=SPARE + 28,
          rs=SPARE + 30, glr=SPARE + 31, st=SPARE + 16, att=SPARE + 22)


def program(nc, ins, consts, out):
    x_in = ins["x"].rearrange("a (n p) d -> p (a n) d", p=P)
    out_t = out.rearrange("a (n p) d -> p (a n) d", p=P)

    units, jobs, schedule, ada_count = [], {}, [], [0]

    def unit(w, k0, nk, c0, nc_, ada=None):
        units.append(dict(src=w[k0 * P:(k0 + nk) * P, c0:c0 + nc_].rearrange("(k p) n -> p k n", p=P),
                          nk=nk, n=nc_, ada=ada, order=len(units), index=sum(u["ada"] is None for u in units)))
        return len(units) - 1

    def job(name, kind, i, layout_, unit_list, nk, x0, ready, col=0, k0=0, blocks=(P, P), x_of=None):
        steps = [(u, k0 + k, x_of[n * nk + k] if x_of else x0 + n * nk + k) for n, u in enumerate(unit_list) for k in range(nk)]
        jobs[name, i] = dict(order=len(jobs), kind=kind, i=i, layout=layout_, steps=steps, ready=ready, col=col,
                             blocks=blocks, name=name)
        schedule.append(("job", (name, i)))

    def early(name, i):
        assert schedule[-1] == ("job", (name, i))
        schedule[-1] = ("project", (name, i))

    def finish(name, i):
        schedule.append(("evacuate", (name, i)))

    def proj(name, kind, w, c0, n, x0, ready, layout_="F", kparts=1):
        for i in range(n):
            us = [unit(w, KD * kp, KD, c0 + i * CB, CB) for kp in range(kparts)]
            job(name, kind, i, layout_, us, KD, x0, ready)

    def step(name, i=None):
        schedule.append(("step", (name, i)))

    def ada(layer, part, i):
        c0 = part * D + i * CB
        schedule.append(("ada", unit(ins["ada_w"][layer], 0, KD, c0, CB, ada=(layer, c0 // P, ada_count[0]))))
        ada_count[0] += 1

    even_w, odd_w, w2nd = ins["even_in_w"][0], ins["odd_in_w"][0], ins["w_in_2"][0]
    HR = lambda n: (lambda xc: ("operand_ready", 8 * n + xc + 1))
    later_ada = [(0, 2, i) for i in range(4)] + [(1, part, i) for part in range(3) for i in range(4)]

    def even(name, kind, w, c0, layout_="F"):
        for i in range(4):
            job(name, kind, i, layout_, [unit(w, 0, KD, c0 + i * CB, CB)], KD, 0, HR(0))
            if i < 3 and len(later_ada) > 4 and name != "eu":
                ada(*later_ada.pop(0))

    step("load_x")
    step("first_sum")
    for part in range(2):
        for i in range(4):
            ada(0, part, i)
            if (part, i) == (0, 3):
                step("first_scale")
    step("params")
    step("ada_first")
    step("norm", 0)
    even("ev", "copy_t", even_w, 2048, "T")
    step("sgu_w")
    even("ea", "copy", even_w, 0)
    step("sgu_v")
    for i in range(4):
        job("eu", "copy", i, "F", [unit(even_w, 0, KD, 1024 + i * CB, CB)], KD, 0, HR(0))
        step("windows", i)
    for i in range(4):
        step("sgu_z", i)
        job("egb", "gate", i, "F", [unit(even_w, 0, KD, 4096 + i * CB, CB)], KD, 0, HR(0))
        if i < 3:
            ada(*later_ada.pop(0))
    pool_u = unit(ins["pool_w"][0].rearrange("g c d -> (g c) d"), 0, 8, 0, CB)
    for g in range(4):
        job("pool", "pool", g, "F", [pool_u], 2, 8 + 2 * g, lambda xc: ("p_lo", 1), k0=2 * g)
    even("ega", "gate", even_w, 3072)
    step("ada_rest")
    for i in range(4):
        us = [unit(ins["even_out_w"][0], KD * kp, KD, i * CB, CB) for kp in (1, 0)]
        job("eo", "residual", i, "F", us, KD, None, lambda xc: ("y_lo", 1 + (xc - 16) // 2 if xc >= 16 else 5 + (xc - 8) // 2),
            x_of=[16 + k for k in range(KD)] + [8 + k for k in range(KD)])
    def odd(name, kind, c0, i, layout_="F", n=CB, blocks=(P, P)):
        job(name, kind, i, layout_, [unit(odd_w, 0, KD, c0 + i * CB, n)], KD, 0, HR(1), blocks=blocks)

    def pipeline(names, n):
        for slot in range(n + len(names) - 1):
            yield [(names[k], slot - k) for k in reversed(range(len(names))) if 0 <= slot - k < n]

    step("norm", 1)
    for i in range(2):
        odd("gk", "copy", 512, i)
    odd("glr", "copy16", 2048, 0, n=16, blocks=(16,))
    odd("gq", "copy", 0, 0)
    step("gla_z")
    odd("gq", "copy", 0, 1)
    for i in range(4):
        odd("gv", "copy_t", 1024, i, "T")
        if i == 1:
            step("gla_decay")
    odd("sq", "copy", 2064, 0)
    step("gla_kt")
    gla = pipeline(("gla_att", "gla_o", "gla_n"), GLA_H)
    sbs = pipeline(("sb_z", "sb_c", "sb_o"), SB_H)
    order = [("sk", "copy", 3088, 0), ("sv", "copy_t", 4112, 0)]
    for i in range(1, 4):
        order += [("sq", "copy", 2064, i), ("sk", "copy", 3088, i), ("sv", "copy_t", 4112, i)]
    for n, (name, kind, c0, i) in enumerate(order):
        odd(name, kind, c0, i, "T" if kind == "copy_t" else "F")
        for st in next(gla, None) or next(sbs, []):
            step(*st)
    left = list(sbs)
    for i in range(8):
        odd("gga" if i < 4 else "ggb", "gate", 5136 if i < 4 else 6160, i % 4)
        for st in left[i] if i < len(left) else []:
            step(*st)
        if i >= 4:
            ada(*later_ada.pop(0))
    assert len(left) <= 8
    step("ada_last")
    proj("oo", "residual", ins["odd_out_w"][0], 0, 4, 8, lambda xc: ("y_lo", 8 + (xc - 8) // 2 + 1), kparts=2)
    step("final_norm")
    def second(name, kind, c0, i, layout_="F", n=CB, blocks=(P, P)):
        job(name, kind, i, layout_, [unit(w2nd, 0, KD, c0 + i * CB, n)], KD, 0, HR(2), blocks=blocks)

    step("mix_pre")
    second("wx", "wx", 3840, 0, n=160, blocks=(64, 96))
    step("shift_x")
    second("wk", "shifted", 2816, 0)
    second("wk", "shifted", 2816, 1)
    step("lora_w")
    step("lora_a")
    step("shift_k")
    step("key_sq")
    for i in range(2):
        second("wv", "shifted", 3328, i)
    step("key_norms")
    for i in range(2):
        second("wr", "shifted", 2304, i)
    step("shift_v")
    attn = [("aq", "rope", 0, i, "F") for i in range(3)] + [("ak", "rope", 768, i, "F") for i in range(3)]
    attn += [("av", "copy_t", 1536, i, "T") for i in range(3)]
    waiting = []

    def ahead():
        if attn:
            name, kind, c0, i, lay = attn.pop(0)
            second(name, kind, c0, i, lay)
            early(name, i)
            waiting.append((name, i))

    def catch_up(n=1):
        for _ in range(n):
            if waiting:
                finish(*waiting.pop(0))

    ahead()
    step("turn_v")
    step("shift_r")
    ahead()
    ahead()
    step("decays")
    step("key_unit")
    ahead()
    step("rw_inputs")
    step("bonus")
    step("turn_bk")
    catch_up()
    for c in range(2):
        for s_ in range(2):
            step("rw_pairs", 2 * c + s_)
            ahead()
            step("rw_pair_t", 2 * c + s_)
            if s_ == 0:
                catch_up()
        for n in range(6):
            step("rw_u", 6 * c + n)
            step("rw_t", 6 * c + n)
            if c == 0 or n % 3 == 2:
                catch_up()
            if n == 3:
                ahead()
        step("solve_w", c)
        if attn:
            ahead()
        else:
            second("wga", "sigmoid", 4000, 0)
            early("wga", 0)
        catch_up(2)
        step("solve_u", c)
        step("solve_y", c)
    assert not attn and not waiting, (attn, waiting)
    at = pipeline(("at_s", "at_t", "at_o"), 2 * AT_H)
    for i in range(4):
        if i > 0:
            second("wga", "sigmoid", 4000, i)
        if i == 0:
            step("gn_mean")
            finish("wga", 0)
        if i == 1:
            step("rw_gate")
        for st in next(at, []):
            step(*st)
        if i == 0:
            step("gn_var")
    for i in range(4):
        second("wgb", "sigmoid", 5024, i)
        for st in next(at, []):
            step(*st)
    for sts in at:
        for st in sts:
            step(*st)
    step("mixed")
    for i in range(0, 4, 2):
        us = unit(ins["w_rwkv_up_2"][0], 0, 4, i * CB, 2 * CB)
        for k in range(2):
            job("ru", "up", i + k, "F", [us], 4, 8, lambda xc: ("mixed_lo", 1), col=k * CB)
        if i == 0:
            ua = unit(ins["w_attn_up_2"][0], 0, 2, 0, 4 * CB)
        for k in range(2):
            job("au", "up", i + k, "F", [ua], 2, 12, lambda xc: ("mixed_lo", 2), col=(i + k) * CB)
    proj("wo", "out", ins["w_out_2"][0], 0, 4, 16, lambda xc: ("merged_lo", (xc - 16) // 2 + 1))
    step("mix_post")
    step("ffn_pre")
    for half in range(2):
        for i in range(8):
            job("fi", "relu2", 8 * half + i, "F", [unit(ins["w_ff_in_2"][0], 0, KD, (8 * half + i) * CB, CB)], KD, 0, HR(3))
        for i in range(4):
            us = [unit(ins["w_ff_out_2"][0], 16 * half + 8 * kp, KD, i * CB, CB) for kp in range(2)]
            job(f"fo{half}", f"ffn{half}", i, "F", us, KD, 8, lambda xc, half=half: ("y_lo", 16 + 8 * half + (xc - 8) // 2 + 1))
    step("turn_p")
    step("ffn_post")
    us = unit(ins["w_ple_2"][0], 0, 2, 0, 4 * CB)
    for i in range(4):
        job("pe", "ple", i, "F", [us], 2, 8, lambda xc: ("p_lo", 2), col=i * CB)
        early("pe", i)
    for i in range(4):
        finish("pe", i)
    step("ple_x")
    for i in range(4):
        job("pg", "ple_gate", i, "F", [unit(ins["w_ple_gate_2"][0], 0, KD, i * CB, CB)], KD, 0, HR(4))
    step("ple_post")
    step("store")

    visits = 0
    for j in jobs.values():
        for u in sorted({u for u, _, _ in j["steps"]}):
            visits += 1
            units[u]["visited"] = visits
        j["projected"] = visits

    ctx = ExitStack()
    with ctx:
        def sb(name, shape, dt=F32):
            return ctx.enter_context(nc.sbuf_tensor(name, shape, dt))

        sems = {}

        def S(name):
            if name not in sems:
                sems[name] = ctx.enter_context(nc.semaphore(name))
            return sems[name]

        raw = sb("raw", [P, RAW, UNIT])
        w_hi = sb("w_hi", [P, SPL, UNIT], F32R)
        w_lo = sb("w_lo", [P, SPL, UNIT], F32R)
        h_hi = sb("h_hi", [P, KD, T], F32R)
        h_lo = sb("h_lo", [P, KD, T], F32R)
        x = sb("x", [P, KD, T])
        cst = sb("cst", [P, CONST_PLACES[0][1]])
        cst_phase = sb("cst_phase", [P, max(CONST_PLACES[2][1], CONST_PLACES[3][1])])
        rows = sb("rows", [P, 2, P])
        cols = sb("cols", [P, 2, P])
        ada_c = sb("ada_c", [P, 2, 24])
        mod = sb("mod", [P, 2, KD])
        silu_c = sb("silu_c", [P, KD])
        small = sb("small", [P, 64])
        rstd = sb("rstd", [P, T])
        s0 = sb("s0", [P, 4, HD])
        work = sb("work", [P, WORK, T])
        with nc.sbuf_tensor("spare", [P, 32, T], F32) as spare:
            pass
        y_hi = sb("y_hi", [P, 16, T], F32R)
        y_lo = sb("y_lo", [P, 16, T], F32R)
        PJ = [ctx.enter_context(nc.psum_tensor(f"pj{i}", [P, 512], F32)) for i in range(NBANK)]
        M = [ctx.enter_context(nc.psum_tensor(f"m{i}", [P, 512], F32)) for i in range(4)]

        def ar(c, n=1):
            return work[:, c:c + n, :] if c < SPARE else spare[:, c - SPARE:c - SPARE + n, :]

        def flat(c, n):
            return ar(c, n).rearrange("p c t -> p (c t)")

        def K(name):
            for ph, (places, _) in enumerate(CONST_PLACES):
                if name in places:
                    a, n = places[name]
                    return (cst, flat(E_["inv"], 4), cst_phase, cst_phase)[ph][:, a:a + n]
            raise KeyError(name)

        def vec(name, i=0, n=1):
            places, half = (ROWS_A, 0) if name in ROWS_A else (ROWS_B, 1)
            return cols[:, half, places[name][0] + i:places[name][0] + i + n]

        def bc(ap, n, at=1):
            shape = list(ap.shape)
            return ap.unsqueeze(at).broadcast_to(shape[:at] + [n] + shape[at:])

        def operand(part, xc):
            h, y = ((h_hi, y_hi), (h_lo, y_lo))[part]
            return h[:, xc, :] if xc < KD else y[:, xc - KD, :]

        def evacuated(eng, key):
            n = jobs[key]["order"]
            eng.wait_ge(S(f"evacuated{n % NBANK}"), n // NBANK + 1)

        def projected(eng, key):
            eng.wait_ge(S("projected"), jobs[key]["projected"])

        def split_done(eng, i):
            eng.wait_ge(S(f"split{i % SPL}"), i // SPL + 1)

        def bank_of(key):
            return PJ[jobs[key]["order"] % NBANK]

        def done_reading(ins_, key):
            ins_.then_inc(S(f"evacuated{jobs[key]['order'] % NBANK}"), 1)

        for k in range(4):
            S(f"evacuated{k}")
        for k in range(RAW):
            S(f"unit_loaded{k}")
        for k in range(SPL):
            S(f"split{k}")

        dest = {"ev": E_["v"], "ea": None, "eu": E_["u"], "gq": O_["q"], "gk": O_["k"], "gv": O_["v"],
                "sq": O_["sqq"], "sk": O_["skk"], "sv": O_["svv"], "av": S_["av"]}
        shifted = {"wr": (S_["zr"], S_["r"], 4, 0), "wk": (S_["zk"], S_["k"], 4, 4), "wv": (S_["zv"], S_["v"], 4, 8),
                   "wx": (S_["zx"], S_["xx"], 2, 12)}
        a_pad = work[:, E_["a"]:E_["a"] + 9, :].rearrange("p c t -> p (c t)")[:, 0:8 * (T + PAD)].rearrange(
            "p (c t) -> p c t", c=8)
        lev = [work[:, c:c + 9, :].rearrange("p c t -> p (c t)")[:, 0:8 * (T + PAD)].rearrange(
            "p (c t) -> p c t", c=8) for c in (E_["lev1"], E_["lev2"])]
        gates = [k for kind, k in schedule if kind == "job" and jobs[k]["kind"] in ("gate", "relu2")]
        ropes = [k for kind, k in schedule if kind in ("job", "evacuate") and jobs[k]["kind"] == "rope"]
        gate_mix = {"egb": lambda i: (ar(E_["u"] + 2 * i, 2), 8 + 2 * i),
                    "ega": lambda i: (a_pad[:, 2 * i:2 * i + 2, PAD:], 2 * i),
                    "gga": lambda i: (GO(i), 2 * i),
                    "ggb": lambda i: (ar(O_["sqq"] + 2 * i, 2), 8 + 2 * i)}

        def GO(h):
            return work[:, O_["q"]:O_["q"] + 8, :].rearrange("p (b c) t -> p b c t", c=4)[:, :, h, :]

        s0_flat = s0[:, :, :].rearrange("p b d -> p (b d)")
        ada_acc = (flat(55, 1), s0_flat)
        c_rows = s0_flat[0:KD, 0:P]
        v_tok = flat(E_["v"], 8).rearrange("p (n d) -> p n d", n=2)
        w_raw = flat(E_["wraw"], 4).rearrange("p (h s) -> p h s", h=8)
        w_t = flat(E_["wt"], 4).rearrange("p (h s) -> p h s", h=8)
        b_all = flat(E_["bb"], 4).rearrange("p (h s) -> p h s", h=8)
        gv_tok = flat(O_["v"], 8).rearrange("p (n d) -> p n d", n=2)
        kt = flat(O_["kt"], 4).rearrange("p (h n k) -> p h n k", h=GLA_H, n=2)
        sv_tok = flat(O_["svv"], 8).rearrange("p (n d) -> p n d", n=2)

        small_zero = small[:, 40:41]
        eps_col = small[:, 41:42]
        gn_eps_col = small[:, 42:43]
        gate_w = work[0:16, 56:58, :].rearrange("p c t -> p (c t)")
        ar_ = flat(S_["ar"], 8).rearrange("p (b c k t) -> p b c k t", b=4, c=2, k=2)
        b_f = flat(S_["b"], 4).rearrange("p (b t) -> p b t", b=4)
        kb_f = flat(S_["kb"], 4).rearrange("p (b t) -> p b t", b=4)
        r_f, k_f, v_f = (flat(S_[n], 4).rearrange("p (b t) -> p b t", b=4) for n in "rkv")
        xx = flat(S_["xx"], 2).rearrange("p (b t) -> p b t", b=2)
        lora = flat(S_["lora"], 4).rearrange("p (w n) -> p w n", w=2)
        vt = flat(S_["vt"], 4).rearrange("p (c n) -> p c n", c=2)
        bt, kbt = flat(S_["bt"], 2), flat(S_["kbt"], 2)
        y_f = flat(S_["y"], 4).rearrange("p (b t) -> p b t", b=4)
        av_tok = flat(S_["av"], 6).rearrange("p (n d) -> p n d", n=2)
        oa = ar(S_["oa"], 2)
        log_decay = -KAPPA

        def zpad(name):
            at, _, n, _ = shifted[name]
            return flat(at, 5 if n == 4 else 3)[:, 0:n * (T + 1)].rearrange("p (b t) -> p b t", b=n)

        def rset(s):
            c = S_["sets"] + 16 * s
            nm_b = flat(c, 4).rearrange("p (q w) -> p q w", q=4)
            nm_k = flat(c + 4, 4).rearrange("p (q w) -> p q w", q=4)
            t_, tt_, um = (flat(c + 8 + 2 * i, 2).rearrange("p (q w) -> p q w", q=4) for i in range(3))
            return nm_b, nm_k, t_, tt_, um

        w0_all, u_all = flat(S_["sets"] + 14, 2), flat(S_["sets"] + 30, 2)

        def head_of(s, q):
            return 2 * s + q % 2, q // 2

        def wcol(s, q):
            c = (q // 2) * 256 + s * 128 + (q % 2) * HD
            return slice(c, c + HD)

        def sc(n):
            return flat(S_["sc"] + 3 * (n % 2), 3)[:, 0:(n % 2 + 1) * 384]

        def pt(n):
            return flat(S_["pt"] + 3 * (n % 2), 3)

        split_units = [u for u in units if u["ada"] is None]
        last_unit = {key: units[j["steps"][-1][0]]["index"] for key, j in jobs.items()}

        def normed_at(n):
            return ar((E_["h"], O_["h"], S_["h"], S_["h"], S_["h"])[n], 8)

        def gate_tmp(which, g):
            places = E_ if g < 8 else O_ if g < 16 else S_
            return ar(places[which] + 2 * (g % 2), 2)

        def gst(h, c):
            return flat(O_["st"] + 3 * (h % 2) + c, 1)

        def gatt(h):
            return flat(O_["att"] + h % 2, 1)

        def sbw(k):
            return flat(O_["sb"], 8)[:, 384 * k:384 * (k + 1)]

        def run(steps, job_part, split_to, ada_part=None):
            for kind, what in schedule:
                if kind == "job":
                    if split_to is not None:
                        split_to(last_unit[what] + SPL)
                    job_part(what)
                elif kind == "project":
                    if split_to is not None:
                        split_to(last_unit[what] + SPL)
                    else:
                        job_part(what)
                elif kind == "evacuate":
                    if split_to is not None:
                        job_part(what)
                elif kind == "ada" and ada_part:
                    ada_part(what)
                elif kind == "step" and what[0] in steps:
                    if what[1] is None:
                        steps[what[0]]()
                    else:
                        steps[what[0]](what[1])

        block = ctx.enter_context(nc.Block())

        @block.sync
        def _(sp):
            def load_all_rows():
                sp.wait_ge(S("rows_zero"), 1)
                n = 0

                def load_rows(half, r, src):
                    sp.dma_start(rows[r:r + src.shape[0], half, 0:src.shape[1]], src).then_inc(S("rows_loaded"), 16)

                for half, places in ((0, ROWS_A), (1, ROWS_B)):
                    for name, (r, nr) in places.items():
                        a = ins[name]
                        if name == "rwkv_mu_2":
                            load_rows(half, r, a[0:1, 0:1536].rearrange("a (n p) -> (a n) p", p=P))
                            load_rows(half, r + 12, a[0:1, 1536:1600])
                            load_rows(half, r + 13, a[0:1, 1600:1696])
                            n += 3
                            continue
                        if name == "gla_norm_g":
                            a = a.rearrange("a h (n p) -> (a h n) p", p=P)
                        elif name == "rwkv_r_k_2":
                            a = a.rearrange("a (b h) d -> (a b) (h d)", h=2)
                        elif len(a.shape) == 1:
                            a = a.rearrange("(n p) -> n p", p=P)
                        else:
                            a = a.rearrange("a (n p) -> (a n) p", p=P)
                        load_rows(half, r, a)
                        n += 1
                assert n == N_ROW_LOADS, n

            sp.dma_start(c_rows, ins["c"].rearrange("a (n p) -> (a n) p", p=P)).then_inc(S("c_in"), 16)
            for u, un in enumerate(units):
                if u == RAW:
                    load_all_rows()
                if u >= RAW:
                    old = units[u - RAW]
                    if old["ada"] is None:
                        split_done(sp, old["index"])
                    else:
                        n = old["ada"][2]
                        if n in ADA_PE:
                            sp.wait_ge(S("ada_used"), n + 1)
                        else:
                            sp.wait_ge(S("ada_acc"), ADA_DVE.index(n) + 1)
                sp.dma_start(raw[:, u % RAW, 0:un["nk"] * un["n"]].rearrange("p (k n) -> p k n", k=un["nk"]),
                             un["src"]).then_inc(S(f"unit_loaded{u % RAW}"), 16)

        def unit_loaded(eng, u):
            eng.wait_ge(S(f"unit_loaded{u % RAW}"), 16 * (u // RAW + 1))

        def chainer(eng, name):
            count = [0]

            def link(ins_):
                count[0] += 1
                ins_.then_inc(S(name), 1)
                eng.wait_ge(S(name), count[0])
            return link

        @block.gpsimd
        def _(pool):
            pool.memset(small_zero, 0.0).then_inc(S("scalars_set"), 1)
            pool.memset(gn_eps_col, GN_EPS).then_inc(S("scalars_set"), 1)
            pool.memset(eps_col, EPS).then_inc(S("scalars_set"), 1)
            pool.memset(rows[:, :, :], 0.0).then_inc(S("rows_zero"), 1)
            pool.memset(a_pad[:, :, 0:PAD], 0.0).then_inc(S("pad_zero"), 1)
            pool.memset(lev[0][:, :, 0:PAD], 0.0).then_inc(S("pad_zero"), 1)
            pool.memset(lev[1][:, :, 0:PAD], 0.0).then_inc(S("pad_zero"), 1)
            pool.wait_ge(S("rstd_inv"), 1)
            nc.gpsimd.tensor_tensor(normed_at(0), x[:, :, :], bc(rstd[:, :], KD), ALU.mult).then_inc(S("x_scaled"), 1)
            for i in range(0, len(split_units), 2):
                u, n = split_units[i]["order"], split_units[i]["nk"] * split_units[i]["n"]
                pool.wait_ge(S("split_hi"), i + 1)
                nc.gpsimd.tensor_tensor(w_lo[:, i % SPL, 0:n], raw[:, u % RAW, 0:n], w_hi[:, i % SPL, 0:n].bitcast(F32), ALU.subtract).then_inc(S(f"split{i % SPL}"), 1)

        @block.scalar
        def _(act):
            link = chainer(act, "act_chain")
            act.dma_start(cst[:, :], consts[:, CONST_AT[0]:CONST_AT[1]]).then_inc(S("const_in"), 16)
            act.dma_start(ar(0, 8).rearrange("p (n c) t -> p n (c t)", n=2), x_in).then_inc(S("x_in"), 16)
            act.dma_start(flat(E_["inv"], 4), consts[:, CONST_AT[1]:CONST_AT[2]]).then_inc(S("inv_in"), 16)
            act.dma_start(cst_phase[:, 0:CONST_PLACES[2][1]], consts[:, CONST_AT[2]:CONST_AT[3]]).then_inc(S("odd_const_in"), 16)
            act.dma_start(gate_w, ins["gla_gate_w"][0]).then_inc(S("gate_w_in"), 16)
            act.dma_start(w_raw, ins["sgu_w"][0].rearrange("h t s -> t h s")).then_inc(S("sgu_in"), 16)
            act.dma_start(b_all, ins["sgu_b"][0].rearrange("h t -> (h t)").partition_broadcast(P).rearrange("p (h t) -> p h t", h=8)).then_inc(S("sgu_in"), 16)
            next_split = [0]

            def split_to(end):
                while next_split[0] < min(end, len(split_units)):
                    i = next_split[0]
                    next_split[0] += 1
                    u, n = split_units[i]["order"], split_units[i]["nk"] * split_units[i]["n"]
                    unit_loaded(act, u)
                    if i >= SPL:
                        act.wait_ge(S("projected"), split_units[i - SPL]["visited"])
                    nc.scalar.activation(w_hi[:, i % SPL, 0:n], raw[:, u % RAW, 0:n], ACT.Copy).then_inc(S("split_hi"), 1)

            def squares(n, src, sq, wait):
                for q in range(4):
                    wait(act, q)
                    nc.scalar.activation(ar(sq + 2 * q, 2), src[:, 2 * q:2 * q + 2, :], ACT.Square).then_inc(S("squares"), 1)
                link(nc.scalar.activation(small[:, 44:45], eps_col, ACT.Sqrt))
                act.wait_ge(S("sum_sq"), n + 1)
                nc.scalar.activation(rstd[:, :], M[0][:, 0:T], ACT.Sqrt, bias=eps_col, scale=1.0 / D).then_inc(S("rstd"), 1)

            def upper(n):
                for k in range(KD):
                    act.wait_ge(S("normed"), 8 * n + k + 1)
                    nc.scalar.activation(h_hi[:, k, :], normed_at(n)[:, k, :], ACT.Copy).then_inc(S("operand_hi"), 1)

            def load_x():
                act.wait_ge(S("c_turned"), 1)
                nc.scalar.activation(silu_c[:, :], PJ[0][:, 0:KD], ACT.Silu).then_inc(S("silu_c"), 1)
                for q in range(4):
                    act.wait_ge(S("x_turned"), q + 1)
                    nc.scalar.activation(x[:, 2 * q:2 * q + 2, :], M[q][:, :].rearrange("p (c t) -> p c t", c=2), ACT.Copy).then_inc(S("x_ready"), 1)

            def params():
                act.wait_ge(S("params_turned"), 1)
                nc.scalar.activation(cols[:, :, :], PJ[1][:, 0:2 * P].rearrange("p (c t) -> p c t", c=2), ACT.Copy).then_inc(S("params"), 1)

            def first_sum():
                squares(0, x, E_["sq"], lambda e, q: e.wait_ge(S("x_ready"), q + 1))

            def norm(n):
                if n == 0:
                    split_to(1)
                else:
                    squares(1, x, O_["sq"], lambda e, q: evacuated(e, ("eo", q)))
                upper(n)

            def final_norm():
                act.wait_ge(S("sb_arg"), SB_H)
                act.wait_ge(S("sb_y"), SB_H)
                act.wait_ge(S("gla_states"), GLA_H)
                act.dma_start(cst_phase[:, 0:CONST_PLACES[3][1]], consts[:, CONST_AT[3]:CONST_AT[4]]).then_inc(S("late_in"), 16)
                act.dma_start(lora[0:32, 0, :], ins["rwkv_w2_2"][0]).then_inc(S("late_in"), 16)
                act.dma_start(lora[32:64, 0, :], ins["rwkv_a2_2"][0]).then_inc(S("late_in"), 16)
                act.dma_start(lora[0:96, 1, :], ins["rwkv_g2_2"][0]).then_inc(S("late_in"), 16)
                squares(2, x, O_["sq"], lambda e, q: evacuated(e, ("oo", q)))

            def sgu_v():
                for tt in range(2):
                    for i in range(4):
                        evacuated(act, ("ev", i))
                    if tt == 1:
                        act.wait_ge(S("v_sq"), 1)
                    nc.scalar.activation(flat(E_["vsq"], 4), v_tok[:, tt, :], ACT.Square, accum_out=small[:, tt:tt + 1]).then_inc(S("v_sq"), 1)
                act.wait_ge(S("v_sq"), 2)
                link(nc.scalar.activation(small[:, 2:4], small[:, 0:2], ACT.Ln, bias=eps_col, scale=1.0 / D))
                nc.scalar.activation(small[:, 4:6], small[:, 2:4], ACT.Exp, scale=-0.5).then_inc(S("v_rstd"), 1)

            def windows(part):
                if part < 3:
                    return
                act.wait_ge(S("p"), 1)
                nc.scalar.activation(y_hi[:, 0:8, :], lev[0][:, :, PAD:], ACT.Copy).then_inc(S("p_hi"), 1)

            def gla_z():
                for h in range(GLA_H):
                    act.wait_ge(S("gla_z"), h // 2 + 1)
                    nc.scalar.activation(ar(O_["la"] + h), M[h // 2][:, (h % 2) * T:(h % 2 + 1) * T].unsqueeze(1), ACT.Identity,
                                         bias=vec("gla_gate_b", h)).then_inc(S("gla_la"), 1)
                act.wait_ge(S("gla_la"), 4)
                link(nc.scalar.activation(flat(O_["t1"], 4), flat(O_["la"], 4), ACT.Abs))
                link(nc.scalar.activation(flat(O_["t1"], 4), flat(O_["t1"], 4), ACT.Exp, scale=-1.0))
                nc.scalar.activation(flat(O_["t1"], 4), flat(O_["t1"], 4), ACT.Ln, bias=1.0).then_inc(S("gla_l1p"), 1)

            def gla_decay():
                act.wait_ge(S("gla_cum"), 1)
                nc.scalar.activation(flat(O_["e"], 4), flat(O_["la"], 4), ACT.Exp, scale=1 / GLA_TAU).then_inc(S("gla_exp"), 1)
                act.wait_ge(S("gla_t1_free"), 1)
                nc.scalar.activation(flat(O_["t1"], 4), flat(O_["la"], 4), ACT.Exp, scale=-1 / GLA_TAU).then_inc(S("gla_exp"), 1)
                act.wait_ge(S("gla_rest"), 1)
                nc.scalar.activation(flat(O_["t1"], 4), flat(O_["t1"], 4), ACT.Exp, scale=1 / GLA_TAU).then_inc(S("gla_exp"), 1)

            def gla_kt():
                for b in range(2):
                    act.wait_ge(S("gla_kt_turned"), b + 1)
                    nc.scalar.activation(flat(O_["kt"] + 2 * b, 2), M[b][:, :], ACT.Copy).then_inc(S("gla_kt"), 1)

            def gla_o(h):
                act.wait_ge(S("gla_o_done"), h + 1)
                nc.scalar.activation(GO(h), M[2][:, :].rearrange("p (c t) -> p c t", c=2), ACT.Copy).then_inc(S("gla_o"), 1)
                if h >= 1:
                    act.wait_ge(S("gla_ss"), h)
                nc.scalar.activation(flat(O_["sqt"], 2), M[2][:, :], ACT.Square).then_inc(S("gla_sq"), 1)

            def gla_n(h):
                act.wait_ge(S("gla_ss"), h + 1)
                if h >= 1:
                    act.wait_ge(S("gla_yc"), h)
                link(nc.scalar.activation(flat(O_["rs"], 1), M[3][:, 0:T], ACT.Ln, bias=eps_col, scale=1.0 / 256))
                nc.scalar.activation(flat(O_["rs"], 1), flat(O_["rs"], 1), ACT.Exp, scale=-0.5).then_inc(S("gla_rs"), 1)

            def sb_z(h):
                act.wait_ge(S("sb_z_done"), h + 1)
                if h >= 1:
                    act.wait_ge(S("sb_arg"), h)
                z = sbw(0)
                scale = float(P) ** -0.5
                nc.scalar.activation(z, M[0][:, 0:384], ACT.Copy, scale=scale).then_inc(S("sb_zs"), 1)
                if h >= 1:
                    act.wait_ge(S("sb_l"), h)
                link(nc.scalar.activation(sbw(1), M[0][:, 0:384], ACT.Abs, scale=scale))
                link(nc.scalar.activation(sbw(1), sbw(1), ACT.Exp, scale=-1.0))
                nc.scalar.activation(sbw(1), sbw(1), ACT.Ln, bias=1.0).then_inc(S("sb_l1p"), 1)

            def sb_c(h):
                act.wait_ge(S("sb_arg"), h + 1)
                if h >= 1:
                    act.wait_ge(S("sb_o_done"), h)
                nc.scalar.activation(sbw(4), sbw(3), ACT.Exp).then_inc(S("sb_w"), 1)

            def sb_o(h):
                act.wait_ge(S("sb_o_done"), h + 1)
                nc.scalar.activation(ar(O_["sqq"] + h), M[2][:, 0:T].unsqueeze(1), ACT.Copy).then_inc(S("sb_y"), 1)

            def mix_pre():
                squares(3, x, S_["sq"], lambda e, q: e.wait_ge(S("x_update"), 2 * q + 2))
                upper(2)

            def shift_x():
                act.wait_ge(S("shift"), 1)
                nc.scalar.activation(xx[0:32, 0, :], xx[0:32, 0, :], ACT.Tanh).then_inc(S("lora_x"), 1)

            def lora_w():
                act.wait_ge(S("lora_w"), 1)
                for b in range(4):
                    nc.scalar.activation(flat(S_["sw"] + b, 1), M[2 + b // 2][:, (b % 2) * T:(b % 2 + 1) * T], ACT.Sigmoid, bias=vec("rwkv_w0_2", b)).then_inc(S("sw"), 1)

            def lora_a():
                act.wait_ge(S("lora_a"), 1)
                for b in range(4):
                    nc.scalar.activation(flat(S_["a"] + b, 1), M[b // 2][:, (b % 2) * T:(b % 2 + 1) * T], ACT.Sigmoid, bias=vec("rwkv_a0_2", b)).then_inc(S("iclr"), 1)

            def decays():
                act.wait_ge(S("cc"), 1)
                nc.scalar.activation(flat(S_["er"], 4), flat(S_["cc"], 4), ACT.Exp, scale=log_decay).then_inc(S("decays"), 1)
                nc.scalar.activation(flat(S_["sw"], 4), flat(S_["cc"], 4), ACT.Exp, scale=-log_decay).then_inc(S("decays"), 1)
                nc.scalar.activation(flat(S_["cs"], 4), flat(S_["cs"], 4), ACT.Exp, scale=log_decay).then_inc(S("decays"), 1)
                nc.scalar.activation(small[:, 16:20], small[:, 16:20], ACT.Exp, scale=log_decay).then_inc(S("decays"), 1)

            def key_sq():
                act.wait_ge(S("kk"), 1)
                nc.scalar.activation(flat(S_["rn"], 4), flat(S_["kk"], 4), ACT.Square).then_inc(S("kk_sq"), 1)

            def key_norms():
                act.wait_ge(S("kk"), 2)
                link(nc.scalar.activation(flat(S_["rn"], 4), flat(S_["rn"], 4), ACT.Ln))
                nc.scalar.activation(flat(S_["rn"], 4), flat(S_["rn"], 4), ACT.Exp, scale=-0.5).then_inc(S("kk_root"), 1)

            def turn_v():
                for c in range(2):
                    act.wait_ge(S("v_turned"), c + 1)
                    nc.scalar.activation(vt[:, c, :], M[2 + c][:, :], ACT.Copy).then_inc(S("vt"), 1)

            def turn_bk():
                for c in range(2):
                    act.wait_ge(S("bk_turned"), c + 1)
                    nc.scalar.activation((bt, kbt)[c], M[2 + c][:, :], ACT.Copy).then_inc(S("bkt"), 1)

            def solve_w(c):
                act.wait_ge(S("rw_w0"), c + 1)
                link(nc.scalar.activation(w0_all[:, 0:T], M[0][:, 0:T], ACT.Copy))
                nc.scalar.activation(w0_all[:, T:2 * T], M[1][:, 0:T], ACT.Copy).then_inc(S("w0"), 1)

            def solve_u(c):
                act.wait_ge(S("rw_u0"), c + 1)
                nc.scalar.activation(u_all, M[2][:, :], ACT.Copy).then_inc(S("u0"), 1)

            def solve_y(c):
                act.wait_ge(S("rw_y"), c + 1)
                act.wait_ge(S("roped"), 6)
                nc.scalar.activation(y_f[:, :, c * P:(c + 1) * P], M[3][:, :].rearrange("p (b t) -> p b t", b=4), ACT.Copy).then_inc(S("yr"), 1)

            def gn_var():
                act.wait_ge(S("gn_c"), 1)
                nc.scalar.activation(flat(S_["gsum"], 4), flat(S_["y"], 4), ACT.Square).then_inc(S("gn_sq"), 1)
                act.wait_ge(S("gn_ss"), 1)
                for q in range(2):
                    nc.scalar.activation(flat(S_["grs2"] + 2 * q, 2), M[q + 2][:, :], ACT.Ln, bias=gn_eps_col, scale=1.0 / HD).then_inc(S("gn_ln"), 1)
                act.wait_ge(S("gn_ln"), 2)
                nc.scalar.activation(flat(S_["grs2"], 4), flat(S_["grs2"], 4), ACT.Exp, scale=-0.5).then_inc(S("gn_rs"), 1)

            def gn_mean():
                nc.scalar.activation(xx[0:96, 1, :], xx[0:96, 1, :], ACT.Sigmoid).then_inc(S("gate_x"), 1)

            def at_s(n):
                act.wait_ge(S("at_max"), n + 1)
                nc.scalar.activation(sc(n), sc(n), ACT.Exp, bias=small[:, 20 + n:21 + n], accum_out=small[:, 28 + n:29 + n]).then_inc(S("at_exp"), 1)

            def at_t(n):
                act.wait_ge(S("at_turned"), n + 1)
                if n % 2 == 0:
                    nc.scalar.activation(pt(n)[:, 0:384], M[2][:, 0:384], ACT.Copy).then_inc(S("at_pt"), 2)
                else:
                    nc.scalar.activation(pt(n)[:, 0:512], M[2][:, :], ACT.Copy).then_inc(S("at_pt"), 1)
                    nc.scalar.activation(pt(n)[:, 512:768], M[3][:, 0:T], ACT.Copy).then_inc(S("at_pt"), 1)

            def at_o(n):
                h, i = n // 2, n % 2
                half = slice(HD * (h % 2), HD * (h % 2 + 1))
                act.wait_ge(S("at_o"), n + 1)
                nc.scalar.activation(oa[half, h // 2, i * P:(i + 1) * P], M[1][half, T:T + P], ACT.Copy).then_inc(S("at_oa"), 1)

            def mixed():
                act.wait_ge(S("rw_out"), 1)
                nc.scalar.activation(y_hi[:, 0:4, :], ar(S_["y"], 4), ACT.Copy).then_inc(S("mixed_hi"), 1)
                act.wait_ge(S("at_oa"), 2 * AT_H)
                nc.scalar.activation(y_hi[:, 4:6, :], oa, ACT.Copy).then_inc(S("mixed_hi"), 1)

            def mix_post():
                squares(4, ar(S_["o"], 8), S_["osq"], lambda e, q: evacuated(e, ("wo", q)))

            def ffn_pre():
                squares(5, x, S_["sq"], lambda e, q: e.wait_ge(S("x_update"), 8 + 2 * q + 2))
                upper(3)

            def ffn_post():
                squares(6, ar(S_["f"], 8), S_["sq"], lambda e, q: evacuated(e, ("fo1", q)))

            def turn_p():
                act.wait_ge(S("p_turned"), 1)
                nc.scalar.activation(flat(S_["p"], 2), M[1][:, :], ACT.Copy).then_inc(S("p_t"), 1)
                act.wait_ge(S("p_t"), 1)
                projected(act, ("fo1", 3))
                nc.scalar.activation(y_hi[:, 0:2, :], ar(S_["p"], 2), ACT.Copy).then_inc(S("p_hi"), 1)

            def ple_x():
                for k in range(KD):
                    act.wait_ge(S("x_update"), 16 + k + 1)
                    nc.scalar.activation(h_hi[:, k, :], x[:, k, :], ACT.Copy).then_inc(S("operand_hi"), 1)

            def ple_post():
                squares(7, ar(S_["e"], 8), S_["sq"], lambda e, q: e.wait_ge(S("ple"), q + 1))

            steps = dict(mix_pre=mix_pre, shift_x=shift_x, lora_w=lora_w, lora_a=lora_a, decays=decays, key_sq=key_sq, key_norms=key_norms, turn_v=turn_v, turn_bk=turn_bk, solve_w=solve_w, solve_u=solve_u, solve_y=solve_y,
                         gn_mean=gn_mean, gn_var=gn_var, at_s=at_s, at_t=at_t, at_o=at_o, mixed=mixed, mix_post=mix_post, ffn_pre=ffn_pre, ffn_post=ffn_post,
                         turn_p=turn_p, ple_x=ple_x, ple_post=ple_post, load_x=load_x, first_sum=first_sum, params=params, norm=norm, final_norm=final_norm, sgu_v=sgu_v, windows=windows, gla_z=gla_z, gla_decay=gla_decay, gla_kt=gla_kt, gla_o=gla_o, gla_n=gla_n, sb_z=sb_z, sb_c=sb_c, sb_o=sb_o)

            def evac(key):
                j = jobs[key]
                i, b = j["i"], bank_of(key)
                kind = j["kind"]
                if kind in ("copy", "copy_t", "copy16"):
                    projected(act, key)
                    if kind == "copy":
                        if key[0] == "ea":
                            act.wait_ge(S("pad_zero"), 3)
                            to = a_pad[:, 2 * i:2 * i + 2, PAD:]
                        else:
                            to = ar(dest[key[0]] + 2 * i, 2)
                        fr = b[:, :].rearrange("p (c t) -> p c t", c=2)
                    elif kind == "copy_t":
                        to = flat(dest[key[0]], 6 if key[0] == "av" else 8).rearrange("p (n d) -> p n d", n=2)[:, :, i * CB:(i + 1) * CB]
                        fr = b[:, :].rearrange("p (c t) -> p c t", c=2)
                    else:
                        to, fr = flat(O_["glr"], 1)[0:16, :], b[0:16, 0:T]
                    done_reading(nc.scalar.activation(to, fr, ACT.Copy), key)
                two = b[:, :].rearrange("p (c t) -> p c t", c=2)
                if kind in ("shifted", "wx"):
                    projected(act, key)
                    act.wait_ge(S("zpad"), 4)
                    z = zpad(key[0])
                    if kind == "wx":
                        link(nc.scalar.activation(z[0:64, 0, 1:], b[0:64, 0:T], ACT.Copy))
                        done_reading(nc.scalar.activation(z[0:96, 1, 1:], b[0:96, T:2 * T], ACT.Copy), key)
                    else:
                        done_reading(nc.scalar.activation(z[:, 2 * i:2 * i + 2, 1:], two, ACT.Copy), key)
                if kind == "rope":
                    projected(act, key)
                    n = ropes.index(key)
                    if n >= 1:
                        act.wait_ge(S("roped"), n)
                    sw_ = flat(S_["swap"], 2)
                    for g in range(4):
                        to_ = slice(32 * g, 32 * g + 32)
                        fr_ = slice(32 * (g ^ 1), 32 * (g ^ 1) + 32)
                        nc.scalar.activation(sw_[to_, :], b[fr_, :], ACT.Copy).then_inc(S("swapped"), 1)
                if kind == "sigmoid":
                    projected(act, key)
                    if key == ("wga", 0):
                        act.wait_ge(S("yr"), 2)
                    c = S_["gate"] + (0 if key[0] == "wga" else 8) + 2 * i
                    done_reading(nc.scalar.activation(ar(c, 2), two, ACT.Sigmoid), key)
                if kind == "up" and key[0] == "au":
                    act.wait_ge(S("merged"), i + 1)
                    nc.scalar.activation(y_hi[:, 8 + 2 * i:10 + 2 * i, :], ar(S_["m"] + 2 * i, 2), ACT.Copy).then_inc(S("merged_hi"), 1)
                if kind in ("out", "ffn0", "ple"):
                    projected(act, key)
                    done_reading(nc.scalar.activation(ar(S_[{"out": "o", "ffn0": "f", "ple": "e"}[kind]] + 2 * i, 2), two, ACT.Copy), key)
                if kind == "ple_gate":
                    projected(act, key)
                    if i >= 2:
                        act.wait_ge(S("ple"), i - 1)
                    done_reading(nc.scalar.activation(ar(S_["sg"] + 2 * (i % 2), 2), two, ACT.Sigmoid), key)
                if key == ("fi", 1):
                    act.wait_ge(S("operand_ready"), 32)
                    act.dma_start(ar(S_["p_in"], 2), ins["p_2"][0, 0].rearrange("(n p) d -> p n d", p=P)).then_inc(S("p_in"), 16)
                if kind in ("gate", "relu2"):
                    g = gates.index(key)
                    projected(act, key)
                    if g >= 2:
                        act.wait_ge(S("y_f"), g - 1)
                    done_reading(nc.scalar.activation(gate_tmp("sg", g), two, ACT.Silu if kind == "gate" else ACT.Relu), key)
                    act.wait_ge(S("y_f"), g + 1)
                    c = gate_mix[key[0]](i)[1] if kind == "gate" else 2 * (i % 8)
                    if key == ("fi", 8):
                        projected(act, ("fo0", 3))
                    nc.scalar.activation(y_hi[:, c:c + 2, :], gate_tmp("yt", g), ACT.Copy).then_inc(S("y_hi"), 1)

            act.wait_ge(S("scalars_set"), 3)
            run(steps, evac, split_to)
            for n, q in enumerate((0, 2, 1, 3)):
                act.wait_ge(S("out_ready"), n + 1)
                act.dma_start(out_t[:, q // 2, 512 * (q % 2):512 * (q % 2 + 1)], flat(2 * q, 2)).then_inc(S("stored"), 16)
            act.wait_ge(S("stored"), 64)

        @block.vector
        def _(dve):
            V = nc.vector
            link = chainer(dve, "dve_chain")
            next_split = [0]

            def modulation_part(u):
                n = units[u]["ada"][2]
                if n in ADA_PE:
                    return
                n -= sum(m < n for m in ADA_PE)
                unit_loaded(dve, u)
                if n == 0:
                    dve.wait_ge(S("silu_c"), 1)
                if n >= 2:
                    dve.wait_ge(S("ada_used"), ADA_DVE[n - 2] + 1)
                w, acc = raw[:, u % RAW, :].rearrange("p (k n) -> p k n", k=KD), ada_acc[n % 2]
                link(V.tensor_scalar(acc, w[:, 0, :], silu_c[:, 0:1], None, ALU.mult))
                for k in range(1, KD):
                    i_ = V.scalar_tensor_tensor(out=acc, in0=w[:, k, :], scalar=silu_c[:, k:k + 1], in1=acc, op0=ALU.mult, op1=ALU.add)
                    if k < KD - 1:
                        link(i_)
                i_.then_inc(S("ada_acc"), 1)

            def ada_to(u_end):
                while next_split[0] < u_end:
                    split_next()

            def split_to(end):
                u_end = split_units[min(end, len(split_units)) - 1]["order"] + 1
                while next_split[0] < u_end:
                    split_next()

            def split_next():
                u = next_split[0]
                next_split[0] += 1
                i, n = units[u]["index"], units[u]["nk"] * units[u]["n"]
                if units[u]["ada"] is not None:
                    modulation_part(u)
                elif i % 2:
                    dve.wait_ge(S("split_hi"), i + 1)
                    V.tensor_tensor(w_lo[:, i % SPL, 0:n], raw[:, u % RAW, 0:n], w_hi[:, i % SPL, 0:n].bitcast(F32), ALU.subtract).then_inc(S(f"split{i % SPL}"), 1)

            def lower(n, k):
                dve.wait_ge(S("operand_hi"), 8 * n + k + 1)
                V.tensor_tensor(h_lo[:, k, :], normed_at(n)[:, k, :], h_hi[:, k, :].bitcast(F32), ALU.subtract).then_inc(S("operand_ready"), 1)

            def inverse_root(stat):
                dve.wait_ge(S("rstd"), stat + 1)
                link(V.reciprocal(rstd[:, :], rstd[:, :]))

            scaled = [0]

            def apply_norm(stat, n, src, dst, gain, shift=None):
                inverse_root(stat)
                for k in range(KD + 3):
                    if k < KD:
                        V.scalar_tensor_tensor(out=dst[:, k, :], in0=src[:, k, :], scalar=gain(k), in1=rstd[:, :], op0=ALU.mult,
                                               op1=ALU.mult).then_inc(S("normed" if shift is None else "scaled"), 1)
                        scaled[0] += shift is not None
                    if shift is not None and 1 <= k <= KD:
                        dve.wait_ge(S("scaled"), scaled[0] - (k < KD))
                        V.tensor_scalar(dst[:, k - 1, :], dst[:, k - 1, :], shift(k - 1), None, ALU.add).then_inc(S("normed"), 1)
                    if k >= 3:
                        lower(n, k - 3)

            def modulation(layer):
                return V.scalar_tensor_tensor(out=mod[:, layer, :], in0=ada_c[:, layer, 8:16], scalar=1.0,
                                              in1=vec("norm_g", 8 * layer, 8), op0=ALU.add, op1=ALU.mult)

            def ada_first():
                dve.wait_ge(S("params"), 1)
                dve.wait_ge(S("ada_used"), 8)
                V.tensor_tensor(ada_c[:, 0, 0:16], M[3][:, 0:16], vec("ada_b", 0, 16), ALU.add).then_inc(S("ada_read"), 1)
                dve.wait_ge(S("ada_read"), 1)
                link(modulation(0))

            def ada_rest():
                dve.wait_ge(S("ada_used"), 20)
                V.tensor_tensor(ada_c[:, :, :].rearrange("p l c -> p (l c)")[:, 16:40], M[3][:, 16:40], vec("ada_b", 16, 24), ALU.add).then_inc(S("ada_read"), 1)
                dve.wait_ge(S("ada_read"), 2)
                link(modulation(1))

            def ada_last():
                dve.wait_ge(S("ada_used"), 24)
                V.tensor_tensor(ada_c[:, 1, 16:24], M[3][:, 40:48], vec("ada_b", 40, 8), ALU.add).then_inc(S("ada_read"), 1)
                dve.wait_ge(S("ada_read"), 3)

            def first_scale():
                dve.wait_ge(S("rstd"), 1)
                V.reciprocal(rstd[:, :], rstd[:, :]).then_inc(S("rstd_inv"), 1)

            def norm(n):
                if n == 0:
                    dve.wait_ge(S("x_scaled"), 1)
                    h0 = normed_at(0)
                    for k in range(KD + 3):
                        if k < KD:
                            V.tensor_scalar(h0[:, k, :], h0[:, k, :], mod[:, 0, k:k + 1], ada_c[:, 0, k:k + 1], ALU.mult, ALU.add).then_inc(S("normed"), 1)
                        if k >= 3:
                            lower(0, k - 3)
                    return
                apply_norm(n, n, x[:, :, :], normed_at(n), lambda k: mod[:, n, k:k + 1], lambda k: ada_c[:, n, k:k + 1])

            def final_norm():
                projected(dve, ("oo", 3))
                for name in ("wr", "wk", "wv", "wx"):
                    V.memset(zpad(name)[:, :, 0:1], 0.0).then_inc(S("zpad"), 1)
                inverse_root(2)
                for k in range(KD):
                    V.scalar_tensor_tensor(out=x[:, k, :], in0=x[:, k, :], scalar=vec("final_g", k), in1=rstd[:, :], op0=ALU.mult, op1=ALU.mult).then_inc(S("x_update"), 1)
                dve.wait_ge(S("x_update"), 8)

            def sgu_w():
                dve.wait_ge(S("const_in"), 16)
                for b in range(2):
                    dve.wait_ge(S("sgu_w_turned"), b + 1)
                    V.tensor_tensor(w_t[:, 4 * b:4 * b + 4, :], M[1 + b][:, :].rearrange("p (h t) -> p h t", h=4), bc(K("upto"), 4), ALU.mult).then_inc(S("sgu_w"), 1)

            def sgu_v():
                dve.wait_ge(S("v_rstd"), 1)
                for tt in range(2):
                    V.tensor_scalar(v_tok[:, tt, :], v_tok[:, tt, :], small[:, 4 + tt:5 + tt], None, ALU.mult).then_inc(S("v_normed"), 1)

            def windows(part):
                if part == 0:
                    dve.wait_ge(S("pad_zero"), 3)
                    for i in range(4):
                        evacuated(dve, ("ea", i))
                for g, wd in ((0, 2),) if part == 0 else tuple(enumerate(WINDOWS))[1:] if part == 1 else ():
                    src, to = (lev[1 - g % 2] if g else a_pad), lev[g % 2]
                    sh = wd // 2
                    if g == 0:
                        link(V.tensor_tensor(to[:, 0:8, sh:], src[:, 0:8, sh:], src[:, 0:8, 0:-sh], ALU.add))
                    else:
                        link(V.tensor_tensor(to[:, 2 * g:8, PAD:], src[:, 2 * g:8, PAD:], src[:, 2 * g:8, PAD - sh:-sh], ALU.add))
                if part == 2:
                    dve.wait_ge(S("inv_in"), 16)
                inv = K("inv_count").rearrange("p (g t) -> p g t", g=4)
                for g in range(4 if part == 2 else 0):
                    link(V.tensor_tensor(lev[0][:, 2 * g:2 * g + 2, PAD:], lev[g % 2][:, 2 * g:2 * g + 2, PAD:], bc(inv[:, g, :], 2), ALU.mult))
                if part < 3:
                    return
                V.tensor_tensor(lev[0][:, :, PAD:], lev[0][:, :, PAD:], a_pad[:, :, PAD:], ALU.subtract).then_inc(S("p"), 1)
                dve.wait_ge(S("p_hi"), 1)
                V.tensor_tensor(y_lo[:, 0:8, :], lev[0][:, :, PAD:], y_hi[:, 0:8, :].bitcast(F32), ALU.subtract).then_inc(S("p_lo"), 1)

            def sgu_z(i):
                evacuated(dve, ("eu", i))
                dve.wait_ge(S("sgu_in"), 32)
                dve.wait_ge(S("sgu_z"), i + 1)
                for h in (2 * i, 2 * i + 1):
                    z = M[i % 3][:, (h % 2) * T:(h % 2 + 1) * T].rearrange("p (n t) -> p n t", n=2)
                    t = flat(E_["z"], 1)
                    link(V.scalar_tensor_tensor(out=t.rearrange("p (n t) -> p n t", n=2), in0=z, scalar=vec("sgu_norm_g", h),
                                                in1=bc(b_all[:, h, :], 2), op0=ALU.mult, op1=ALU.add))
                    u = flat(E_["u"] + h, 1)
                    V.tensor_tensor(u, u, t, ALU.mult).then_inc(S("sgu_y"), 1)
                    dve.wait_ge(S("sgu_y"), h + 1)

            def gla_z():
                dve.wait_ge(S("gla_l1p"), 1)
                dve.wait_ge(S("odd_const_in"), 16)
                link(V.scalar_tensor_tensor(out=flat(O_["t1"], 4), in0=flat(O_["la"], 4), scalar=0.0, in1=flat(O_["t1"], 4), op0=ALU.min, op1=ALU.subtract))
                for h in range(GLA_H):
                    V.tensor_tensor_scan(flat(O_["la"] + h, 1), K("gla_run"), flat(O_["t1"] + h, 1), 0.0, ALU.mult, ALU.add).then_inc(S("gla_cum_h"), 1)
                dve.wait_ge(S("gla_cum_h"), 4)
                V.tensor_copy(small[:, 10:11], small_zero).then_inc(S("gla_cum"), 1)
                V.tensor_copy(small[:, 11:12], small_zero).then_inc(S("gla_t1_free"), 1)

            def gla_decay():
                for i in range(2):
                    evacuated(dve, ("gq", i))
                    evacuated(dve, ("gk", i))
                dve.wait_ge(S("gla_exp"), 1)
                link(V.scalar_tensor_tensor(out=flat(O_["q"], 4), in0=flat(O_["q"], 4), scalar=float(P) ** -0.5, in1=flat(O_["e"], 4), op0=ALU.mult, op1=ALU.mult))
                dve.wait_ge(S("gla_exp"), 2)
                link(V.tensor_tensor(flat(O_["ki"], 4), flat(O_["k"], 4), flat(O_["t1"], 4), ALU.mult))
                la = flat(O_["la"], 4).rearrange("p (c t) -> p c t", t=GLA_C)
                V.tensor_tensor(flat(O_["t1"], 4).rearrange("p (c t) -> p c t", t=GLA_C), la[:, :, GLA_C - 1:GLA_C].broadcast_to([P, 16, GLA_C]), la, ALU.subtract).then_inc(S("gla_rest"), 1)
                dve.wait_ge(S("gla_exp"), 3)
                V.tensor_tensor(flat(O_["k"], 4), flat(O_["k"], 4), flat(O_["t1"], 4), ALU.mult).then_inc(S("gla_kend"), 1)
                dve.wait_ge(S("gla_kend"), 1)
                link(V.memset(flat(O_["att"], 2), 0.0))

            def gla_att(h):
                dve.wait_ge(S("gla_att"), h + 1)
                if h >= 2:
                    dve.wait_ge(S("gla_o_done"), h - 1)
                link(V.copy_predicated(gatt(h), K("gla_mask").bitcast(U32), M[0][:, 0:T]))
                e = flat(O_["e"], 4).rearrange("p (h t) -> p h t", h=GLA_H)
                us = [M[1][:, 0:T], M[0][:, T:2 * T], M[1][:, T:2 * T]]
                link(V.tensor_copy(gst(h, 0), us[0]))
                for c in (1, 2):
                    ins_ = V.scalar_tensor_tensor(out=gst(h, c), in0=gst(h, c - 1), scalar=e[:, h, GLA_C * (c + 1) - 1:GLA_C * (c + 1)], in1=us[c], op0=ALU.mult, op1=ALU.add)
                    if c == 1:
                        link(ins_)
                ins_.then_inc(S("gla_states"), 1)

            def gla_n(h):
                dve.wait_ge(S("gla_rs"), h + 1)
                dve.wait_ge(S("gla_o"), h + 1)
                for vh in range(2):
                    o = GO(h)[:, vh, :]
                    ins_ = V.scalar_tensor_tensor(out=o, in0=o, scalar=vec("gla_norm_g", 2 * h + vh), in1=flat(O_["rs"], 1), op0=ALU.mult, op1=ALU.mult)
                    if vh == 0:
                        link(ins_)
                ins_.then_inc(S("gla_yc"), 1)

            def sb_z(h):
                dve.wait_ge(S("sb_l1p"), h + 1)
                dve.wait_ge(S("sb_zs"), h + 1)
                if h >= 1:
                    dve.wait_ge(S("sb_c_done"), h)
                link(V.scalar_tensor_tensor(out=sbw(2), in0=sbw(0), scalar=0.0, in1=sbw(1), op0=ALU.max, op1=ALU.add))
                V.tensor_tensor(sbw(2), sbw(2), K("sb_mask"), ALU.mult).then_inc(S("sb_l"), 1)
                if h >= 1:
                    dve.wait_ge(S("sb_w"), h)
                link(V.tensor_tensor(sbw(3), sbw(0), K("sb_neg"), ALU.add))

            def add_normed(stat, src, gain):
                inverse_root(stat)
                for k in range(KD + 1):
                    if k < KD:
                        V.scalar_tensor_tensor(out=src[:, k, :], in0=src[:, k, :], scalar=vec(gain, k), in1=rstd[:, :], op0=ALU.mult, op1=ALU.mult).then_inc(S("scaled"), 1)
                        scaled[0] += 1
                    if k >= 1:
                        dve.wait_ge(S("scaled"), scaled[0] - (k < KD))
                        V.tensor_tensor(x[:, k - 1, :], x[:, k - 1, :], src[:, k - 1, :], ALU.add).then_inc(S("x_update"), 1)

            def mix_pre():
                apply_norm(3, 2, x[:, :, :], normed_at(2), lambda k: vec("mix_pre_norm_2", k))

            def token_shift(names):
                for name in names:
                    _, to, n, mu = shifted[name]
                    for i in range(2 if n == 4 else 1):
                        evacuated(dve, (name, i))
                    z = zpad(name)
                    to = flat(to, n).rearrange("p (b t) -> p b t", b=n)
                    if name == "wx":
                        for b, rows_ in ((0, 64), (1, 96)):
                            link(V.tensor_tensor(to[0:rows_, b, :], z[0:rows_, b, 0:T], z[0:rows_, b, 1:], ALU.subtract))
                            link(V.scalar_tensor_tensor(out=to[0:rows_, b, :], in0=to[0:rows_, b, :], scalar=vec("rwkv_mu_2", mu + b)[0:rows_], in1=z[0:rows_, b, 1:], op0=ALU.mult, op1=ALU.add))
                        continue
                    link(V.tensor_tensor(to, z[:, :, 0:T], z[:, :, 1:], ALU.subtract))
                    for b in range(4):
                        link(V.scalar_tensor_tensor(out=to[:, b, :], in0=to[:, b, :], scalar=vec("rwkv_mu_2", mu + b), in1=z[:, b, 1:], op0=ALU.mult, op1=ALU.add))
                V.tensor_copy(small[:, 9:10], small_zero).then_inc(S("shift"), 1)
                dve.wait_ge(S("shift"), {"wx": 1, "wk": 2, "wv": 3, "wr": 4}[names[0]])

            def shift_x():
                token_shift(("wx",))

            def shift_k():
                token_shift(("wk",))

            def shift_r():
                token_shift(("wr",))

            def shift_v():
                token_shift(("wv",))

            def decays():
                dve.wait_ge(S("late_in"), 64)
                dve.wait_ge(S("sw"), 4)
                for b in range(4):
                    link(V.tensor_tensor_scan(flat(S_["cs"] + b, 1), K("rw_run"), flat(S_["sw"] + b, 1), 0.0, ALU.mult, ALU.add))
                cs = flat(S_["cs"], 4).rearrange("p (b t) -> p b t", t=RW_C)
                mid = cs[:, :, RW_C // 2 - 1:RW_C // 2]
                link(V.tensor_copy(small[:, 16:20].unsqueeze(2), mid[:, 1:8:2, :]))
                link(V.tensor_tensor(flat(S_["cc"], 4).rearrange("p (b t) -> p b t", t=RW_C), cs, mid.broadcast_to([P, 8, RW_C]), ALU.subtract))
                V.tensor_tensor(flat(S_["cs"], 4), flat(S_["cc"], 4), flat(S_["sw"], 4), ALU.subtract).then_inc(S("cc"), 1)

            k4, kk4, rn4 = flat(S_["k"], 4), flat(S_["kk"], 4), flat(S_["rn"], 4)

            def key_sq():
                for b in range(4):
                    i_ = V.tensor_scalar(kk4[:, b * T:(b + 1) * T], k4[:, b * T:(b + 1) * T], vec("rwkv_k_k_2", b), None, ALU.mult)
                    if b < 3:
                        link(i_)
                i_.then_inc(S("kk"), 1)
                dve.wait_ge(S("kk"), 1)

            def key_norms():
                dve.wait_ge(S("kk_ss"), 1)
                for q in range(2):
                    i_ = V.tensor_scalar(rn4[:, 512 * q:512 * (q + 1)], M[2 + q][:, :], 1e-24, None, ALU.max)
                    if q == 0:
                        link(i_)
                i_.then_inc(S("kk"), 1)

            a4 = flat(S_["a"], 4)

            def key_unit():
                dve.wait_ge(S("kk_root"), 1)
                link(V.tensor_tensor(kk4, kk4, rn4, ALU.mult))
                dve.wait_ge(S("iclr"), 4)
                kt4 = flat(S_["kt"], 4)
                for b in range(4):
                    link(V.tensor_scalar(kt4[:, b * T:(b + 1) * T], a4[:, b * T:(b + 1) * T], -1.0, vec("rwkv_k_a_2", b), ALU.add, ALU.mult))
                link(V.scalar_tensor_tensor(out=k4, in0=kt4, scalar=1.0, in1=k4, op0=ALU.add, op1=ALU.mult))
                for b in range(4):
                    i_ = V.scalar_tensor_tensor(out=flat(S_["rk"] + b, 1), in0=r_f[:, b, :], scalar=vec("rwkv_r_k_2", b), in1=k_f[:, b, :], op0=ALU.mult, op1=ALU.mult)
                    if b < 3:
                        link(i_)
                i_.then_inc(S("rk"), 1)

            def rw_inputs():
                dve.wait_ge(S("decays"), 4)
                ea = flat(S_["cs"], 4).rearrange("p (b c t) -> p b c t", b=4, c=2)
                er = flat(S_["er"], 4).rearrange("p (b c t) -> p b c t", b=4, c=2)
                ei = flat(S_["sw"], 4)
                for c in range(2):
                    link(V.scalar_tensor_tensor(out=ar_[:, :, c, 0, :], in0=kk4.rearrange("p (b c t) -> p b c t", b=4, c=2)[:, :, c, :], scalar=-1.0,
                                                in1=ea[:, :, c, :], op0=ALU.mult, op1=ALU.mult))
                    link(V.tensor_tensor(ar_[:, :, c, 1, :], r_f[:, :, c * P:(c + 1) * P], er[:, :, c, :], ALU.mult))
                link(V.tensor_tensor(flat(S_["b"], 4), kk4, a4, ALU.mult))
                link(V.tensor_tensor(flat(S_["b"], 4), flat(S_["b"], 4), ei, ALU.mult))
                link(V.tensor_tensor(flat(S_["kb"], 4), k4, ei, ALU.mult))
                V.tensor_copy(small[:, 12:16].unsqueeze(2), er[:, :, 0, P - 1:P]).then_inc(S("rw_operands"), 1)
                dve.wait_ge(S("rw_operands"), 1)

            def bonus():
                for q in range(2):
                    dve.wait_ge(S("bonus_sum"), q + 1)
                    i_ = V.tensor_tensor(flat(S_["bonus"] + 2 * q, 2), M[q][:, :], flat(S_["v"] + 2 * q, 2), ALU.mult)
                    if q == 0:
                        link(i_)
                i_.then_inc(S("bonus"), 1)
                dve.wait_ge(S("bonus"), 1)

            def rw_pairs(n):
                mask = cst[:, CONST_PLACES[0][0]["before"][0]:CONST_PLACES[0][0]["before"][0] + 2 * P]
                nm_b, nm_k = rset(n % 2)[0:2]
                dve.wait_ge(S("rw_pairs"), 2 * n + 1)
                if n == 0:
                    dve.wait_ge(S("vt"), 2)
                for k in range(4):
                    i_ = V.tensor_tensor((nm_b, nm_k)[k // 2][:, 2 * (k % 2):2 * (k % 2) + 2, :], M[k][:, :].rearrange("p (j w) -> p j w", j=2), bc(mask, 2), ALU.mult)
                    i_.then_inc(S("rw_masked"), 1)

            def rw_pair_t(n):
                nm_b, _, t_, tt_, _ = rset(n % 2)
                dve.wait_ge(S("rw_masked"), 4 * n + 4)
                link(V.tensor_tensor(tt_, nm_b[:, :, 0:P], bc(K("pair1_t"), 4), ALU.mult))
                link(V.tensor_tensor(tt_, tt_, bc(K("ident"), 4), ALU.add))
                dve.wait_ge(S("rw_pairs"), 2 * n + 2)
                for k in range(2):
                    link(V.tensor_tensor(t_[:, 2 * k:2 * k + 2, :], M[k][:, 0:T].rearrange("p (j w) -> p j w", j=2), bc(K("pair1"), 2), ALU.mult))
                V.tensor_tensor(t_, t_, bc(K("ident"), 4), ALU.add).then_inc(S("rw_t0"), 1)
                dve.wait_ge(S("rw_t0"), n + 1)

            def rw_u(m):
                for s_ in range(2):
                    dve.wait_ge(S("rw_u"), 2 * m + s_ + 1)
                    um = rset(s_)[4]
                    V.tensor_tensor(um, M[s_][:, :].rearrange("p (q w) -> p q w", q=4), bc(K(f"pair{2 ** (m % 6 + 1)}"), 4), ALU.mult).then_inc(S("rw_um"), 1)

            def rw_t(m):
                for s_ in range(2):
                    dve.wait_ge(S("rw_t"), 2 * m + s_ + 1)
                    _, _, t_, tt_, _ = rset(s_)
                    if m % 6 < 5:
                        link(V.tensor_tensor(t_, t_, M[s_][:, :].rearrange("p (q w) -> p q w", q=4), ALU.add))
                    V.tensor_tensor(tt_, tt_, M[2 + s_][:, :].rearrange("p (q w) -> p q w", q=4), ALU.add).then_inc(S("rw_new"), 1)
                    dve.wait_ge(S("rw_new"), 2 * m + s_ + 1)

            def solve_y(c):
                if c == 0:
                    dve.wait_ge(S("rw_s"), 1)
                    for b in range(4):
                        i_ = V.tensor_scalar(s0[:, b, :], M[0][:, b * HD:(b + 1) * HD], small[:, 12 + b:13 + b], small[:, 16 + b:17 + b], ALU.mult, ALU.mult)
                        i_.then_inc(S("s0"), 1)

            def gn_mean():
                for q in range(2):
                    dve.wait_ge(S("gn_sum"), q + 1)
                    y2 = flat(S_["y"] + 2 * q, 2)
                    i_ = V.scalar_tensor_tensor(out=y2, in0=M[q][:, :], scalar=-1.0 / HD, in1=y2, op0=ALU.mult, op1=ALU.add)
                    if q == 0:
                        link(i_)
                i_.then_inc(S("gn_c"), 1)
                dve.wait_ge(S("gn_c"), 1)

            def gn_var():
                dve.wait_ge(S("gn_rs"), 1)
                link(V.tensor_tensor(flat(S_["y"], 4), flat(S_["y"], 4), flat(S_["grs2"], 4), ALU.mult))
                for b in range(4):
                    link(V.tensor_scalar(y_f[:, b, :], y_f[:, b, :], vec("rwkv_ln_w_2", b), vec("rwkv_ln_b_2", b), ALU.mult, ALU.add))
                link(V.tensor_tensor(flat(S_["y"], 4), flat(S_["y"], 4), flat(S_["bonus"], 4), ALU.add))

            def rw_gate():
                for q in range(2):
                    dve.wait_ge(S("rw_g"), q + 1)
                    y2 = flat(S_["y"] + 2 * q, 2)
                    i_ = V.tensor_tensor(y2, y2, M[2 + q][:, :], ALU.mult)
                    if q == 0:
                        link(i_)
                i_.then_inc(S("rw_out"), 1)
                dve.wait_ge(S("rw_out"), 1)

            def at_s(n):
                i = n % 2
                if n >= 2:
                    dve.wait_ge(S("at_turned"), n - 1)
                dve.wait_ge(S("at_s"), n + 1)
                neg = K(f"at_neg{i}")
                parts = ((0, 384, 0),) if i == 0 else ((0, 512, 0), (512, 768, 1))
                for a_, b_, bank in parts:
                    link(V.scalar_tensor_tensor(out=sc(n)[:, a_:b_], in0=M[bank][:, 0:b_ - a_], scalar=float(HD) ** -0.5, in1=neg[:, a_:b_], op0=ALU.mult, op1=ALU.add))
                V.tensor_reduce(small[:, 20 + n:21 + n], sc(n), AX.X, ALU.max, negate=True).then_inc(S("at_max"), 1)
                dve.wait_ge(S("at_exp"), n + 1)
                link(V.reciprocal(small[:, 28 + n:29 + n], small[:, 28 + n:29 + n]))
                V.tensor_scalar(sc(n), sc(n), small[:, 28 + n:29 + n], None, ALU.mult).then_inc(S("at_p"), 1)

            def mixed():
                dve.wait_ge(S("mixed_hi"), 1)
                V.tensor_tensor(y_lo[:, 0:4, :], ar(S_["y"], 4), y_hi[:, 0:4, :].bitcast(F32), ALU.subtract).then_inc(S("mixed_lo"), 1)
                dve.wait_ge(S("mixed_hi"), 2)
                V.tensor_tensor(y_lo[:, 4:6, :], oa, y_hi[:, 4:6, :].bitcast(F32), ALU.subtract).then_inc(S("mixed_lo"), 1)

            def mix_post():
                add_normed(4, ar(S_["o"], 8), "mix_post_norm_2")

            def ffn_pre():
                for k in range(KD):
                    dve.wait_ge(S("x_update"), 8 + k + 1)
                apply_norm(5, 3, x[:, :, :], normed_at(3), lambda k: vec("ffn_pre_norm_2", k))

            def ffn_post():
                add_normed(6, ar(S_["f"], 8), "ffn_post_norm_2")

            def turn_p():
                dve.wait_ge(S("p_hi"), 2)
                V.tensor_tensor(y_lo[:, 0:2, :], ar(S_["p"], 2), y_hi[:, 0:2, :].bitcast(F32), ALU.subtract).then_inc(S("p_lo"), 1)

            def ple_x():
                for k in range(KD):
                    dve.wait_ge(S("operand_hi"), 32 + k + 1)
                    V.tensor_tensor(h_lo[:, k, :], x[:, k, :], h_hi[:, k, :].bitcast(F32), ALU.subtract).then_inc(S("operand_ready"), 1)

            def ple_post():
                add_normed(7, ar(S_["e"], 8), "ple_post_norm_2")

            def sb_c(h):
                dve.wait_ge(S("sb_c_done"), h + 1)
                V.scalar_tensor_tensor(out=sbw(3), in0=M[1][:, 0:384], scalar=-1.0, in1=sbw(3), op0=ALU.mult, op1=ALU.add).then_inc(S("sb_arg"), 1)

            steps = dict(mix_pre=mix_pre, shift_x=shift_x, shift_k=shift_k, shift_r=shift_r, shift_v=shift_v, decays=decays, key_sq=key_sq, key_norms=key_norms, key_unit=key_unit, rw_inputs=rw_inputs, bonus=bonus,
                         rw_pairs=rw_pairs, rw_pair_t=rw_pair_t, rw_u=rw_u, rw_t=rw_t, solve_y=solve_y, gn_mean=gn_mean, gn_var=gn_var, rw_gate=rw_gate,
                         at_s=at_s, mixed=mixed, mix_post=mix_post, ffn_pre=ffn_pre, ffn_post=ffn_post, turn_p=turn_p, ple_x=ple_x,
                         ple_post=ple_post, ada_first=ada_first, ada_rest=ada_rest, ada_last=ada_last, first_scale=first_scale, norm=norm, final_norm=final_norm, sgu_w=sgu_w, sgu_v=sgu_v, windows=windows, sgu_z=sgu_z, gla_z=gla_z, gla_decay=gla_decay, gla_att=gla_att, gla_n=gla_n, sb_z=sb_z, sb_c=sb_c)

            def evac(key):
                j = jobs[key]
                i, b = j["i"], bank_of(key)
                kind = j["kind"]
                if kind == "rope":
                    n = ropes.index(key)
                    dve.wait_ge(S("swapped"), 4 * n + 4)
                    to = ar(S_["q" if key[0] == "aq" else "ak"] + 2 * i, 2)
                    sw_ = ar(S_["swap"], 2)
                    done_reading(V.tensor_tensor(to, b[:, :].rearrange("p (c t) -> p c t", c=2), bc(K("cos"), 2), ALU.mult), key)
                    link(V.tensor_tensor(sw_, sw_, bc(K("sin"), 2), ALU.mult))
                    evacuated(dve, key)
                    V.tensor_tensor(to, to, sw_, ALU.add).then_inc(S("roped"), 1)
                if kind == "up":
                    projected(dve, key)
                    two = b[:, :].rearrange("p (c t) -> p c t", c=2)
                    ga, gr = ar(S_["gate"] + 2 * i, 2), ar(S_["gate"] + 8 + 2 * i, 2)
                    mm = ar(S_["m"] + 2 * i, 2)
                    if key[0] == "ru":
                        evacuated(dve, ("wgb", i))
                        done_reading(V.tensor_tensor(mm, two, gr, ALU.mult), key)
                    else:
                        done_reading(V.tensor_tensor(ga, two, ga, ALU.mult), key)
                        evacuated(dve, key)
                        evacuated(dve, ("ru", i))
                        V.tensor_tensor(mm, mm, ga, ALU.add).then_inc(S("merged"), 1)
                        dve.wait_ge(S("merged_hi"), i + 1)
                        V.tensor_tensor(y_lo[:, 8 + 2 * i:10 + 2 * i, :], mm, y_hi[:, 8 + 2 * i:10 + 2 * i, :].bitcast(F32), ALU.subtract).then_inc(S("merged_lo"), 1)
                if kind == "ffn1":
                    projected(dve, key)
                    f_ = ar(S_["f"] + 2 * i, 2)
                    evacuated(dve, ("fo0", i))
                    done_reading(V.tensor_tensor(f_, b[:, :].rearrange("p (c t) -> p c t", c=2), f_, ALU.add), key)
                if kind == "ple_gate":
                    evacuated(dve, key)
                    e_ = ar(S_["e"] + 2 * i, 2)
                    V.tensor_tensor(e_, e_, ar(S_["sg"] + 2 * (i % 2), 2), ALU.mult).then_inc(S("ple"), 1)
                if kind == "relu2":
                    g = gates.index(key)
                    evacuated(dve, key)
                    c = 2 * (i % 8)
                    if g >= 2:
                        dve.wait_ge(S("y_lo"), g - 1)
                    V.tensor_tensor(gate_tmp("yt", g), gate_tmp("sg", g), gate_tmp("sg", g), ALU.mult).then_inc(S("y_f"), 1)
                    dve.wait_ge(S("y_hi"), g + 1)
                    V.tensor_tensor(y_lo[:, c:c + 2, :], gate_tmp("yt", g), y_hi[:, c:c + 2, :].bitcast(F32), ALU.subtract).then_inc(S("y_lo"), 1)
                if kind == "gate":
                    g = gates.index(key)
                    evacuated(dve, key)
                    mix, c = gate_mix[key[0]](i)
                    if key[0] == "ega":
                        evacuated(dve, ("pool", i))
                    if key[0] == "gga":
                        dve.wait_ge(S("gla_yc"), i + 1)
                    if key[0] == "ggb":
                        dve.wait_ge(S("sb_y"), 2 * i + 2)
                    if g >= 2:
                        dve.wait_ge(S("y_lo"), g - 1)
                    V.tensor_tensor(gate_tmp("yt", g), gate_tmp("sg", g), mix, ALU.mult).then_inc(S("y_f"), 1)
                    dve.wait_ge(S("y_hi"), g + 1)
                    V.tensor_tensor(y_lo[:, c:c + 2, :], gate_tmp("yt", g), y_hi[:, c:c + 2, :].bitcast(F32), ALU.subtract).then_inc(S("y_lo"), 1)
                if kind == "pool":
                    projected(dve, key)
                    for fb in range(2):
                        ins_ = V.tensor_scalar(a_pad[:, 2 * i + fb, PAD:], b[:, fb * T:(fb + 1) * T], vec("pool_scale", 2 * i + fb), None, ALU.mult)
                        if fb == 0:
                            link(ins_)
                    done_reading(ins_, key)
                if kind == "residual":
                    projected(dve, key)
                    layer = 0 if key[0] == "eo" else 1
                    for fb in range(2):
                        xc = x[:, 2 * i + fb, :]
                        ins_ = V.scalar_tensor_tensor(out=xc, in0=b[:, fb * T:(fb + 1) * T], scalar=ada_c[:, layer, 16 + 2 * i + fb:17 + 2 * i + fb],
                                                      in1=xc, op0=ALU.mult, op1=ALU.add)
                        if fb == 0:
                            link(ins_)
                    done_reading(ins_, key)

            dve.wait_ge(S("scalars_set"), 3)
            run(steps, evac, split_to, lambda u: ada_to(u + 1))
            for n, q in enumerate((0, 2, 1, 3)):
                dve.wait_ge(S("out_turned"), n + 1)
                V.tensor_copy(ar(2 * q, 2), M[q][:, :].rearrange("p (c t) -> p c t", c=2)).then_inc(S("out_ready"), 1)

        @block.tensor
        def _(pe):
            def turn(to, src):
                n = src.shape[0]
                return nc.tensor.transpose(to, src, K("ident")[0:n, 0:n])

            def sum_squares(n, sq):
                for k in range(KD):
                    if k % 2 == 0:
                        pe.wait_ge(S("squares"), 4 * n + k // 2 + 1)
                    m = nc.tensor.matmul(M[0][:, 0:T], K("ones"), ar(sq + k)[:, 0, :], start=(k == 0), stop=(k == KD - 1))
                m.then_inc(S("sum_sq"), 1)

            def load_x():
                pe.wait_ge(S("const_in"), 16)
                pe.wait_ge(S("c_in"), 16)
                turn(PJ[0][:, 0:KD], c_rows).then_inc(S("c_turned"), 1)
                pe.wait_ge(S("x_in"), 16)
                xt = ar(0, 8).rearrange("p (n c) t -> p n (c t)", n=2)
                for q in range(4):
                    for c in range(2):
                        for tt in range(2):
                            m = turn(M[q][:, c * T + tt * P:c * T + (tt + 1) * P], xt[:, tt, (2 * q + c) * P:(2 * q + c + 1) * P])
                    m.then_inc(S("x_turned"), 1)

            def params():
                pe.wait_ge(S("rows_loaded"), 16 * N_ROW_LOADS)
                turn(PJ[1][:, 0:P], rows[:, 0, :])
                turn(PJ[1][:, P:2 * P], rows[:, 1, :]).then_inc(S("params_turned"), 1)

            def first_sum():
                sum_squares(0, E_["sq"])

            def norm(n):
                if n == 1:
                    sum_squares(1, O_["sq"])

            def final_norm():
                sum_squares(2, O_["sq"])

            def sgu_w():
                pe.wait_ge(S("sgu_in"), 32)
                for b in range(2):
                    for h in range(4):
                        m = turn(M[1 + b][:, h * P:(h + 1) * P], w_raw[:, 4 * b + h, :])
                    m.then_inc(S("sgu_w_turned"), 1)

            def sgu_z(i):
                pe.wait_ge(S("v_normed"), 2)
                pe.wait_ge(S("sgu_w"), 2)
                if i == 3:
                    pe.wait_ge(S("sgu_y"), 2)
                for h in (2 * i, 2 * i + 1):
                    for n in range(2):
                        m = nc.tensor.matmul(M[i % 3][:, (h % 2) * T + n * P:(h % 2) * T + (n + 1) * P], v_tok[:, n, h * P:(h + 1) * P], w_t[:, h, :], start=True, stop=True)
                m.then_inc(S("sgu_z"), 1)

            def gla_z():
                pe.wait_ge(S("gate_w_in"), 16)
                evacuated(pe, ("glr", 0))
                for h in range(GLA_H):
                    m = nc.tensor.matmul(M[h // 2][:, (h % 2) * T:(h % 2 + 1) * T], gate_w[:, h * P:(h + 1) * P], flat(O_["glr"], 1)[0:16, :], start=True, stop=True)
                    if h % 2:
                        m.then_inc(S("gla_z"), 1)

            def gla_kt():
                pe.wait_ge(S("gla_kend"), 1)
                for b in range(2):
                    for i in range(4):
                        h, n = 2 * b + i // 2, i % 2
                        m = turn(M[b][:, i * P:(i + 1) * P], flat(O_["k"] + h, 1)[:, n * P:(n + 1) * P])
                    m.then_inc(S("gla_kt_turned"), 1)

            def gla_att(h):
                if h == 0:
                    pe.wait_ge(S("gla_kt"), 2)
                evacuated(pe, ("gv", h))
                if h >= 1:
                    pe.wait_ge(S("gla_states"), h)
                q, ki = flat(O_["q"] + h, 1), flat(O_["ki"] + h, 1)
                for n in range(2):
                    nc.tensor.matmul(M[0][:, n * P:(n + 1) * P], ki[:, n * P:(n + 1) * P], q[:, n * P:(n + 1) * P], start=True, stop=True)
                us = [M[1][:, 0:T], M[0][:, T:2 * T], M[1][:, T:2 * T]]
                for c in range(3):
                    half = slice(GLA_C * (c % 2), GLA_C * (c % 2 + 1))
                    m = nc.tensor.matmul(us[c], kt[half, h, c // 2, :], gv_tok[half, c // 2, h * T:(h + 1) * T], start=True, stop=True)
                m.then_inc(S("gla_att"), 1)

            def gla_o(h):
                pe.wait_ge(S("gla_states"), h + 1)
                if h >= 1:
                    pe.wait_ge(S("gla_sq"), h)
                q = flat(O_["q"] + h, 1)
                for vh in range(2):
                    for n in range(2):
                        at = vh * T + n * P
                        nc.tensor.matmul(M[2][:, at:at + P], gv_tok[:, n, h * T + vh * P:h * T + (vh + 1) * P], gatt(h)[:, n * P:(n + 1) * P], start=True, stop=False, skip_group_check=True)
                        for c in range(max(1, 2 * n), 2 * n + 2):
                            m = nc.tensor.matmul(M[2][:, vh * T + c * GLA_C:vh * T + (c + 1) * GLA_C], gst(h, c - 1)[:, vh * P:(vh + 1) * P],
                                                 q[:, c * GLA_C:(c + 1) * GLA_C], start=False, stop=(c == 2 * n + 1), skip_group_check=True)
                m.then_inc(S("gla_o_done"), 1)

            def gla_n(h):
                pe.wait_ge(S("gla_sq"), h + 1)
                if h >= 1:
                    pe.wait_ge(S("gla_rs"), h)
                for vh in range(2):
                    m = nc.tensor.matmul(M[3][:, 0:T], K("ones"), flat(O_["sqt"] + vh, 1), start=(vh == 0), stop=(vh == 1))
                m.then_inc(S("gla_ss"), 1)

            def sb_z(h):
                if h == 0:
                    pe.wait_ge(S("gla_states"), GLA_H)
                evacuated(pe, ("sq", h // 2))
                evacuated(pe, ("sk", h // 2))
                if h >= 1:
                    pe.wait_ge(S("sb_l1p"), h)
                q, k = flat(O_["sqq"] + h, 1), flat(O_["skk"] + h, 1)
                nc.tensor.matmul(M[0][:, 0:T], k[:, 0:P], q, start=True, stop=True)
                nc.tensor.matmul(M[0][:, T:T + P], k[:, P:T], q[:, P:T], start=True, stop=True).then_inc(S("sb_z_done"), 1)

            def mix_pre():
                sum_squares(3, S_["sq"])

            def mix_post():
                sum_squares(4, S_["osq"])

            def ffn_pre():
                sum_squares(5, S_["sq"])

            def ffn_post():
                sum_squares(6, S_["sq"])

            def ple_post():
                sum_squares(7, S_["sq"])

            def lora_w():
                pe.wait_ge(S("late_in"), 64)
                pe.wait_ge(S("lora_x"), 1)
                for b in range(4):
                    m = nc.tensor.matmul(M[2 + b // 2][:, (b % 2) * T:(b % 2 + 1) * T], lora[0:32, 0, b * P:(b + 1) * P], xx[0:32, 0, :], start=True, stop=True)
                m.then_inc(S("lora_w"), 1)

            def lora_a():
                for b in range(4):
                    m = nc.tensor.matmul(M[b // 2][:, (b % 2) * T:(b % 2 + 1) * T], lora[32:64, 0, b * P:(b + 1) * P], xx[32:64, 0, :], start=True, stop=True)
                m.then_inc(S("lora_a"), 1)

            def head_sums(banks, src, sem_name, each=False):
                for b in range(4):
                    m = nc.tensor.matmul(M[banks + b // 2][:, (b % 2) * T:(b % 2 + 1) * T], K("ones_head"), flat(src + b, 1), start=True, stop=True)
                    if each and b % 2:
                        m.then_inc(S(sem_name), 1)
                if not each:
                    m.then_inc(S(sem_name), 1)

            def key_norms():
                pe.wait_ge(S("kk_sq"), 1)
                pe.wait_ge(S("sw"), 4)
                head_sums(2, S_["rn"], "kk_ss")

            def turn_v():
                pe.wait_ge(S("shift"), 3)
                pe.wait_ge(S("kk"), 2)
                for c in range(2):
                    for b in range(4):
                        m = turn(M[2 + c][:, b * P:(b + 1) * P], v_f[:, b, c * P:(c + 1) * P])
                    m.then_inc(S("v_turned"), 1)

            def bonus():
                pe.wait_ge(S("rk"), 1)
                pe.wait_ge(S("iclr"), 4)
                head_sums(0, S_["rk"], "bonus_sum", each=True)

            def turn_bk():
                pe.wait_ge(S("rw_operands"), 1)
                pe.wait_ge(S("vt"), 2)
                for c in range(2):
                    for b in range(4):
                        m = turn(M[2 + c][:, b * P:(b + 1) * P], (b_f, kb_f)[c][:, b, 0:P])
                    m.then_inc(S("bk_turned"), 1)

            def rw_pairs(n):
                c, s_ = n // 2, n % 2
                if n == 0:
                    pe.wait_ge(S("bonus"), 1)
                    pe.wait_ge(S("bkt"), 2)
                elif n == 2:
                    pe.wait_ge(S("yr"), 1)
                    pe.wait_ge(S("s0"), 4)
                else:
                    pe.wait_ge(S("rw_t0"), n)
                for q in range(4):
                    b, half = head_of(s_, q)
                    hs = slice(HD * half, HD * (half + 1))
                    for k, src in enumerate((b_f, kb_f)):
                        m = nc.tensor.matmul(M[2 * k + half][:, (q % 2) * T:(q % 2 + 1) * T], src[hs, b, c * P:(c + 1) * P],
                                             ar_[hs, b, c, :, :].rearrange("p k t -> p (k t)"), start=True, stop=True)
                m.then_inc(S("rw_pairs"), 1)

            def rw_pair_t(n):
                c, s_ = n // 2, n % 2
                pe.wait_ge(S("rw_masked"), 4 * n + 2)
                for q in range(4):
                    b, half = head_of(s_, q)
                    hs = slice(HD * half, HD * (half + 1))
                    m = nc.tensor.matmul(M[half][:, (q % 2) * P:(q % 2 + 1) * P], ar_[hs, b, c, 0, :], b_f[hs, b, c * P:(c + 1) * P], start=True, stop=True)
                m.then_inc(S("rw_pairs"), 1)

            def rw_u(m_):
                for s_ in range(2):
                    if m_ % 6 == 0:
                        pe.wait_ge(S("rw_t0"), 2 * (m_ // 6) + 2)
                    else:
                        pe.wait_ge(S("rw_new"), 2 * (m_ - 1) + s_ + 1)
                    nm_b, _, t_, _, _ = rset(s_)
                    for q in range(4):
                        m = nc.tensor.matmul(M[s_][:, q * P:(q + 1) * P], nm_b[:, q, 0:P], t_[:, q, :], start=True, stop=True)
                    m.then_inc(S("rw_u"), 1)

            def rw_t(m_):
                for s_ in range(2):
                    pe.wait_ge(S("rw_um"), 2 * m_ + s_ + 1)
                    _, _, t_, tt_, um = rset(s_)
                    for q in range(4):
                        m = nc.tensor.matmul(M[2 + s_][:, q * P:(q + 1) * P], um[:, q, :], tt_[:, q, :], start=True, stop=True)
                        if m_ % 6 < 5:
                            m = nc.tensor.matmul(M[s_][:, q * P:(q + 1) * P], tt_[:, q, :], um[:, q, :], start=True, stop=True)
                    m.then_inc(S("rw_t"), 1)

            def solve_w(c):
                pe.wait_ge(S("rw_new"), 12 * c + 12)
                for s_ in range(2):
                    nm_k = rset(s_)[1]
                    for q in range(4):
                        b, half = head_of(s_, q)
                        hs = slice(HD * half, HD * (half + 1))
                        to = M[half][:, s_ * P + (q % 2) * HD:s_ * P + (q % 2 + 1) * HD]
                        m = nc.tensor.matmul(to, nm_k[:, q, 0:P], vt[:, c, (2 * b + half) * HD:(2 * b + half + 1) * HD], start=True, stop=(c == 0), skip_group_check=True)
                        if c == 1:
                            m = nc.tensor.matmul(to, ar_[hs, b, c, 0, :], s0[hs, b, :], start=False, stop=True, skip_group_check=True)
                m.then_inc(S("rw_w0"), 1)

            def solve_u(c):
                pe.wait_ge(S("w0"), c + 1)
                for s_ in range(2):
                    tt_ = rset(s_)[3]
                    for q in range(4):
                        m = nc.tensor.matmul(M[2][:, wcol(s_, q)], tt_[:, q, :], w0_all[:, wcol(s_, q)], start=True, stop=True)
                m.then_inc(S("rw_u0"), 1)

            def solve_y(c):
                pe.wait_ge(S("u0"), c + 1)
                for s_ in range(2):
                    nm_b, nm_k = rset(s_)[0:2]
                    for q in range(4):
                        b, half = head_of(s_, q)
                        hs = slice(HD * half, HD * (half + 1))
                        to = M[3][hs, b * P:(b + 1) * P]
                        nc.tensor.matmul(to, u_all[:, wcol(s_, q)], nm_b[:, q, P:2 * P], start=True, stop=False, skip_group_check=True)
                        m = nc.tensor.matmul(to, vt[:, c, (2 * b + half) * HD:(2 * b + half + 1) * HD], nm_k[:, q, P:2 * P], start=False, stop=(c == 0), skip_group_check=True)
                        if c == 1:
                            m = nc.tensor.matmul(to, s0[hs, b, :], ar_[hs, b, c, 1, :], start=False, stop=True, skip_group_check=True)
                m.then_inc(S("rw_y"), 1)
                if c == 0:
                    for s_ in range(2):
                        for q in range(4):
                            b, half = head_of(s_, q)
                            hd = slice((2 * b + half) * HD, (2 * b + half + 1) * HD)
                            to = M[0][HD * half:HD * (half + 1), b * HD:(b + 1) * HD]
                            nc.tensor.matmul(to, bt[:, hd], u_all[:, wcol(s_, q)], start=True, stop=False, skip_group_check=True)
                            m = nc.tensor.matmul(to, kbt[:, hd], vt[:, 0, hd], start=False, stop=True, skip_group_check=True)
                    m.then_inc(S("rw_s"), 1)

            def gn_mean():
                pe.wait_ge(S("yr"), 2)
                head_sums(0, S_["y"], "gn_sum", each=True)

            def gn_var():
                pe.wait_ge(S("gn_sq"), 1)
                head_sums(2, S_["gsum"], "gn_ss")

            def rw_gate():
                pe.wait_ge(S("gate_x"), 1)
                pe.wait_ge(S("gn_ln"), 2)
                for b in range(4):
                    m = nc.tensor.matmul(M[2 + b // 2][:, (b % 2) * T:(b % 2 + 1) * T], lora[0:96, 1, b * P:(b + 1) * P], xx[0:96, 1, :], start=True, stop=True)
                    if b % 2:
                        m.then_inc(S("rw_g"), 1)

            def at_s(n):
                h, i = n // 2, n % 2
                hs = slice(HD * (h % 2), HD * (h % 2 + 1))
                if n == 0:
                    pe.wait_ge(S("roped"), 6)
                    pe.wait_ge(S("gn_c"), 1)
                else:
                    pe.wait_ge(S("at_max"), n)
                if i == 1 and n >= 3:
                    pe.wait_ge(S("at_oa"), n - 1)
                q_, k_ = flat(S_["q"], 6).rearrange("p (c t) -> p c t", t=T), flat(S_["ak"], 6).rearrange("p (c t) -> p c t", t=T)
                for g in range(AT_G):
                    at = g * (i + 1) * P
                    m = nc.tensor.matmul(M[at // 512][:, at % 512:at % 512 + (i + 1) * P], q_[hs, 2 * g + h // 2, i * P:(i + 1) * P], k_[hs, 2 * g + h // 2, 0:(i + 1) * P], start=True, stop=True)
                m.then_inc(S("at_s"), 1)

            def at_t(n):
                i = n % 2
                pe.wait_ge(S("at_p"), n + 1)
                if n == 0:
                    pe.wait_ge(S("rw_out"), 1)
                else:
                    pe.wait_ge(S("at_pt"), 2 * n)
                for k in range(AT_G * (i + 1)):
                    m = turn(M[2 + k // 4][:, (k % 4) * P:(k % 4 + 1) * P], sc(n)[:, k * P:(k + 1) * P])
                m.then_inc(S("at_turned"), 1)

            def at_o(n):
                h, i = n // 2, n % 2
                hs = slice(HD * (h % 2), HD * (h % 2 + 1))
                pe.wait_ge(S("at_pt"), 2 * n + 2)
                for k in range(3):
                    evacuated(pe, ("av", k))
                pe.wait_ge(S("at_max"), min(n + 2, 2 * AT_H))
                if n >= 1:
                    pe.wait_ge(S("at_oa"), n)
                total = AT_G * (i + 1)
                for k in range(total):
                    g, st = k // (i + 1), k % (i + 1)
                    m = nc.tensor.matmul(M[1][hs, T:T + P], av_tok[:, st, g * AT_W + h * HD:g * AT_W + (h + 1) * HD], pt(n)[:, k * P:(k + 1) * P],
                                         start=(k == 0), stop=(k == total - 1), skip_group_check=True)
                m.then_inc(S("at_o"), 1)

            def turn_p():
                pe.wait_ge(S("p_in"), 16)
                for c in range(2):
                    for n in range(2):
                        m = turn(M[1][:, c * T + n * P:c * T + (n + 1) * P], ar(S_["p_in"], 2)[:, n, c * P:(c + 1) * P])
                m.then_inc(S("p_turned"), 1)

            def sb_c(h):
                pe.wait_ge(S("sb_l"), h + 1)
                if h >= 1:
                    pe.wait_ge(S("sb_arg"), h)
                nc.tensor.matmul(M[1][:, 0:384], K("from_here"), sbw(2), start=True, stop=False, skip_group_check=True)
                nc.tensor.matmul(M[1][:, P:2 * P], K("ones"), sbw(2)[:, 2 * P:3 * P], start=False, stop=True, skip_group_check=True).then_inc(S("sb_c_done"), 1)

            def sb_o(h):
                pe.wait_ge(S("sb_w"), h + 1)
                evacuated(pe, ("sv", h // 2))
                if h == 0:
                    pe.wait_ge(S("gla_sq"), GLA_H)
                    pe.wait_ge(S("gla_o"), GLA_H)
                if h >= 1:
                    pe.wait_ge(S("sb_y"), h)
                nc.tensor.matmul(M[2][:, 0:T], sv_tok[:, 0, h * P:(h + 1) * P], sbw(4)[:, 0:T], start=True, stop=False, skip_group_check=True)
                nc.tensor.matmul(M[2][:, P:T], sv_tok[:, 1, h * P:(h + 1) * P], sbw(4)[:, T:T + P], start=False, stop=True, skip_group_check=True).then_inc(S("sb_o_done"), 1)

            steps = dict(mix_pre=mix_pre, mix_post=mix_post, ffn_pre=ffn_pre, ffn_post=ffn_post, ple_post=ple_post, lora_w=lora_w, lora_a=lora_a,
                         key_norms=key_norms, turn_v=turn_v, bonus=bonus, turn_bk=turn_bk, rw_pairs=rw_pairs, rw_pair_t=rw_pair_t, rw_u=rw_u, rw_t=rw_t,
                         solve_w=solve_w, solve_u=solve_u, solve_y=solve_y, gn_mean=gn_mean, gn_var=gn_var, rw_gate=rw_gate, at_s=at_s, at_t=at_t, at_o=at_o, turn_p=turn_p,
                         load_x=load_x, first_sum=first_sum, params=params, norm=norm, final_norm=final_norm, sgu_w=sgu_w, sgu_z=sgu_z, gla_z=gla_z, gla_kt=gla_kt, gla_att=gla_att, gla_o=gla_o, gla_n=gla_n, sb_z=sb_z, sb_c=sb_c, sb_o=sb_o)

            def ada_unit(u):
                layer, blk, n = units[u]["ada"]
                if n == 0:
                    pe.wait_ge(S("x_ready"), 4)
                if n in (8, 20):
                    pe.wait_ge(S("ada_read"), 1 + n // 20)
                if n == 20:
                    pe.wait_ge(S("gla_rs"), GLA_H)
                if n in ADA_PE:
                    unit_loaded(pe, u)
                    pe.wait_ge(S("silu_c"), 1)
                    w = raw[:, u % RAW, :].rearrange("p (k n) -> p k n", k=KD)
                else:
                    a = ADA_DVE.index(n)
                    pe.wait_ge(S("ada_acc"), a + 1)
                for fb in range(2):
                    to = M[3][:, 24 * layer + blk + fb:24 * layer + blk + fb + 1]
                    if n in ADA_PE:
                        for k in range(KD):
                            m = nc.tensor.matmul(to, w[:, k, fb * P:(fb + 1) * P], silu_c[:, k:k + 1], start=(k == 0), stop=(k == KD - 1))
                    else:
                        m = nc.tensor.matmul(to, ada_acc[a % 2][:, fb * P:(fb + 1) * P], K("ones")[:, 0:1], start=True, stop=True)
                m.then_inc(S("ada_used"), 1)

            def run_job(key):
                j = jobs[key]
                n = j["order"]
                if n >= NBANK:
                    pe.wait_ge(S(f"evacuated{n % NBANK}"), n // NBANK)
                b = bank_of(key)
                blocks, steps_ = j["blocks"], j["steps"]
                together = len(set(blocks)) == 1
                order_ = [(s, fb) for s in range(len(steps_)) for fb in range(len(blocks))]
                if not together:
                    order_.sort(key=lambda sf: (sf[1], sf[0]))
                for at, (s, fb) in enumerate(order_):
                    (u, k, xc), un, width = steps_[s], units[steps_[s][0]], blocks[fb]
                    if fb == 0 and (s == 0 or steps_[s - 1][0] != u):
                        split_done(pe, un["index"])
                    if fb == 0:
                        pe.wait_ge(S(j["ready"](xc)[0]), j["ready"](xc)[1])
                    wh, wl = (w[:, un["index"] % SPL, k * un["n"]:(k + 1) * un["n"]] for w in (w_hi, w_lo))
                    xh, xl = operand(0, xc), operand(1, xc)
                    if j["layout"] == "F":
                        c = j["col"] + sum(blocks[:fb])
                        to, cs = b[0:width, fb * T:(fb + 1) * T], slice(c, c + width)
                        pairs = ((wh[:, cs], xh), (wh[:, cs], xl), (wl[:, cs], xh))
                    else:
                        ts = slice(fb * P, (fb + 1) * P)
                        cs = slice(j["col"], j["col"] + CB)
                        to = b[:, fb * CB:(fb + 1) * CB]
                        pairs = ((xh[:, ts], wh[:, cs]), (xh[:, ts], wl[:, cs]), (xl[:, ts], wh[:, cs]))
                    for q, (a_, b_) in enumerate(pairs):
                        m = nc.tensor.matmul(to, a_, b_, start=(s == 0 and q == 0 and (fb == 0 or not together)),
                                             stop=(s == len(steps_) - 1 and q == 2), skip_group_check=True)
                    if at + 1 == len(order_) or (together and steps_[order_[at + 1][0]][0] != u):
                        m.then_inc(S("projected"), 1)

            run(steps, run_job, None, ada_unit)
            for q in (0, 2, 1, 3):
                pe.wait_ge(S("x_update"), 28 + 4 * (q % 2))
                for c in range(2):
                    for tt in range(2):
                        at = (c * 2 + tt) * P
                        m = turn(M[q][:, at:at + P], x[:, 4 * (q % 2) + 2 * c + tt, (q // 2) * P:(q // 2 + 1) * P])
                m.then_inc(S("out_turned"), 1)


def kernel(**inputs):
    import numpy as _np
    import concourse.bacc as _bacc
    from concourse import mybir as _mybir
    from concourse.bass_utils import run_bass_kernel_spmd as _run

    nc = _bacc.Bacc("TRN2", target_bir_lowering=False, num_devices=1)
    arrays, ins = {}, {}
    for name, a in inputs.items():
        a = _np.ascontiguousarray(a)
        arrays[f"in_{name}_dram"] = a
        ins[name] = nc.dram_tensor(f"in_{name}_dram", a.shape, _mybir.dt.from_np(a.dtype), kind="ExternalInput").ap()
    table = constants()
    a = _np.ascontiguousarray(_np.concatenate([table[name] for names in PHASES for name in names], 1))
    arrays["in_constants_dram"] = a
    consts = nc.dram_tensor("in_constants_dram", a.shape, _mybir.dt.from_np(a.dtype), kind="ExternalInput").ap()
    out = nc.dram_tensor("out_0_dram", (1, T, D), F32, kind="ExternalOutput").ap()
    program(nc, ins, consts, out)
    r = _run(nc, [arrays], core_ids=[0])
    return r.results[0]["out_0_dram"]
```
